# Optimizing a Trainium2 kernel written in Bass

```python
import math
import numpy as np
import jax, jax.numpy as jnp
from jax import lax

D_MODEL = 1024
BATCH = 1
SEQ = 1024
DEPTH = 1

D_MIX = D_MODEL
D_PLE = 256
DA = D_MIX // 2
HA = 4
DA_V = DA // HA
DA_QK = DA_V // 2
DB = D_MIX - DA
HB = 16
DB_H = DB // HB
D_IN = 3 * DA + 3 * DB
GRID_W = 64
WIN_R = 8
WIN_C = 16
Q_COLS = 16
K_COLS = 32
ROPE_THETA = 10000.0
EPS = 1e-6
Q_BLOCK = 128
NEG = -1e30
N_GROUPS = 4
EXPERTS_PER_GROUP = 8
N_EXPERTS = N_GROUPS * EXPERTS_PER_GROUP
TOP_K = 2
D_EXPERT = 512
MOE_BLOCK = 128


def rms_norm(x, g):
    xf = x.astype(jnp.float32)
    y = xf * lax.rsqrt(jnp.mean(xf * xf, axis=-1, keepdims=True) + EPS)
    return (y * g.astype(jnp.float32)).astype(x.dtype)

def rope_tables(seq, dim):
    inv = ROPE_THETA ** (-jnp.arange(0, dim, 2, dtype=jnp.float32) / dim)
    ang = jnp.arange(seq, dtype=jnp.float32)[:, None] * inv[None, :]
    return jnp.cos(ang), jnp.sin(ang)

def apply_rope(x, cos, sin):
    s = x.shape[1]
    bshape = (s,) + (1,) * (x.ndim - 3) + (-1,)
    c = cos.reshape(bshape)
    sn = sin.reshape(bshape)
    x1, x2 = jnp.split(x.astype(jnp.float32), 2, axis=-1)
    return jnp.concatenate([x1 * c - x2 * sn, x2 * c + x1 * sn], axis=-1).astype(x.dtype)

def diff_attention(q, k, v, g_q, g_k, lam_q1, lam_k1, lam_q2, lam_k2, g_sub, lam_init):
    b, s = q.shape[:2]
    cos, sin = rope_tables(s, DA_QK)
    q = apply_rope(rms_norm(q, g_q), cos, sin)
    k = apply_rope(rms_norm(k, g_k), cos, sin)
    lam = (jnp.exp(jnp.sum(lam_q1.astype(jnp.float32) * lam_k1.astype(jnp.float32)))
           - jnp.exp(jnp.sum(lam_q2.astype(jnp.float32) * lam_k2.astype(jnp.float32)))
           + lam_init)
    scale = DA_QK ** -0.5
    qt = q.transpose(0, 2, 1, 3, 4)
    kt = k.transpose(0, 2, 1, 3, 4)
    vt = v.transpose(0, 2, 1, 3)
    k1, k2 = kt[..., 0, :], kt[..., 1, :]
    nqb = s // Q_BLOCK
    qb = qt.reshape(b, HA, nqb, Q_BLOCK, 2, DA_QK).transpose(2, 0, 1, 3, 4, 5)

    def block(qblk):
        s1 = jnp.einsum('bhqd,bhkd->bhqk', qblk[..., 0, :], k1).astype(jnp.float32) * scale
        s2 = jnp.einsum('bhqd,bhkd->bhqk', qblk[..., 1, :], k2).astype(jnp.float32) * scale
        w = (jax.nn.softmax(s1, axis=-1) - lam * jax.nn.softmax(s2, axis=-1)).astype(vt.dtype)
        return jnp.einsum('bhqk,bhkd->bhqd', w, vt)

    o = lax.map(block, qb)
    o = o.transpose(1, 0, 3, 2, 4).reshape(b, s, HA, DA_V)
    o = rms_norm(o, g_sub) * (1.0 - lam_init)
    return o.reshape(b, s, HA * DA_V)

def neighbourhood_attention(q, k, v, g_q, g_k, rpb):
    b, s, h, d = q.shape
    rows = s // GRID_W
    kr = min(WIN_R, rows)
    ncb = GRID_W // Q_COLS
    q = rms_norm(q, g_q)
    k = rms_norm(k, g_k)
    r = np.arange(rows)
    rs = np.clip(r - kr // 2, 0, rows - kr)
    key_rows = rs[:, None] + np.arange(kr)[None, :]
    row_off = (key_rows - r[:, None] + (WIN_R - 1)).astype(np.int32)
    c = np.arange(GRID_W).reshape(ncb, Q_COLS)
    cs = np.clip(c - WIN_C // 2, 0, GRID_W - WIN_C)
    kb = np.minimum(cs[:, 0], GRID_W - K_COLS)
    key_cols = kb[:, None] + np.arange(K_COLS)[None, :]
    col_valid = ((key_cols[:, None, :] >= cs[:, :, None])
                 & (key_cols[:, None, :] < cs[:, :, None] + WIN_C))
    col_off = np.clip(key_cols[:, None, :] - c[:, :, None] + (WIN_C - 1), 0, 2 * WIN_C - 2)
    key_idx = (key_rows[:, None, :, None] * GRID_W + key_cols[None, :, None, :])
    key_idx = key_idx.reshape(rows, ncb * kr * K_COLS).astype(np.int32)
    bias_cols = rpb.astype(jnp.float32)[:, :, col_off]
    bias_cols = jnp.where(col_valid, bias_cols, NEG)
    scale = d ** -0.5
    q_rows = q.reshape(b, rows, GRID_W, h, d).transpose(1, 0, 2, 3, 4)

    def row_step(args):
        q_row, idx, roff = args
        qb = q_row.reshape(b, ncb, Q_COLS, h, d)
        kg = k[:, idx].reshape(b, ncb, kr * K_COLS, h, d)
        vg = v[:, idx].reshape(b, ncb, kr * K_COLS, h, d)
        bias = bias_cols[:, roff]
        bias = bias.transpose(0, 2, 3, 1, 4).reshape(h, ncb, Q_COLS, kr * K_COLS)
        sc = jnp.einsum('bjqhd,bjkhd->bhjqk', qb, kg).astype(jnp.float32) * scale + bias
        pr = jax.nn.softmax(sc, axis=-1).astype(vg.dtype)
        o = jnp.einsum('bhjqk,bjkhd->bjqhd', pr, vg)
        return o.reshape(b, GRID_W, h, d)

    o = lax.map(row_step, (q_rows, jnp.asarray(key_idx), jnp.asarray(row_off)))
    return o.transpose(1, 0, 2, 3, 4).reshape(b, s, h * d)

def hier_moe(x, w_rg, w_re, w1, w3, w2):
    b, s, dm = x.shape
    t = b * s
    xf = x.reshape(t, dm)
    g_prob = jax.nn.softmax((xf @ w_rg).astype(jnp.float32), axis=-1)
    g_gate, g_idx = lax.top_k(g_prob, 1)
    e_logits = (xf @ w_re).astype(jnp.float32).reshape(t, N_GROUPS, EXPERTS_PER_GROUP)
    e_logits = jnp.take_along_axis(e_logits, g_idx[:, :, None], axis=1)[:, 0]
    e_w, e_i = lax.top_k(jax.nn.softmax(e_logits, axis=-1), TOP_K)
    weights = g_gate * (e_w / jnp.sum(e_w, axis=-1, keepdims=True))
    experts = (g_idx * EXPERTS_PER_GROUP + e_i).astype(jnp.int32)
    n = t * TOP_K
    slot_e = experts.reshape(n)
    slot_tok = jnp.repeat(jnp.arange(t, dtype=jnp.int32), TOP_K)
    slot_w = weights.reshape(n)
    order = jnp.argsort(slot_e)
    se = slot_e[order]
    counts = jnp.zeros((N_EXPERTS,), jnp.int32).at[slot_e].add(1)
    starts = jnp.cumsum(counts) - counts
    padded = (counts + MOE_BLOCK - 1) // MOE_BLOCK * MOE_BLOCK
    pad_end = jnp.cumsum(padded)
    pad_start = pad_end - padded
    dest = pad_start[se] + jnp.arange(n, dtype=jnp.int32) - starts[se]
    n_blocks = n // MOE_BLOCK + N_EXPERTS
    p_len = n_blocks * MOE_BLOCK
    pad_tok = jnp.full((p_len,), t, jnp.int32).at[dest].set(slot_tok[order])
    pad_w = jnp.zeros((p_len,), jnp.float32).at[dest].set(slot_w[order])
    block_e = jnp.minimum(jnp.searchsorted(pad_end, jnp.arange(n_blocks, dtype=jnp.int32) * MOE_BLOCK,
                                           side='right'), N_EXPERTS - 1).astype(jnp.int32)
    xf_pad = jnp.concatenate([xf, jnp.zeros((1, dm), xf.dtype)], axis=0)
    xs = xf_pad[pad_tok].reshape(n_blocks, MOE_BLOCK, dm)

    def expert_block(args):
        xb, e = args
        hdn = jax.nn.silu(xb @ w1[e]) * (xb @ w3[e])
        return hdn @ w2[e]

    ys = lax.map(expert_block, (xs, block_e)).reshape(p_len, dm)
    out = jnp.zeros((t + 1, dm), ys.dtype).at[pad_tok].add(ys * pad_w[:, None].astype(ys.dtype))
    return out[:t].reshape(b, s, dm).astype(x.dtype)

def first_inputs(seed: int = 0) -> dict:
    key = jax.random.key(seed)
    ks = jax.random.split(key, 25)
    f = jnp.float32

    def nrm(k, shape, scale):
        return jax.random.normal(k, shape, f) * scale

    return {
        'x': nrm(ks[0], (BATCH, SEQ, D_MODEL), 1.0),
        'p': nrm(ks[1], (DEPTH, BATCH, SEQ, D_PLE), 1.0),
        'g_mix': 1.0 + nrm(ks[2], (DEPTH, D_MODEL), 0.02),
        'w_in': nrm(ks[3], (DEPTH, D_MODEL, D_IN), D_MODEL ** -0.5),
        'g_qa': 1.0 + nrm(ks[4], (DEPTH, DA_QK), 0.02),
        'g_ka': 1.0 + nrm(ks[5], (DEPTH, DA_QK), 0.02),
        'lam_q1': nrm(ks[6], (DEPTH, DA_QK), 0.1),
        'lam_k1': nrm(ks[7], (DEPTH, DA_QK), 0.1),
        'lam_q2': nrm(ks[8], (DEPTH, DA_QK), 0.1),
        'lam_k2': nrm(ks[9], (DEPTH, DA_QK), 0.1),
        'g_sub': 1.0 + nrm(ks[10], (DEPTH, DA_V), 0.02),
        'g_qb': 1.0 + nrm(ks[11], (DEPTH, DB_H), 0.02),
        'g_kb': 1.0 + nrm(ks[12], (DEPTH, DB_H), 0.02),
        'rpb': nrm(ks[13], (DEPTH, HB, 2 * WIN_R - 1, 2 * WIN_C - 1), 0.1),
        'w_out': nrm(ks[14], (DEPTH, D_MIX, D_MODEL), D_MIX ** -0.5),
        'g_ffn': 1.0 + nrm(ks[15], (DEPTH, D_MODEL), 0.02),
        'w_rg': nrm(ks[16], (DEPTH, D_MODEL, N_GROUPS), D_MODEL ** -0.5),
        'w_re': nrm(ks[17], (DEPTH, D_MODEL, N_EXPERTS), D_MODEL ** -0.5),
        'w1': nrm(ks[18], (DEPTH, N_EXPERTS, D_MODEL, D_EXPERT), D_MODEL ** -0.5),
        'w3': nrm(ks[19], (DEPTH, N_EXPERTS, D_MODEL, D_EXPERT), D_MODEL ** -0.5),
        'w2': nrm(ks[20], (DEPTH, N_EXPERTS, D_EXPERT, D_MODEL), D_EXPERT ** -0.5),
        'g_plg': 1.0 + nrm(ks[21], (DEPTH, D_MODEL), 0.02),
        'w_plg': nrm(ks[22], (DEPTH, D_MODEL, D_MODEL), D_MODEL ** -0.5),
        'w_ple': nrm(ks[23], (DEPTH, D_PLE, D_MODEL), D_PLE ** -0.5),
        'g_ple': 1.0 + nrm(ks[24], (DEPTH, D_MODEL), 0.02),
    }

def first_block(x, p, g_mix, w_in, g_qa, g_ka, lam_q1, lam_k1, lam_q2, lam_k2, g_sub, g_qb, g_kb,
              rpb, w_out, g_ffn, w_rg, w_re, w1, w3, w2, g_plg, w_plg, w_ple, g_ple):
    b, s, _ = x.shape
    h = x
    for i in range(DEPTH):
        lam_init = 0.8 - 0.6 * math.exp(-0.3 * i)
        a = rms_norm(h, g_mix[i])
        proj = a @ w_in[i]
        qa, ka, va, qb, kb, vb = jnp.split(proj, np.cumsum([DA, DA, DA, DB, DB])[:5].tolist(), axis=-1)
        oa = diff_attention(qa.reshape(b, s, HA, 2, DA_QK), ka.reshape(b, s, HA, 2, DA_QK),
                            va.reshape(b, s, HA, DA_V), g_qa[i], g_ka[i],
                            lam_q1[i], lam_k1[i], lam_q2[i], lam_k2[i], g_sub[i], lam_init)
        ob = neighbourhood_attention(qb.reshape(b, s, HB, DB_H), kb.reshape(b, s, HB, DB_H),
                                     vb.reshape(b, s, HB, DB_H), g_qb[i], g_kb[i], rpb[i])
        h = h + jnp.concatenate([oa, ob], axis=-1) @ w_out[i]
        h = h + hier_moe(rms_norm(h, g_ffn[i]), w_rg[i], w_re[i], w1[i], w3[i], w2[i])
        h = h + rms_norm(p[i] @ w_ple[i], g_ple[i]) * jax.nn.sigmoid(rms_norm(h, g_plg[i]) @ w_plg[i])
    return h


DEPTH_2 = 2

CHUNK = 64
D_MIX_2 = D_MODEL
D_RET = D_MIX_2 // 2
D_SB = D_MIX_2 - D_RET
RET_HEADS = 4
RET_HEAD_DIM = D_RET // RET_HEADS
SB_HEADS = 8
SB_HEAD_DIM = D_SB // SB_HEADS
ROPE_BASE = 10000.0
ADA_SCALE = 0.2
SPLIT_SIZES = [D_RET] * 4 + [D_SB] * 4
D_IN_2 = sum(SPLIT_SIZES)


def rms_norm_2(x, g):
    xf = x.astype(jnp.float32)
    return xf * lax.rsqrt(jnp.mean(xf * xf, axis=-1, keepdims=True) + EPS) * g.astype(jnp.float32)

def split_heads(x, n_heads):
    b, s, _ = x.shape
    return x.reshape(b, s, n_heads, -1).transpose(0, 2, 1, 3)

def merge_heads(x):
    b, h, s, d = x.shape
    return x.transpose(0, 2, 1, 3).reshape(b, s, h * d)

def rotary(x, pos):
    half = x.shape[-1] // 2
    inv = ROPE_BASE ** (-jnp.arange(half, dtype=jnp.float32) / half)
    ang = pos[:, None] * inv[None, :]
    cos, sin = jnp.cos(ang), jnp.sin(ang)
    x1, x2 = x[..., :half], x[..., half:]
    return jnp.concatenate([x1 * cos - x2 * sin, x1 * sin + x2 * cos], axis=-1)

def retention(q, k, v):
    b, h, s, d = q.shape
    n = s // CHUNK
    log_gamma = jnp.log1p(-(2.0 ** (-5.0 - jnp.arange(h, dtype=jnp.float32))))
    idx = jnp.arange(CHUNK, dtype=jnp.float32)
    dmask = jnp.exp(jnp.abs(idx[:, None] - idx[None, :])[None] * log_gamma[:, None, None])
    q_dec = jnp.exp((idx + 1.0)[None, :] * log_gamma[:, None])
    k_dec = jnp.exp((CHUNK - 1.0 - idx)[None, :] * log_gamma[:, None])
    chunk_dec = jnp.exp(CHUNK * log_gamma)

    k = k * (d ** -0.5)
    qc = q.reshape(b, h, n, CHUNK, d)
    kc = k.reshape(b, h, n, CHUNK, d)
    vc = v.reshape(b, h, n, CHUNK, v.shape[-1])

    scores = jnp.einsum('bhncd,bhnmd->bhncm', qc, kc) * dmask[None, :, None]
    o_inner = jnp.einsum('bhncm,bhnme->bhnce', scores, vc)

    kv = jnp.einsum('bhnmd,bhnme->nbhde', kc * k_dec[None, :, None, :, None], vc)

    def step(state, kv_i):
        return state * chunk_dec[None, :, None, None] + kv_i, state

    init = jnp.zeros((b, h, d, v.shape[-1]), dtype=kv.dtype)
    _, prev = lax.scan(step, init, kv)
    o_cross = jnp.einsum('bhncd,nbhde->bhnce', qc, prev) * q_dec[None, :, None, :, None]

    o = (o_inner + o_cross).reshape(b, h, s, v.shape[-1])
    mu = jnp.mean(o, axis=-1, keepdims=True)
    var = jnp.mean(jnp.square(o - mu), axis=-1, keepdims=True)
    return (o - mu) * lax.rsqrt(var + EPS)

def stick_breaking(q, k, v):
    b, h, s, d = q.shape
    nb = s // Q_BLOCK
    scale = d ** -0.5
    q_blocks = q.reshape(b, h, nb, Q_BLOCK, d).transpose(2, 0, 1, 3, 4)
    key_pos = jnp.arange(s)

    def block(args):
        qi, bi = args
        t = bi * Q_BLOCK + jnp.arange(Q_BLOCK)
        mask = key_pos[None, :] < t[:, None]
        z = jnp.einsum('bhqd,bhsd->bhqs', qi, k) * scale
        log_beta = jax.nn.log_sigmoid(z)
        log_keep = jnp.where(mask, jax.nn.log_sigmoid(-z), 0.0)
        suffix = lax.cumsum(log_keep, axis=3, reverse=True) - log_keep
        a = jnp.where(mask, jnp.exp(log_beta + suffix), 0.0)
        return jnp.einsum('bhqs,bhse->bhqe', a, v)

    out = lax.map(block, (q_blocks, jnp.arange(nb)))
    return out.transpose(1, 2, 0, 3, 4).reshape(b, h, s, v.shape[-1])

def hybrid_layer(x, c_act, norm_g, w_ada, b_ada, w_in, w_out, pos):
    mod = c_act @ w_ada + b_ada
    shift, scale, gate = jnp.split(mod, 3, axis=-1)
    h = rms_norm_2(x, norm_g) * (1.0 + scale[:, None, :]) + shift[:, None, :]
    proj = h @ w_in
    split_at = [int(i) for i in np.cumsum(SPLIT_SIZES)[:-1]]
    rq, rk, rv, rg, sq, sk, sv, sg = jnp.split(proj, split_at, axis=-1)

    y_ret = retention(rotary(split_heads(rq, RET_HEADS), pos),
                      rotary(split_heads(rk, RET_HEADS), pos),
                      split_heads(rv, RET_HEADS))
    y_ret = merge_heads(y_ret) * jax.nn.silu(rg)

    y_sb = stick_breaking(split_heads(sq, SB_HEADS), split_heads(sk, SB_HEADS),
                          split_heads(sv, SB_HEADS))
    y_sb = merge_heads(y_sb) * jax.nn.silu(sg)

    y = jnp.concatenate([y_ret, y_sb], axis=-1) @ w_out
    return x + gate[:, None, :] * y

def second_inputs(seed: int = 0) -> dict:
    key = jax.random.key(seed)
    ks = jax.random.split(key, 8)
    f32 = jnp.float32
    x = jax.random.normal(ks[0], (BATCH, SEQ, D_MODEL), f32)
    c = jax.random.normal(ks[1], (BATCH, D_MODEL), f32)
    norm_g = 1.0 + 0.02 * jax.random.normal(ks[2], (DEPTH_2, D_MODEL), f32)
    w_ada = jax.random.normal(ks[3], (DEPTH_2, D_MODEL, 3 * D_MODEL), f32) * (ADA_SCALE * D_MODEL ** -0.5)
    b_ada = 0.02 * jax.random.normal(ks[4], (DEPTH_2, 3 * D_MODEL), f32)
    w_in = jax.random.normal(ks[5], (DEPTH_2, D_MODEL, D_IN_2), f32) * (D_MODEL ** -0.5)
    w_out = jax.random.normal(ks[6], (DEPTH_2, D_MIX_2, D_MODEL), f32) * (D_MIX_2 ** -0.5)
    final_g = 1.0 + 0.02 * jax.random.normal(ks[7], (D_MODEL,), f32)
    return {"x": x, "c": c, "norm_g": norm_g, "w_ada": w_ada, "b_ada": b_ada,
            "w_in": w_in, "w_out": w_out, "final_g": final_g}

def second_block(x, c, norm_g, w_ada, b_ada, w_in, w_out, final_g):
    pos = jnp.arange(x.shape[1], dtype=jnp.float32)
    c_act = jax.nn.silu(c.astype(jnp.float32))
    h = x.astype(jnp.float32)
    for layer in range(DEPTH_2):
        h = hybrid_layer(h, c_act, norm_g[layer], w_ada[layer], b_ada[layer],
                         w_in[layer], w_out[layer], pos)
    return rms_norm_2(h, final_g).astype(x.dtype)


def setup_inputs(seed=0):
    out = dict(first_inputs(seed))
    for name, value in second_inputs(seed + 1).items():
        if name != "x":
            out[name + "_2"] = value
    return out


def reference(
    x, p, g_mix, w_in, g_qa, g_ka, lam_q1, lam_k1, lam_q2, lam_k2, g_sub, g_qb, g_kb, rpb,
    w_out, g_ffn, w_rg, w_re, w1, w3, w2, g_plg, w_plg, w_ple, g_ple, c_2, norm_g_2, w_ada_2,
    b_ada_2, w_in_2, w_out_2, final_g_2,
):
    x = first_block(
        x, p, g_mix, w_in, g_qa, g_ka, lam_q1, lam_k1, lam_q2, lam_k2, g_sub, g_qb, g_kb, rpb,
        w_out, g_ffn, w_rg, w_re, w1, w3, w2, g_plg, w_plg, w_ple, g_ple,
    )
    return second_block(
        x, c_2, norm_g_2, w_ada_2, b_ada_2, w_in_2, w_out_2, final_g_2,
    )


_drawn_inputs = setup_inputs


def setup_inputs(seed=0):
    import zlib

    import numpy as np

    out = dict(_drawn_inputs(seed))
    spreads = {}
    factors = {'g_qa': 2.821,
     'g_ka': 2.707,
     'lam_q1': 2.734,
     'lam_k2': 6.045,
     'g_sub': 3.097,
     'g_qb': 8.0,
     'g_kb': 8.0,
     'rpb': 3.646,
     'g_ffn': 2.7,
     'g_plg': 8.0,
     'g_ple': 6.71,
     'norm_g_2': 8.0,
     'b_ada_2': 4.494,
     'final_g_2': 2.797}
    for name, (base, spread) in spreads.items():
        noise = np.random.default_rng([zlib.crc32(name.encode()), seed]).standard_normal(out[name].shape)
        drawn = base * np.exp(spread * noise) if base else spread * noise
        out[name] = __import__('jax').numpy.asarray(drawn.astype(out[name].dtype))
    for name, factor in factors.items():
        out[name] = (out[name] * factor).astype(out[name].dtype)
    return out
```

```python
import concourse.bass as bass
import numpy as np
from concourse import mybir
from contextlib import ExitStack

F = mybir.dt.float32
R = mybir.dt.float32r
BF = mybir.dt.bfloat16
I32 = mybir.dt.int32
ACT = mybir.ActivationFunctionType
ALU = mybir.AluOpType
X = mybir.AxisListType.X

P = 128
SEQ = 1024
DM = 1024
NT = SEQ // P
KT = DM // P
CH = 512
EPS = 1e-6
BIG = 1e30


class Scope:

    def __init__(self, nc, tag, stack):
        self.nc, self.tag, self.stack = nc, tag, stack
        self.handles = []
        stack.callback(self.finish)

    def finish(self):
        self.nc.clear_and_free_semaphores(self.handles)
        self.nc.all_engine_barrier()

    def sb(self, name, shape, dt=F):
        return self.stack.enter_context(self.nc.sbuf_tensor(f"{self.tag}_{name}", shape, dt))

    def sem(self, name):
        self.handles.append(self.nc.alloc_semaphore(name=f"{self.tag}_{name}"))
        return self.handles[-1]

    def pool_sem(self, name):
        return self.nc.alloc_semaphore(name=f"{self.tag}_{name}")

    def sems(self, name, n):
        return [self.sem(f"{name}{i}") for i in range(n)]

    def pool_sems(self, name, n):
        return [self.pool_sem(f"{name}{i}") for i in range(n)]

    def block(self):
        return self.stack.enter_context(self.nc.Block())


def row_to_all(row, n):
    return row.rearrange("(a n) -> a n", a=1).to_broadcast([P, n])


def dense_phase(nc, k, tag, src, w, dst, kinds, gain=None, shift=None, rope=None, head=None,
                head_gain=None, resid=None, gate=None, times=None):
    C = len(kinds)
    norm = gain is not None
    has_norm = [q in ("norm", "normrope") for q in kinds]
    has_rope = [q in ("normrope", "rope") for q in kinds]
    is_head = [a or b for a, b in zip(has_norm, has_rope)]
    extras = resid is not None

    def before(flags, c):
        return NT * sum(flags[:c])

    with ExitStack() as stack:
        s = Scope(nc, tag, stack)
        x = [s.sb(f"x{p}", [P, DM]) for p in range(2)]
        xh = s.sb("xh", [P, KT, SEQ], R)
        xl = s.sb("xl", [P, KT, SEQ], R)
        raw = s.sb("raw", [P, 2, KT, CH])
        wh = s.sb("wh", [P, 2, KT, CH], R)
        wl = s.sb("wl", [P, 2, KT, CH], R)
        out = [s.sb(f"out{p}", [P, CH]) for p in range(2)]
        psT = k.ps[:, 0:2, :].rearrange("p b n -> p (b n)")

        x_loaded = s.pool_sems("x_loaded", 2)
        raw_loaded, stored, extra_loaded = (s.sems(n, 2) for n in ("raw_loaded", "stored", "extra_loaded"))
        consts_loaded = s.sem("consts_loaded")
        x_ss, x_ms, x_sd, x_rs, x_scaled, x_ready, x_turned, x_hi, x_lo = (s.sem(n) for n in (
            "x_ss", "x_ms", "x_sd", "x_rs", "x_scaled", "x_ready", "x_turned", "x_hi", "x_lo"))
        w_hi, w_lo, product, out_ready = (s.sem(n) for n in ("w_hi", "w_lo", "product", "out_ready"))

        consts = []
        if norm:
            junk = s.sb("junk", [P, DM], BF)
            ss, ms, sd, rs = (s.sb(n, [P, NT]) for n in ("ss", "ms", "sd", "rs"))
            gain_b = s.sb("gain", [P, DM])
            consts.append((gain_b[:], row_to_all(gain, DM)))
            if shift is not None:
                shift_b = s.sb("shift", [P, DM])
                consts.append((shift_b[:], row_to_all(shift, DM)))
        if any(is_head):
            y = [s.sb(f"y{p}", [P, CH]) for p in range(2)]
            y2 = [s.sb(f"sq{p}", [P, CH]) for p in range(2)]
            z = [s.sb(f"z{p}", [P, CH]) for p in range(2)]
            hss, hms, hsd, hrs = (s.sb(n, [P, 16]) for n in ("hss", "hms", "hsd", "hrs"))
            h_val, hd_sq, hd_ss, hd_ms, hd_sd, hd_rs, hd_scaled, hd_gained, hd_cos, hd_sin = (
                s.sem(n) for n in ("h_val", "hd_sq", "hd_ss", "hd_ms", "hd_sd", "hd_rs", "hd_scaled",
                                   "hd_gained", "hd_cos", "hd_sin"))
            if any(has_rope):
                RD = rope[2]
                cos_t = s.sb("cos", [P, NT, RD // 2])
                sin_t = s.sb("sin", [P, NT, RD])
                consts.append((cos_t[:], rope[0].rearrange("(t p) d -> p t d", p=P)))
                consts.append((sin_t[:], rope[1].rearrange("(t p) d -> p t d", p=P)))
            hg = {}
            for c, row in (head_gain or {}).items():
                hg[c] = s.sb(f"hg{c}", [P, head[c]])
                consts.append((hg[c][:], row_to_all(row, head[c])))
        if extras:
            rt = [s.sb(f"rt{p}", [P, CH]) for p in range(2)]
            mid = [s.sb(f"mid{p}", [P, CH]) for p in range(2)]
            mid_done = s.sem("mid_done")
            if times is not None:
                tt = [s.sb(f"tt{p}", [P, CH]) for p in range(2)]
                sg = s.sb("sg", [P, CH])
                sg_done = s.sem("sg_done")
            if gate is not None:
                gate_b = s.sb("gate", [P, DM])
                consts.append((gate_b[:], row_to_all(gate, DM)))
        n_extra = 32 if times is not None else 16
        block = s.block()
        w_v = w.rearrange("(k p) n -> p k n", p=P)

        @block.sync
        def _(sp):
            sp.dma_start(raw[:, 0, 0:KT // 2, :], w_v[:, 0:KT // 2, 0:CH]).then_inc(raw_loaded[0], 16)
            sp.dma_start(raw[:, 0, KT // 2:, :], w_v[:, KT // 2:, 0:CH]).then_inc(raw_loaded[0], 16)
            for to, of in consts:
                sp.dma_start(to, of).then_inc(consts_loaded, 16)
            sp.dma_start(raw[:, 1, :, :], w_v[:, :, CH:2 * CH]).then_inc(raw_loaded[1], 16)

            def load_extra(c, t, p):
                rows = bass.ds(t * P, P)
                sp.dma_start(rt[p][:], resid[rows, c * CH:(c + 1) * CH]).then_inc(extra_loaded[p], 16)
                if times is not None:
                    sp.dma_start(tt[p][:], times[rows, c * CH:(c + 1) * CH]).then_inc(extra_loaded[p], 16)

            def tile(c, t, p, ahead):
                sp.wait_ge(out_ready, c * NT + t + 1)
                sp.dma_start(dst[bass.ds(t * P, P), c * CH:(c + 1) * CH], out[p][:]).then_inc(stored[p], 16)
                if extras and ahead is not None:
                    load_extra(*ahead, p)

            if extras:
                for p in range(2):
                    load_extra(0, p, p)
            for c in range(C):
                if c + 2 < C:
                    sp.wait_ge(w_lo, KT * (c + 1))
                    sp.dma_start(raw[:, c % 2, :, :], w_v[:, :, (c + 2) * CH:(c + 3) * CH]).then_inc(raw_loaded[c % 2], 16)
                with sp.Fori(0, NT // 2 - 1) as j:
                    for p in range(2):
                        tile(c, 2 * j + p, p, (c, 2 * j + p + 2))
                for p in range(2):
                    tile(c, NT - 2 + p, p, (c + 1, p) if c + 1 < C else None)
            for p in range(2):
                sp.wait_ge(stored[p], 16 * C * NT // 2)

        @block.gpsimd
        def _(pool):
            for p in range(2):
                pool.dma_start(x[p][:], src[p * P:(p + 1) * P, :]).then_inc(x_loaded[p], 16)
            with pool.Fori(0, NT // 2 - 1) as j:
                for p in range(2):
                    pool.wait_ge(x_turned, 2 * j + p + 1)
                    pool.dma_start(x[p][:], src[bass.ds((2 * j + p + 2) * P, P), :]).then_inc(x_loaded[p], 16)

        @block.scalar
        def _(act):
            def split(c, kt):
                act.copy(wh[:, c % 2, bass.ds(kt, 1), :], raw[:, c % 2, bass.ds(kt, 1), :]).then_inc(w_hi, 1)

            def normalise(t, p, j):
                if norm:
                    act.wait_ge(x_loaded[p], 16 * (j + 1))
                    act.activation(junk[:], x[p][:], ACT.Square, accum_out=ss[:, bass.ds(t, 1)]).then_inc(x_ss, 1)
                    act.wait_ge(x_ms, t + 1)
                    act.activation(sd[:, bass.ds(t, 1)], ms[:, bass.ds(t, 1)], ACT.Sqrt).then_inc(x_sd, 1)
                act.wait_ge(x_turned, t + 1)
                act.copy(xh[:, :, bass.ds(t * P, P)], psT.rearrange("p (k n) -> p k n", k=KT)).then_inc(x_hi, 1)

            def post(c, t, p, j):
                kind = kinds[c]
                act.wait_ge(product, c * NT + t + 1)
                if kind in ("copy", "silu"):
                    act.wait_ge(stored[p], 16 * (c * NT // 2 + j))
                    if kind == "copy":
                        act.copy(out[p][:], k.ps[:, 2 + p, :]).then_inc(out_ready, 1)
                    else:
                        act.activation(out[p][:], k.ps[:, 2 + p, :], ACT.Silu).then_inc(out_ready, 1)
                elif is_head[c]:
                    act.copy(y[p][:], k.ps[:, 2 + p, :]).then_inc(h_val, 1)
                    if has_norm[c]:
                        act.activation(y2[p][:], k.ps[:, 2 + p, :], ACT.Square).then_inc(hd_sq, 1)
                        n = before(has_norm, c) + t
                        act.wait_ge(hd_ms, n + 1)
                        G = CH // head[c]
                        act.activation(hsd[:, 0:G], hms[:, 0:G], ACT.Sqrt).then_inc(hd_sd, 1)
                elif kind == "gated":
                    if not isinstance(t, int) or c * NT + t > 0:
                        act.wait_ge(mid_done, c * NT + t)
                    act.activation(sg[:], k.ps[:, 2 + p, :], ACT.Sigmoid).then_inc(sg_done, 1)

            act.preload_act_table(ACT.Sqrt if norm or any(has_norm) else ACT.Sigmoid if times is not None else ACT.Copy)
            act.wait_ge(raw_loaded[0], 32)
            with act.Fori(0, KT) as kt:
                split(0, kt)
            normalise(0, 0, 0)
            for c in range(C):
                if kinds[c] == "silu":
                    act.preload_act_table(ACT.Silu)
                if c + 1 < C:
                    act.wait_ge(raw_loaded[(c + 1) % 2], 16 * ((c + 1) // 2 + 1 + ((c + 1) % 2 == 0)))
                if c == 0:
                    with act.Fori(0, NT // 2 - 1) as j:
                        for p in range(2):
                            normalise(2 * j + p + 1, 1 - p, j + p)
                            post(c, 2 * j + p, p, j)
                            if c + 1 < C:
                                split(c + 1, 2 * j + p)
                    normalise(NT - 1, 1, NT // 2 - 1)
                    for p in range(2):
                        post(c, NT - 2 + p, p, NT // 2 - 1)
                        if c + 1 < C:
                            split(c + 1, NT - 2 + p)
                else:
                    with act.Fori(0, NT // 2) as j:
                        for p in range(2):
                            post(c, 2 * j + p, p, j)
                            if c + 1 < C:
                                split(c + 1, 2 * j + p)

        @block.vector
        def _(dve):
            def split(c, kt):
                dve.wait_ge(w_hi, c * KT + kt + 1)
                dve.tensor_tensor(wl[:, c % 2, bass.ds(kt, 1), :], raw[:, c % 2, bass.ds(kt, 1), :],
                                  wh[:, c % 2, bass.ds(kt, 1), :].bitcast(F), ALU.subtract).then_inc(w_lo, 1)

            def normalise(t, p):
                one = bass.ds(t, 1)
                if norm:
                    dve.wait_ge(x_ss, t + 1)
                    dve.tensor_scalar(ms[:, one], ss[:, one], 1.0 / DM, EPS, ALU.mult, ALU.add).then_inc(x_ms, 1)
                    dve.wait_ge(x_sd, t + 1)
                    dve.reciprocal(rs[:, one], sd[:, one]).then_inc(x_rs, 1)
                    dve.wait_ge(x_rs, t + 1)
                    last = dve.scalar_tensor_tensor(out=x[p][:], in0=x[p][:], scalar=rs[:, one], in1=gain_b[:],
                                                    op0=ALU.mult, op1=ALU.mult)
                    if shift is not None:
                        last.then_inc(x_scaled, 1)
                        dve.wait_ge(x_scaled, t + 1)
                        last = dve.tensor_tensor(x[p][:], x[p][:], shift_b[:], ALU.add)
                    last.then_inc(x_ready, 1)
                dve.wait_ge(x_hi, t + 1)
                cols = bass.ds(t * P, P)
                dve.tensor_tensor(xl[:, :, cols], psT.rearrange("p (k n) -> p k n", k=KT),
                                  xh[:, :, cols].bitcast(F), ALU.subtract).then_inc(x_lo, 1)

            def post(c, t, p, j):
                g = c * NT + t
                if is_head[c]:
                    n, r, h = before(has_norm, c) + t, before(has_rope, c) + t, before(is_head, c) + t
                    dve.wait_ge(h_val, h + 1)
                    if has_norm[c]:
                        D = head[c]
                        G = CH // D
                        yv = y[p][:].rearrange("p (g d) -> p g d", d=D)
                        dve.wait_ge(hd_sq, n + 1)
                        dve.tensor_reduce(hss[:, 0:G], y2[p][:].rearrange("p (g d) -> p g d", d=D), X,
                                          ALU.add).then_inc(hd_ss, 1)
                        dve.wait_ge(hd_ss, n + 1)
                        dve.tensor_scalar(hms[:, 0:G], hss[:, 0:G], 1.0 / D, EPS, ALU.mult, ALU.add).then_inc(hd_ms, 1)
                        dve.wait_ge(hd_sd, n + 1)
                        dve.reciprocal(hrs[:, 0:G], hsd[:, 0:G]).then_inc(hd_rs, 1)
                        dve.wait_ge(hd_rs, n + 1)
                        dve.tensor_tensor(yv, yv, hrs[:, 0:G].rearrange("p (g o) -> p g o", o=1).to_broadcast([P, G, D]),
                                          ALU.mult).then_inc(hd_scaled, 1)
                        dve.wait_ge(hd_scaled, n + 1)
                        gb = hg[c][:].rearrange("p (o d) -> p o d", o=1).to_broadcast([P, G, D])
                        if not has_rope[c]:
                            dve.wait_ge(stored[p], 16 * (c * NT // 2 + j))
                            dve.tensor_tensor(out[p][:].rearrange("p (g d) -> p g d", d=D), yv, gb,
                                              ALU.mult).then_inc(out_ready, 1)
                        else:
                            dve.tensor_tensor(yv, yv, gb, ALU.mult).then_inc(hd_gained, 1)
                            dve.wait_ge(hd_gained, r + 1)
                    if has_rope[c]:
                        dve.wait_ge(stored[p], 16 * (c * NT // 2 + j))
                        G, Hf = CH // RD, RD // 2
                        y4 = y[p][:].rearrange("p (g a d) -> p g a d", a=2, d=Hf)
                        c4 = cos_t[:, bass.ds(t, 1), :].rearrange("p o (a d) -> p o a d", a=1).to_broadcast([P, G, 2, Hf])
                        dve.tensor_tensor(y2[p][:].rearrange("p (g a d) -> p g a d", a=2, d=Hf), y4, c4,
                                          ALU.mult).then_inc(hd_cos, 1)
                        s4 = sin_t[:, bass.ds(t, 1), :].rearrange("p o (a d) -> p o a d", a=2).to_broadcast([P, G, 2, Hf])
                        dve.tensor_tensor(z[p][:].rearrange("p (g a d) -> p g a d", a=2, d=Hf), y4[:, :, ::-1, :], s4,
                                          ALU.mult).then_inc(hd_sin, 1)
                        dve.wait_ge(hd_cos, r + 1)
                        dve.wait_ge(hd_sin, r + 1)
                        dve.tensor_tensor(out[p][:], y2[p][:], z[p][:], ALU.add).then_inc(out_ready, 1)
                elif kinds[c] == "resid":
                    dve.wait_ge(extra_loaded[p], n_extra * (c * NT // 2 + j + 1))
                    dve.wait_ge(product, g + 1)
                    dve.wait_ge(stored[p], 16 * (c * NT // 2 + j))
                    if gate is None:
                        dve.tensor_tensor(out[p][:], k.ps[:, 2 + p, :], rt[p][:], ALU.add).then_inc(out_ready, 1)
                    else:
                        dve.tensor_tensor(mid[p][:], k.ps[:, 2 + p, :], gate_b[:, c * CH:(c + 1) * CH],
                                          ALU.mult).then_inc(mid_done, 1)
                        dve.wait_ge(mid_done, g + 1)
                        dve.tensor_tensor(out[p][:], mid[p][:], rt[p][:], ALU.add).then_inc(out_ready, 1)
                elif kinds[c] == "gated":
                    dve.wait_ge(extra_loaded[p], n_extra * (c * NT // 2 + j + 1))
                    dve.wait_ge(sg_done, g + 1)
                    dve.wait_ge(stored[p], 16 * (c * NT // 2 + j))
                    dve.tensor_tensor(mid[p][:], sg[:], tt[p][:], ALU.mult).then_inc(mid_done, 1)
                    dve.wait_ge(mid_done, g + 1)
                    dve.tensor_tensor(out[p][:], mid[p][:], rt[p][:], ALU.add).then_inc(out_ready, 1)

            with dve.Fori(0, KT) as kt:
                split(0, kt)
            dve.wait_ge(consts_loaded, 16 * len(consts))
            normalise(0, 0)
            for c in range(C):
                if c > 0 and c + 1 < C:
                    dve.wait_ge(product, c * NT)
                if c == 0:
                    with dve.Fori(0, NT // 2 - 1) as j:
                        for p in range(2):
                            normalise(2 * j + p + 1, 1 - p)
                            post(c, 2 * j + p, p, j)
                            if c + 1 < C:
                                split(c + 1, 2 * j + p)
                    normalise(NT - 1, 1)
                    for p in range(2):
                        post(c, NT - 2 + p, p, NT // 2 - 1)
                        if c + 1 < C:
                            split(c + 1, NT - 2 + p)
                else:
                    with dve.Fori(0, NT // 2) as j:
                        for p in range(2):
                            post(c, 2 * j + p, p, j)
                            if c + 1 < C:
                                split(c + 1, 2 * j + p)

        @block.tensor
        def _(pe):
            def turn(t):
                p = t % 2
                if norm:
                    pe.wait_ge(x_ready, t + 1)
                else:
                    pe.wait_ge(x_loaded[p], 16 * (t // 2 + 1))
                if t:
                    pe.wait_ge(x_lo, t)
                for kt in range(KT):
                    last = pe.transpose(psT[:, kt * P:(kt + 1) * P], x[p][:, kt * P:(kt + 1) * P], k.ident[:])
                last.then_inc(x_turned, 1)

            def multiply(c, b, t):
                p = t % 2
                for kt in range(KT):
                    if isinstance(c, int) and t == 0:
                        pe.wait_ge(w_lo, kt + 1)
                    tok = slice(t * P, (t + 1) * P)
                    o = k.ps[:, 2 + p, :]
                    wb = [v[:, bass.ds(b, 1), kt, :].rearrange("p o n -> p (o n)") for v in (wh, wl)]
                    pe.matmul(o, xh[:, kt, tok], wb[0], start=(kt == 0), stop=False)
                    pe.matmul(o, xh[:, kt, tok], wb[1], start=False, stop=False)
                    last = pe.matmul(o, xl[:, kt, tok], wb[0], start=False, stop=(kt == KT - 1))
                last.then_inc(product, 1)

            turn(0)
            for t in range(NT):
                if t + 1 < NT:
                    turn(t + 1)
                pe.wait_ge(x_lo, t + 1)
                if t >= 2:
                    pe.wait_ge(out_ready, t - 1)
                multiply(0, 0, t)
            with pe.Fori(1, C) as c:
                pe.wait_ge(w_lo, c * KT + KT)
                b = pe.snap(c % 2)
                for t in range(NT):
                    pe.wait_ge(out_ready, c * NT + t - 1)
                    multiply(c, b, t)


N_GROUPS, PER_GROUP, TOP_K, D_EXPERT = 4, 8, 2, 512
N_EXPERTS = N_GROUPS * PER_GROUP
MAX_BLOCKS = SEQ * TOP_K // P + N_EXPERTS
LEAST_BLOCKS = SEQ * TOP_K // P


def router_phase(nc, k, src, gain, w_rg, w_re, consts, token_ids):
    NL = N_GROUPS + N_EXPERTS
    N_CONSTS = 9
    rev, thresholds, block_no = consts[0:8], consts[8:16], consts[16:16 + MAX_BLOCKS]
    with ExitStack() as stack:
        s = Scope(nc, "rt", stack)
        x = [s.sb(f"x{p}", [P, DM]) for p in range(2)]
        junk = s.sb("junk", [P, DM], BF)
        gain_b = s.sb("gain", [P, DM])
        xt = [s.sb(f"xt{p}", [P, DM]) for p in range(2)]
        wr = s.sb("wr", [P, KT, NL])
        ss, ms, sd, rs = (s.sb(n, [P, NT]) for n in ("ss", "ms", "sd", "rs"))
        L = s.sb("L", [P, NT, NL])
        tri, ones = s.sb("tri", [P, P]), s.sb("ones", [P, P])
        tok = s.sb("tok", [P, TOP_K, NT, 2], I32)
        spare = s.sb("spare", [P, MAX_BLOCKS, 2], I32)
        slot = s.sb("slot", [P, TOP_K, NT], I32)
        rev_b, thr_b, no_b = s.sb("rev", [P, 8]), s.sb("thr", [P, 8]), s.sb("no", [P, MAX_BLOCKS])
        gmax, gsum, gate, kmax = (s.sb(n, [P, NT]) for n in ("gmax", "gsum", "gate", "kmax"))
        gd, gexp, gkey, goh = (s.sb(n, [P, NT, N_GROUPS]) for n in ("gd", "gexp", "gkey", "goh"))
        grouped = s.sb("grouped", [P, NT, N_EXPERTS])
        sel, d1, key, low = (s.sb(n, [P, NT, PER_GROUP]) for n in ("sel", "d1", "key", "low"))
        oh = [s.sb(f"oh{i}", [P, NT, PER_GROUP]) for i in range(2)]
        top = [s.sb(f"top{i}", [P, NT]) for i in range(2)]
        dtop, etop, den, rden = (s.sb(n, [P, NT]) for n in ("dtop", "etop", "den", "rden"))
        M = [s.sb(f"M{i}", [P, NT, N_EXPERTS]) for i in range(2)]
        both = s.sb("both", [P, NT, N_EXPERTS])
        ahead = s.sb("ahead", [P, NT + 1, N_EXPERTS])
        more = s.sb("more", [P, N_EXPERTS, 8])
        blocks, upto, first = (s.sb(n, [P, N_EXPERTS]) for n in ("blocks", "upto", "first"))
        place, mine = (s.sb(n, [P, NT, N_EXPERTS]) for n in ("place", "mine"))
        slot_f = s.sb("slot_f", [P, NT])
        past = s.sb("past", [P, MAX_BLOCKS, N_EXPERTS])
        be_f = s.sb("be_f", [P, MAX_BLOCKS])
        psT = k.ps[:, 0:2, :].rearrange("p b n -> p (b n)")
        ps_logit = k.ps[:, 2, 0:NT * NL]
        ps_rank = k.ps[:, 3, 0:NT * N_EXPERTS]
        ps_count = k.ps[:, 4, 0:N_EXPERTS]

        x_loaded, x_stored = s.pool_sems("x_loaded", 2), s.sems("x_stored", 2)
        consts_loaded, cleared, spare_written = (s.sem(n) for n in ("consts_loaded", "cleared", "spare_written"))
        scattered = s.pool_sem("scattered")
        x_ss, x_ms, x_sd, x_rs, x_ready, x_turned, x_out, logits = (s.sem(n) for n in (
            "x_ss", "x_ms", "x_sd", "x_rs", "x_ready", "x_turned", "x_out", "logits"))
        did, gd_done, gexp_done, dtop_done, etop_done, ahead_done, ranked, slots_done = (s.sem(n) for n in (
            "did", "gd_done", "gexp_done", "dtop_done", "etop_done", "ahead_done", "ranked", "slots_done"))
        block = s.block()

        @block.sync
        def _(sp):
            loads = [(gain_b[:], row_to_all(gain, DM)), (wr[:, :, 0:N_GROUPS], w_rg.rearrange("(k p) n -> p k n", p=P)),
                     (wr[:, :, N_GROUPS:NL], w_re.rearrange("(k p) n -> p k n", p=P)),
                     (tri[:], k.tri_dram), (tok[:], token_ids[0:TOP_K * SEQ, :].rearrange("(i t p) a -> p i t a", p=P, i=TOP_K)),
                     (spare[:], token_ids[TOP_K * SEQ:, :].rearrange("(b p) a -> p b a", p=P)),
                     (rev_b[:], row_to_all(rev, 8)), (thr_b[:], row_to_all(thresholds, 8)),
                     (no_b[:], row_to_all(block_no, MAX_BLOCKS))]
            for to, of in loads:
                sp.dma_start(to, of, allow_slow_non_contiguous=True).then_inc(consts_loaded, 16)
            sp.wait_ge(consts_loaded, 16 * N_CONSTS)
            sp.dma_start(k.slot_rows.rearrange("(b p) a -> p b a", p=P), spare[:],
                         allow_slow_non_contiguous=True).then_inc(spare_written, 16)
            with sp.Fori(0, NT // 2) as j:
                for p in range(2):
                    t = 2 * j + p
                    sp.wait_ge(x_ready, t + 1)
                    sp.dma_start(k.xn[bass.ds(t * P, P), :], x[p][:]).then_inc(x_stored[p], 16)
            for p in range(2):
                sp.wait_ge(x_stored[p], 16 * NT // 2)

        @block.gpsimd
        def _(pool):
            for p in range(2):
                pool.dma_start(x[p][:], src[p * P:(p + 1) * P, :]).then_inc(x_loaded[p], 16)
            pool.memset(ones[:], 1.0).then_inc(cleared, 1)
            pool.memset(ahead[:, 0, :], 0.0).then_inc(cleared, 1)
            with pool.Fori(0, NT // 2 - 1) as j:
                for p in range(2):
                    pool.wait_ge(x_turned, 2 * j + p + 1)
                    pool.wait_ge(x_stored[p], 16 * (j + 1))
                    pool.dma_start(x[p][:], src[bass.ds((2 * j + p + 2) * P, P), :]).then_inc(x_loaded[p], 16)
            pool.wait_ge(spare_written, 16)
            pool.wait_ge(consts_loaded, 16 * N_CONSTS)
            pool.wait_ge(slots_done, 2)
            for i in range(TOP_K):
                for t in range(NT):
                    pool.indirect_dma_start(
                        out=k.slot_rows[:, :], out_offset=bass.IndirectOffsetOnAxis(ap=slot[:, i, t:t + 1], axis=0),
                        in_=tok[:, i, t, :], in_offset=None).then_inc(scattered, 16)
            pool.wait_ge(scattered, 16 * TOP_K * NT)

        @block.scalar
        def _(act):
            act.preload_act_table(ACT.Sqrt)
            with act.Fori(0, NT // 2) as j:
                for p in range(2):
                    t = 2 * j + p
                    one = bass.ds(t, 1)
                    act.wait_ge(x_loaded[p], 16 * (j + 1))
                    act.activation(junk[:], x[p][:], ACT.Square, accum_out=ss[:, one]).then_inc(x_ss, 1)
                    act.wait_ge(x_ms, t + 1)
                    act.activation(sd[:, one], ms[:, one], ACT.Sqrt).then_inc(x_sd, 1)
                    act.wait_ge(x_turned, t + 1)
                    act.wait_ge(logits, 2 * j)
                    act.copy(xt[p][:], psT).then_inc(x_out, 1)
            act.preload_act_table(ACT.Exp)
            act.wait_ge(gd_done, 1)
            act.activation(gexp[:], gd[:], ACT.Exp).then_inc(gexp_done, 1)
            act.wait_ge(dtop_done, 1)
            act.activation(etop[:], dtop[:], ACT.Exp).then_inc(etop_done, 1)

        @block.tensor
        def _(pe):
            with pe.Fori(0, NT // 2) as j:
                for p in range(2):
                    t = 2 * j + p
                    pe.wait_ge(x_ready, t + 1)
                    pe.wait_ge(x_out, t)
                    for kt in range(KT):
                        last = pe.transpose(psT[:, kt * P:(kt + 1) * P], x[p][:, kt * P:(kt + 1) * P], k.ident[:])
                    last.then_inc(x_turned, 1)
                    pe.wait_ge(consts_loaded, 16 * N_CONSTS)
                    pe.wait_ge(x_out, t + 1)
                    for kt in range(KT):
                        last = pe.matmul(ps_logit[:, bass.ds(t * NL, NL)], xt[p][:, kt * P:(kt + 1) * P], wr[:, kt, :],
                                         start=(kt == 0), stop=(kt == KT - 1))
                    last.then_inc(logits, 1)
            pe.wait_ge(cleared, 2)
            pe.wait_ge(ahead_done, NT + 1)
            pe.matmul(ps_rank, tri[:], both[:].rearrange("p t e -> p (t e)"), start=True, stop=False)
            pe.matmul(ps_rank, ones[:], ahead[:, 0:NT, :].rearrange("p t e -> p (t e)"), start=False, stop=True)
            pe.matmul(ps_count, ones[:], ahead[:, NT, :], start=True, stop=True).then_inc(ranked, 1)

        @block.vector
        def _(dve):
            with dve.Fori(0, NT // 2) as j:
                for p in range(2):
                    t = 2 * j + p
                    one = bass.ds(t, 1)
                    dve.wait_ge(x_ss, t + 1)
                    dve.tensor_scalar(ms[:, one], ss[:, one], 1.0 / DM, EPS, ALU.mult, ALU.add).then_inc(x_ms, 1)
                    dve.wait_ge(x_sd, t + 1)
                    dve.reciprocal(rs[:, one], sd[:, one]).then_inc(x_rs, 1)
                    dve.wait_ge(x_rs, t + 1)
                    dve.wait_ge(consts_loaded, 16 * N_CONSTS)
                    dve.scalar_tensor_tensor(out=x[p][:], in0=x[p][:], scalar=rs[:, one], in1=gain_b[:],
                                             op0=ALU.mult, op1=ALU.mult).then_inc(x_ready, 1)
            n = [0]

            def link(ins):
                n[0] += 1
                ins.then_inc(did, 1)
                dve.wait_ge(did, n[0])

            def spread(row, width):
                return row.rearrange("p (t o) -> p t o", o=1).to_broadcast([P, NT, width])

            def each(row, width):
                return row.rearrange("p (o n) -> p o n", o=1).to_broadcast([P, NT, width])

            def first_of(values, largest, hot, width, keys):
                link(dve.tensor_tensor(keys, values, spread(largest, width), ALU.is_ge))
                link(dve.tensor_tensor(keys, keys, each(rev_b[:, 8 - width:8], width), ALU.mult))
                link(dve.tensor_reduce(kmax[:], keys, X, ALU.max))
                link(dve.tensor_tensor(hot, keys, spread(kmax[:], width), ALU.is_equal))

            dve.wait_ge(logits, NT)
            link(dve.tensor_copy(L[:], ps_logit.rearrange("p (t n) -> p t n", n=NL)))
            gl = L[:, :, 0:N_GROUPS]
            link(dve.tensor_reduce(gmax[:], gl, X, ALU.max))
            dve.tensor_tensor(gd[:], gl, spread(gmax[:], N_GROUPS), ALU.subtract).then_inc(gd_done, 1)
            first_of(gl, gmax[:], goh[:], N_GROUPS, gkey[:])
            link(dve.tensor_tensor(grouped[:].rearrange("p t (g e) -> p t g e", g=N_GROUPS),
                                   L[:, :, N_GROUPS:NL].rearrange("p t (g e) -> p t g e", g=N_GROUPS),
                                   goh[:].rearrange("p t (g o) -> p t g o", o=1).to_broadcast([P, NT, N_GROUPS, PER_GROUP]),
                                   ALU.mult))
            link(dve.tensor_reduce(sel[:], grouped[:].rearrange("p t (g e) -> p t e g", g=N_GROUPS), X, ALU.add))
            link(dve.tensor_reduce(top[0][:], sel[:], X, ALU.max))
            first_of(sel[:], top[0][:], oh[0][:], PER_GROUP, key[:])
            link(dve.scalar_tensor_tensor(out=low[:], in0=oh[0][:], scalar=-BIG, in1=sel[:], op0=ALU.mult, op1=ALU.add))
            link(dve.tensor_reduce(top[1][:], low[:], X, ALU.max))
            dve.tensor_tensor(dtop[:], top[1][:], top[0][:], ALU.subtract).then_inc(dtop_done, 1)
            first_of(low[:], top[1][:], oh[1][:], PER_GROUP, key[:])
            for i in range(2):
                link(dve.tensor_tensor(M[i][:].rearrange("p t (g e) -> p t g e", g=N_GROUPS),
                                       goh[:].rearrange("p t (g o) -> p t g o", o=1).to_broadcast([P, NT, N_GROUPS, PER_GROUP]),
                                       oh[i][:].rearrange("p t (o e) -> p t o e", o=1).to_broadcast([P, NT, N_GROUPS, PER_GROUP]),
                                       ALU.mult))
            dve.tensor_tensor(both[:], M[0][:], M[1][:], ALU.add).then_inc(ahead_done, 1)
            dve.wait_ge(cleared, 2)
            for t in range(NT):
                dve.wait_ge(ahead_done, t + 1)
                dve.tensor_tensor(ahead[:, t + 1, :], ahead[:, t, :], both[:, t, :], ALU.add).then_inc(ahead_done, 1)
            dve.wait_ge(gexp_done, 1)
            link(dve.tensor_reduce(gsum[:], gexp[:], X, ALU.add))
            link(dve.reciprocal(gate[:], gsum[:]))
            dve.wait_ge(etop_done, 1)
            link(dve.tensor_scalar(den[:], etop[:], 1.0, None, ALU.add))
            link(dve.reciprocal(rden[:], den[:]))
            link(dve.tensor_tensor(k.slot_w[:, 0, :], gate[:], rden[:], ALU.mult))
            link(dve.tensor_tensor(k.slot_w[:, 1, :], k.slot_w[:, 0, :], etop[:], ALU.mult))
            dve.wait_ge(ranked, 1)
            link(dve.tensor_copy(blocks[:], ps_count))
            link(dve.tensor_tensor(more[:], blocks[:].rearrange("p (e o) -> p e o", o=1).to_broadcast([P, N_EXPERTS, 8]),
                                   thr_b[:].rearrange("p (o i) -> p o i", o=1).to_broadcast([P, N_EXPERTS, 8]), ALU.is_gt))
            link(dve.tensor_reduce(blocks[:], more[:], X, ALU.add))
            link(dve.tensor_tensor_scan(upto[:], blocks[:], blocks[:], 0.0, ALU.add, ALU.bypass))
            link(dve.tensor_tensor(first[:], upto[:], blocks[:], ALU.subtract))
            link(dve.tensor_scalar(first[:], first[:], float(P), None, ALU.mult))
            link(dve.tensor_tensor(place[:], ps_rank.rearrange("p (t e) -> p t e", e=N_EXPERTS),
                                   each(first[:], N_EXPERTS), ALU.add))
            for i in range(TOP_K):
                link(dve.tensor_tensor(mine[:], place[:], M[i][:], ALU.mult))
                link(dve.tensor_reduce(slot_f[:], mine[:], X, ALU.add))
                dve.tensor_copy(slot[:, i, :], slot_f[:]).then_inc(slots_done, 1)
                dve.wait_ge(slots_done, i + 1)
            link(dve.tensor_tensor(past[:], upto[:].rearrange("p (o e) -> p o e", o=1).to_broadcast([P, MAX_BLOCKS, N_EXPERTS]),
                                   no_b[:].rearrange("p (b o) -> p b o", o=1).to_broadcast([P, MAX_BLOCKS, N_EXPERTS]), ALU.is_le))
            link(dve.tensor_reduce(be_f[:], past[:], X, ALU.add))
            link(dve.tensor_copy(k.block_expert[:, 0:MAX_BLOCKS], be_f[:]))
            link(dve.tensor_scalar(k.block_expert[:, MAX_BLOCKS:MAX_BLOCKS + 1], upto[:, N_EXPERTS - 1:N_EXPERTS],
                                   -2.0, None, ALU.add))


def expert_phase(nc, k, w1, w3, w2):
    HK = KT // 2
    YK = D_EXPERT // P
    with ExitStack() as stack:
        s = Scope(nc, "ex", stack)
        names = ["w1a", "w1b", "w3a", "w3b"]
        raw_h, hi_h, lo_h = ([s.sb(f"{v}_{n}", [P, HK, CH], dt) for n in names]
                             for v, dt in (("raw", F), ("hi", R), ("lo", R)))
        raw_y, hi_y, lo_y = ([s.sb(f"{v}_w2{n}", [P, YK, CH], dt) for n in "ab"]
                             for v, dt in (("raw", F), ("hi", R), ("lo", R)))
        idx = s.sb("idx", [P, 2], I32)
        row = s.sb("row", [P, 2], I32)
        idx_own, row_own = s.sb("idx_own", [P, 2], I32), s.sb("row_own", [P, 2], I32)
        nothing = s.sb("nothing", [P, 2], I32)
        copied = s.sem("copied")
        xg = s.sb("xg", [P, DM])
        xh, xl = s.sb("xh", [P, KT, P], R), s.sb("xl", [P, KT, P], R)
        act1, hid = s.sb("act1", [P, CH]), s.sb("hid", [P, CH])
        hh, hl = s.sb("hh", [P, YK, P], R), s.sb("hl", [P, YK, P], R)
        y = s.sb("y", [P, DM])
        psX = k.ps[:, 0:2, :].rearrange("p b n -> p (b n)")
        psH = [k.ps[:, 2, :], k.ps[:, 3, :]]
        psHT = k.ps[:, 4, :]
        psY = [k.ps[:, 5, :], k.ps[:, 6, :]]

        h_loaded, y_loaded = s.sems("h_loaded", 4), s.sems("y_loaded", 2)
        idx_loaded, row_loaded, gathered, stored = (s.pool_sem(n) for n in ("idx_loaded", "row_loaded", "gathered", "stored"))
        h_hi, h_lo, h_used, y_hi, y_lo, y_used = (s.sem(n) for n in (
            "h_hi", "h_lo", "h_used", "y_hi", "y_lo", "y_used"))
        x_turned, x_hi, x_lo, silu_done, hid_ready, hid_turned, hid_hi, hid_lo, y_out = (s.sem(n) for n in (
            "x_turned", "x_hi", "x_lo", "silu_done", "hid_ready", "hid_turned", "hid_hi", "hid_lo", "y_out"))
        block = s.block()

        def blocks_less_2(eng):
            return eng.value_load(k.block_expert[0:1, MAX_BLOCKS:MAX_BLOCKS + 1], min_val=LEAST_BLOCKS - 2,
                                  max_val=MAX_BLOCKS - 3)

        @block.sync
        def _(sp):
            def expert(n):
                return sp.value_load(k.block_expert[0:1, bass.ds(n, 1)], min_val=0, max_val=N_EXPERTS - 1)

            def load_h(n):
                e = bass.ds(expert(n), 1)
                for i, w in enumerate((w1, w3)):
                    for half in range(2):
                        j = 2 * i + half
                        if not isinstance(n, int) or n > 0:
                            sp.wait_ge(h_lo, 4 * (n - 1) + j + 1)
                        rows = slice(half * HK * P, (half + 1) * HK * P)
                        sp.dma_start(raw_h[j][:], w[e, rows, :].rearrange("o (k p) n -> p (o k) n", p=P)).then_inc(h_loaded[j], 16)

            def load_y(n):
                e = bass.ds(expert(n), 1)
                for j in range(2):
                    if not isinstance(n, int) or n > 0:
                        sp.wait_ge(y_lo, 2 * (n - 1) + j + 1)
                    sp.dma_start(raw_y[j][:], w2[e, :, j * CH:(j + 1) * CH].rearrange("o (k p) n -> p (o k) n", p=P)).then_inc(y_loaded[j], 16)

            N2 = blocks_less_2(sp)
            load_h(0)
            load_y(0)
            load_h(1)
            with sp.Fori(0, N2) as n:
                load_h(n + 2)
                load_y(n + 1)
            load_y(N2 + 1)

        @block.gpsimd
        def _(pool):
            def hand_over(of, to):
                pool.tensor_tensor(to[:], of[:], nothing[:], ALU.add).then_inc(copied, 1)
                pool.wait_ge(copied, 1)
                pool.sem_clear(copied)

            def load_idx(n):
                pool.dma_start(idx[:], k.slot_rows[bass.ds(n * P, P), :]).then_inc(idx_loaded, 16)

            def load_row(n):
                pool.dma_start(row[:], k.slot_rows[bass.ds(n * P, P), :]).then_inc(row_loaded, 16)

            def gather(n):
                pool.wait_ge(idx_loaded, 16 * (n + 1))
                if not isinstance(n, int) or n > 0:
                    pool.wait_ge(gathered, 16 * n)
                hand_over(idx, idx_own)
                pool.indirect_dma_start(out=xg[:], out_offset=None, in_=k.xn[:, :],
                                        in_offset=bass.IndirectOffsetOnAxis(ap=idx_own[:, 0:1], axis=0)).then_inc(gathered, 16)

            def scatter(n):
                pool.wait_ge(row_loaded, 16 * (n + 1))
                pool.wait_ge(stored, 16 * n)
                pool.wait_ge(y_out, 2 * n + 2)
                hand_over(row, row_own)
                pool.indirect_dma_start(out=k.slot_y[:, :], out_offset=bass.IndirectOffsetOnAxis(ap=row_own[:, 1:2], axis=0),
                                        in_=y[:], in_offset=None).then_inc(stored, 16)

            N2 = blocks_less_2(pool)
            pool.memset(nothing[:], 0).then_inc(copied, 1)
            pool.wait_ge(copied, 1)
            pool.sem_clear(copied)
            load_idx(0)
            load_row(0)
            gather(0)
            load_idx(1)
            pool.wait_ge(x_turned, 1)
            gather(1)
            load_idx(2)
            with pool.Fori(1, N2 + 1) as n:
                pool.wait_ge(x_turned, n + 1)
                gather(n + 1)
                load_idx(n + 2)
                scatter(n - 1)
                load_row(n)
            pool.wait_ge(x_turned, N2 + 2)
            gather(N2 + 2)
            scatter(N2)
            load_row(N2 + 1)
            scatter(N2 + 1)
            pool.wait_ge(gathered, 16 * (N2 + 3))
            pool.wait_ge(stored, 16 * (N2 + 2))

        @block.scalar
        def _(act):
            def split_h(n, j):
                act.wait_ge(h_loaded[j], 16 * (n + 1))
                if not isinstance(n, int) or n > 0:
                    act.wait_ge(h_used, 4 * (n - 1) + j + 1)
                act.copy(hi_h[j][:], raw_h[j][:]).then_inc(h_hi, 1)

            def split_y(n, j):
                act.wait_ge(y_loaded[j], 16 * (n + 1))
                if not isinstance(n, int) or n > 0:
                    act.wait_ge(y_used, 2 * (n - 1) + j + 1)
                act.copy(hi_y[j][:], raw_y[j][:]).then_inc(y_hi, 1)

            def take_x(n):
                act.wait_ge(x_turned, n + 1)
                if not isinstance(n, int) or n > 0:
                    act.wait_ge(h_used, 4 * n)
                act.copy(xh[:].rearrange("p k n -> p (k n)"), psX).then_inc(x_hi, 1)

            def block_n(n, first, last):
                for j in range(4):
                    if not last:
                        split_h(n + 1, j)
                    if j == 1:
                        if last:
                            act.wait_ge(h_used, 4 * n + 2)
                        act.activation(act1[:], psH[0], ACT.Silu).then_inc(silu_done, 1)
                take_x(n + 1)
                for j in range(2):
                    if not first:
                        act.wait_ge(y_used, 2 * (n - 1) + j + 1)
                        act.wait_ge(stored, 16 * (n - 1))
                        act.copy(y[:, j * CH:(j + 1) * CH], psY[j]).then_inc(y_out, 1)
                    split_y(n, j)
                act.wait_ge(hid_turned, n + 1)
                act.copy(hh[:].rearrange("p k n -> p (k n)"), psHT).then_inc(hid_hi, 1)

            N2 = blocks_less_2(act)
            act.preload_act_table(ACT.Silu)
            take_x(0)
            for j in range(4):
                split_h(0, j)
            block_n(0, True, False)
            with act.Fori(1, N2 + 1) as n:
                block_n(n, False, False)
            block_n(N2 + 1, False, True)
            for j in range(2):
                act.wait_ge(y_used, 2 * (N2 + 1) + j + 1)
                act.wait_ge(stored, 16 * (N2 + 1))
                act.copy(y[:, j * CH:(j + 1) * CH], psY[j]).then_inc(y_out, 1)

        @block.vector
        def _(dve):
            def split_h(n, j):
                dve.wait_ge(h_hi, 4 * n + j + 1)
                dve.tensor_tensor(lo_h[j][:], raw_h[j][:], hi_h[j][:].bitcast(F), ALU.subtract).then_inc(h_lo, 1)

            def split_y(n, j):
                dve.wait_ge(y_hi, 2 * n + j + 1)
                dve.tensor_tensor(lo_y[j][:], raw_y[j][:], hi_y[j][:].bitcast(F), ALU.subtract).then_inc(y_lo, 1)

            def take_x(n):
                dve.wait_ge(x_hi, n + 1)
                dve.tensor_tensor(xl[:].rearrange("p k n -> p (k n)"), psX,
                                  xh[:].rearrange("p k n -> p (k n)").bitcast(F), ALU.subtract).then_inc(x_lo, 1)

            def block_n(n, last):
                for j in range(4):
                    if j == 3:
                        dve.wait_ge(silu_done, n + 1)
                        dve.wait_ge(h_used, 4 * n + 4)
                        dve.tensor_tensor(hid[:], psH[1], act1[:], ALU.mult).then_inc(hid_ready, 1)
                    if not last:
                        split_h(n + 1, j)
                take_x(n + 1)
                for j in range(2):
                    split_y(n, j)
                dve.wait_ge(hid_hi, n + 1)
                dve.tensor_tensor(hl[:].rearrange("p k n -> p (k n)"), psHT,
                                  hh[:].rearrange("p k n -> p (k n)").bitcast(F), ALU.subtract).then_inc(hid_lo, 1)

            N2 = blocks_less_2(dve)
            take_x(0)
            for j in range(4):
                split_h(0, j)
            block_n(0, False)
            with dve.Fori(1, N2 + 1) as n:
                block_n(n, False)
            block_n(N2 + 1, True)

        @block.tensor
        def _(pe):
            def turn_x(n):
                pe.wait_ge(gathered, 16 * (n + 1))
                if not isinstance(n, int) or n > 0:
                    pe.wait_ge(x_lo, n)
                for kt in range(KT):
                    last = pe.transpose(psX[:, kt * P:(kt + 1) * P], xg[:, kt * P:(kt + 1) * P], k.ident[:])
                last.then_inc(x_turned, 1)

            def up(n):
                pe.wait_ge(x_lo, n + 1)
                if not isinstance(n, int) or n > 0:
                    pe.wait_ge(hid_ready, n)
                for j in range(4):
                    pe.wait_ge(h_lo, 4 * n + j + 1)
                    for q in range(HK):
                        kt = (j % 2) * HK + q
                        pe.matmul(psH[j // 2], xh[:, kt, :], hi_h[j][:, q, :], start=(kt == 0), stop=False)
                        pe.matmul(psH[j // 2], xh[:, kt, :], lo_h[j][:, q, :], start=False, stop=False)
                        last = pe.matmul(psH[j // 2], xl[:, kt, :], hi_h[j][:, q, :], start=False, stop=(kt == KT - 1))
                    last.then_inc(h_used, 1)

            def turn_hid(n):
                pe.wait_ge(hid_ready, n + 1)
                for q in range(YK):
                    last = pe.transpose(psHT[:, q * P:(q + 1) * P], hid[:, q * P:(q + 1) * P], k.ident[:])
                last.then_inc(hid_turned, 1)

            def down(n):
                pe.wait_ge(hid_lo, n + 1)
                pe.wait_ge(y_out, 2 * n)
                for j in range(2):
                    pe.wait_ge(y_lo, 2 * n + j + 1)
                    for q in range(YK):
                        pe.matmul(psY[j], hh[:, q, :], hi_y[j][:, q, :], start=(q == 0), stop=False)
                        pe.matmul(psY[j], hh[:, q, :], lo_y[j][:, q, :], start=False, stop=False)
                        last = pe.matmul(psY[j], hl[:, q, :], hi_y[j][:, q, :], start=False, stop=(q == YK - 1))
                    last.then_inc(y_used, 1)

            N2 = blocks_less_2(pe)
            turn_x(0)
            up(0)
            turn_x(1)
            turn_hid(0)
            with pe.Fori(1, N2 + 2) as n:
                up(n)
                turn_x(n + 1)
                down(n - 1)
                turn_hid(n)
            down(N2 + 1)


def combine_phase(nc, k, src, dst):
    with ExitStack() as stack:
        s = Scope(nc, "cb", stack)
        x = [s.sb(f"x{p}", [P, DM]) for p in range(2)]
        y = [[s.sb(f"y{i}{p}", [P, DM]) for p in range(2)] for i in range(2)]
        mid = [s.sb(f"mid{p}", [P, DM]) for p in range(2)]
        out = [s.sb(f"out{p}", [P, DM]) for p in range(2)]
        x_loaded, y_loaded, stored = s.sems("x_loaded", 2), s.pool_sems("y_loaded", 2), s.sems("stored", 2)
        mid_done, out_ready = s.sem("mid_done"), s.sem("out_ready")
        block = s.block()

        @block.sync
        def _(sp):
            for t in range(NT):
                p = t % 2
                if t >= 2:
                    sp.wait_ge(out_ready, t - 1)
                sp.dma_start(x[p][:], src[t * P:(t + 1) * P, :]).then_inc(x_loaded[p], 16)

        @block.gpsimd
        def _(pool):
            for t in range(NT):
                p = t % 2
                if t >= 2:
                    pool.wait_ge(out_ready, t - 1)
                for i in range(TOP_K):
                    pool.dma_start(y[i][p][:], k.slot_y[i * SEQ + t * P:i * SEQ + (t + 1) * P, :]).then_inc(y_loaded[p], 16)

        @block.vector
        def _(dve):
            for t in range(NT):
                p = t % 2
                dve.wait_ge(x_loaded[p], 16 * (t // 2 + 1))
                dve.wait_ge(y_loaded[p], 32 * (t // 2 + 1))
                if t >= 2:
                    dve.wait_ge(out_ready, t - 1)
                dve.scalar_tensor_tensor(out=mid[p][:], in0=y[0][p][:], scalar=k.slot_w[:, 0, t:t + 1], in1=x[p][:],
                                         op0=ALU.mult, op1=ALU.add).then_inc(mid_done, 1)
                dve.wait_ge(mid_done, t + 1)
                dve.wait_ge(stored[p], 16 * (t // 2))
                dve.scalar_tensor_tensor(out=out[p][:], in0=y[1][p][:], scalar=k.slot_w[:, 1, t:t + 1], in1=mid[p][:],
                                         op0=ALU.mult, op1=ALU.add).then_inc(out_ready, 1)

        @block.scalar
        def _(act):
            for t in range(NT):
                act.wait_ge(out_ready, t + 1)
                act.dma_start(dst[t * P:(t + 1) * P, :], out[t % 2][:]).then_inc(stored[t % 2], 16)
            for p in range(2):
                act.wait_ge(stored[p], 16 * NT // 2)


HA, DQK, DV = 4, 64, 128
LAM_INIT = 0.8 - 0.6


def diff_attention_phase(nc, k, proj, dst, lams, g_sub, rpb):
    TILES = HA * NT
    with ExitStack() as stack:
        s = Scope(nc, "da", stack)
        qk_raw = [s.sb(f"raw{i}", [P, NT, DV]) for i in range(2)]
        v = s.sb("v", [P, NT, DV])
        qT, kT = s.sb("qT", [P, SEQ]), s.sb("kT", [P, SEQ])
        e = [s.sb(f"e{c}", [P, SEQ]) for c in range(2)]
        w = s.sb("w", [P, SEQ])
        wT = s.sb("wT", [P, SEQ])
        o_all = s.sb("o_all", [P, NT, HA * DV])
        junk = s.sb("junk", [P, DV])
        neg_max = [s.sb(f"neg_max{c}", [P, 1]) for c in range(2)]
        total = [s.sb(f"total{c}", [P, 1]) for c in range(2)]
        inv = [s.sb(f"inv{c}", [P, 1]) for c in range(2)]
        coef = s.sb("coef", [P, 1])
        sq, ms, sd, rs = (s.sb(n, [P, TILES]) for n in ("sq", "ms", "sd", "rs"))
        lam_b = [s.sb(f"lam{i}", [P, DQK]) for i in range(4)]
        dots, edots, neg_lam = s.sb("dots", [P, 2]), s.sb("edots", [P, 2]), s.sb("neg_lam", [P, 1])
        prod = [s.sb(f"prod{i}", [P, DQK]) for i in range(2)]
        gs = s.sb("gs", [P, DV])
        psS = [k.ps[:, 2 * c:2 * c + 2, :].rearrange("p b n -> p (b n)") for c in range(2)]
        psT = [k.ps[:, 4 + i, :] for i in range(2)]
        psO = k.ps[:, 6, 0:DV]

        consts_loaded, loaded = s.sem("consts_loaded"), s.sems("loaded", 3)
        turned, taken = s.sem("turned"), s.sem("taken")
        scored, maxed, exped, inverted = (s.sems(n, 2) for n in ("scored", "maxed", "exped", "inverted"))
        coef_done, w_ready, w_turned, wT_ready, pv_done, o_out, sq_done = (s.sem(n) for n in (
            "coef_done", "w_ready", "w_turned", "wT_ready", "pv_done", "o_out", "sq_done"))
        did, dots_done, edots_done, ms_done, sd_done, final, stored = (s.sem(n) for n in (
            "did", "dots_done", "edots_done", "ms_done", "sd_done", "final", "stored"))
        cleared, bias_laid, squared = s.sem("cleared"), s.pool_sem("bias_laid"), s.sem("squared")
        bias = s.sb("bias", [P, PAIRS, OFFS, GRID])
        rpb_sb = s.sb("rpb", [HB, OFFS * (2 * WIN_C - 1)])
        block = s.block()

        @block.sync
        def _(sp):
            for to, row in list(zip(lam_b, lams)):
                sp.dma_start(to[:], row_to_all(row, DQK)).then_inc(consts_loaded, 16)
            sp.dma_start(gs[:], row_to_all(g_sub, DV)).then_inc(consts_loaded, 16)

            def load(first):
                for i, to in enumerate((qk_raw[0], qk_raw[1], v)):
                    sp.dma_start(to[:], proj[:, bass.ds(first[i], DV)].rearrange("(t p) d -> p t d", p=P)).then_inc(loaded[i], 16)

            load([i * HA * DV for i in range(3)])
            with sp.Fori(1, HA) as h:
                first = [sp.snap(i * HA * DV + h * DV) for i in range(3)]
                sp.wait_ge(pv_done, NT * h)
                load(first)
            for t in range(NT):
                sp.wait_ge(final, HA * (t + 1))
                sp.dma_start(dst[t * P:(t + 1) * P, 0:HA * DV], o_all[:, t, :]).then_inc(stored, 16)
            sp.wait_ge(stored, 16 * NT)

        @block.gpsimd
        def _(pool):
            lay_bias(pool, k, bias, rpb_sb, rpb, cleared, bias_laid)

        @block.tensor
        def _(pe):
            def score(i, t):
                for c in range(2):
                    half = slice(c * DQK, (c + 1) * DQK)
                    if not isinstance(i, int) or i > 0:
                        pe.wait_ge(exped[c], i)
                    for n in range(2):
                        last = pe.matmul(psS[c][:, n * CH:(n + 1) * CH], qT[half, t * P:(t + 1) * P],
                                         kT[half, n * CH:(n + 1) * CH], start=True, stop=True)
                    last.then_inc(scored[c], 1)

            with pe.Fori(0, HA) as h:
                for i in range(2):
                    pe.wait_ge(loaded[i], 16 * (h + 1))
                    for b in range(2):
                        pe.wait_ge(wT_ready, 2 * NT * h)
                        pe.wait_ge(taken, 4 * h + 2 * i)
                        for q in range(4):
                            last = pe.transpose(psT[b][:, q * P:(q + 1) * P], qk_raw[i][:, 4 * b + q, :], k.ident[:])
                        last.then_inc(turned, 1)
                pe.wait_ge(taken, 4 * h + 4)
                pe.wait_ge(loaded[2], 16 * (h + 1))
                score(NT * h, 0)
                for t in range(NT):
                    i = NT * h + t
                    if t + 1 < NT:
                        score(i + 1, t + 1)
                    pe.wait_ge(w_ready, i + 1)
                    for b in range(2):
                        for q in range(4):
                            kt = 4 * b + q
                            last = pe.transpose(psT[b][:, q * P:(q + 1) * P], w[:, kt * P:(kt + 1) * P], k.ident[:])
                        last.then_inc(w_turned, 1)
                    pe.wait_ge(o_out, i)
                    for b in range(2):
                        pe.wait_ge(wT_ready, 2 * i + b + 1)
                        for q in range(4):
                            kt = 4 * b + q
                            last = pe.matmul(psO, wT[:, kt * P:(kt + 1) * P], v[:, kt, :], start=(kt == 0), stop=(kt == NT - 1))
                    last.then_inc(pv_done, 1)

        @block.scalar
        def _(act):
            def exps(i, c):
                act.wait_ge(maxed[c], i + 1)
                if not isinstance(i, int) or i > 0:
                    act.wait_ge(w_ready, i)
                act.activation(e[c][:], psS[c], ACT.Exp, bias=neg_max[c][:], accum_out=total[c][:]).then_inc(exped[c], 1)

            def take_turned(i):
                for b in range(2):
                    act.wait_ge(w_turned, 2 * i + b + 1)
                    if b == 0 and (not isinstance(i, int) or i > 0):
                        act.wait_ge(pv_done, i)
                    act.copy(wT[:, b * CH:(b + 1) * CH], psT[b]).then_inc(wT_ready, 1)

            def take_rows(i, h, t):
                act.wait_ge(pv_done, i + 1)
                act.wait_ge(inverted[0], i + 1)
                act.activation(o_all[:, bass.ds(t, 1), bass.ds(h * DV, DV)], psO, ACT.Copy, scale=inv[0][:]).then_inc(o_out, 1)

            act.preload_act_table(ACT.Exp)
            act.wait_ge(dots_done, 2)
            act.activation(edots[:], dots[:], ACT.Exp).then_inc(edots_done, 1)
            with act.Fori(0, HA) as h:
                for g in range(4):
                    act.wait_ge(turned, 4 * h + g + 1)
                    to = (qT, kT)[g // 2][:, (g % 2) * CH:(g % 2 + 1) * CH]
                    act.activation(to, psT[g % 2], ACT.Copy, scale=DQK ** -0.5 if g < 2 else 1.0).then_inc(taken, 1)
                i0 = act.snap(NT * h)
                for c in range(2):
                    exps(i0, c)
                with act.Fori(0, NT - 1) as t:
                    i = i0 + t
                    exps(i + 1, 0)
                    take_turned(i)
                    exps(i + 1, 1)
                    take_rows(i, h, t)
                take_turned(i0 + NT - 1)
                take_rows(i0 + NT - 1, h, NT - 1)
            act.preload_act_table(ACT.Sqrt)
            act.wait_ge(ms_done, 1)
            act.activation(sd[:], ms[:], ACT.Sqrt).then_inc(sd_done, 1)

        @block.vector
        def _(dve):
            n = [0]

            def link(ins):
                n[0] += 1
                ins.then_inc(did, 1)
                dve.wait_ge(did, n[0])

            dve.wait_ge(consts_loaded, 16 * 5)
            for i in range(2):
                link(dve.tensor_tensor(prod[i][:], lam_b[2 * i][:], lam_b[2 * i + 1][:], ALU.mult))
                dve.tensor_reduce(dots[:, i:i + 1], prod[i][:], X, ALU.add).then_inc(dots_done, 1)
            link(dve.tensor_scalar(gs[:], gs[:], 1.0 - LAM_INIT, None, ALU.mult))
            dve.wait_ge(edots_done, 1)
            link(dve.tensor_tensor(neg_lam[:], edots[:, 1:2], edots[:, 0:1], ALU.subtract))
            link(dve.tensor_scalar(neg_lam[:], neg_lam[:], -LAM_INIT, None, ALU.add))

            def maxima(i):
                for c in range(2):
                    dve.wait_ge(scored[c], i + 1)
                    if not isinstance(i, int) or i > 0:
                        dve.wait_ge(exped[c], i)
                    dve.tensor_reduce(neg_max[c][:], psS[c], X, ALU.max, negate=True).then_inc(maxed[c], 1)

            def combine(i):
                dve.wait_ge(exped[1], i + 1)
                dve.wait_ge(exped[0], i + 1)
                if not isinstance(i, int) or i > 0:
                    dve.wait_ge(w_turned, 2 * i)
                dve.reciprocal(inv[1][:], total[1][:]).then_inc(inverted[1], 1)
                dve.wait_ge(inverted[1], i + 1)
                dve.scalar_tensor_tensor(out=coef[:], in0=inv[1][:], scalar=total[0][:], in1=neg_lam[:],
                                         op0=ALU.mult, op1=ALU.mult).then_inc(coef_done, 1)
                dve.wait_ge(coef_done, i + 1)
                dve.scalar_tensor_tensor(out=w[:], in0=e[1][:], scalar=coef[:], in1=e[0][:],
                                         op0=ALU.mult, op1=ALU.add).then_inc(w_ready, 1)

            def invert(i):
                if not isinstance(i, int) or i > 0:
                    dve.wait_ge(o_out, i)
                dve.reciprocal(inv[0][:], total[0][:]).then_inc(inverted[0], 1)

            def squares(i, h, t):
                dve.wait_ge(o_out, i + 1)
                if not isinstance(i, int) or i > 0:
                    dve.wait_ge(sq_done, i)
                o = o_all[:, bass.ds(t, 1), bass.ds(h * DV, DV)].rearrange("p o d -> p (o d)")
                dve.tensor_tensor(junk[:], o, o, ALU.mult).then_inc(squared, 1)
                dve.wait_ge(squared, i + 1)
                dve.tensor_reduce(sq[:, bass.ds(i, 1)], junk[:], X, ALU.add).then_inc(sq_done, 1)

            with dve.Fori(0, HA) as h:
                i0 = dve.snap(NT * h)
                maxima(i0)
                combine(i0)
                invert(i0)
                with dve.Fori(0, NT - 1) as t:
                    i = i0 + t
                    maxima(i + 1)
                    combine(i + 1)
                    squares(i, h, t)
                    invert(i + 1)
                squares(i0 + NT - 1, h, NT - 1)
            dve.wait_ge(sq_done, TILES)
            dve.tensor_scalar(ms[:], sq[:], 1.0 / DV, EPS, ALU.mult, ALU.add).then_inc(ms_done, 1)
            dve.wait_ge(sd_done, 1)
            link(dve.reciprocal(rs[:], sd[:]))
            for t in range(NT):
                for h in range(HA):
                    o = o_all[:, t, h * DV:(h + 1) * DV]
                    i = NT * h + t
                    dve.scalar_tensor_tensor(out=o, in0=o, scalar=rs[:, i:i + 1], in1=gs[:],
                                             op0=ALU.mult, op1=ALU.mult).then_inc(final, 1)


HB, DB_H, GRID, ROWS, WIN_R, WIN_C = 16, 32, 64, 16, 8, 16
OFFS = 2 * WIN_R - 1
PAIRS = HB // 2
QUADS = HB // 4


def lay_bias(pool, k, bias, rpb_sb, rpb, cleared, laid):
    pool.memset(bias[:], BIG).then_inc(cleared, 1)
    pool.dma_start(rpb_sb[:], rpb.rearrange("h r w -> h (r w)")).then_inc(laid, 16)
    pool.wait_ge(laid, 16)
    pool.tensor_scalar(rpb_sb[:], rpb_sb[:], -1.0, None, ALU.mult).then_inc(cleared, 1)
    pool.wait_ge(cleared, 2)
    pool.dma_start(k.neg_rpb.rearrange("h r w -> h (r w)"), rpb_sb[:]).then_inc(laid, 16)
    pool.wait_ge(laid, 32)
    pool.dma_start(k.bias_rows, bias[:]).then_inc(laid, 16)
    pool.wait_ge(laid, 48)
    src = k.neg_rpb.rearrange("(p h) r w -> h p r w", h=2)

    def one(c, first, off):
        for h in range(2):
            pool.dma_start(k.bias_rows[bass.ds(c + h * GRID, 1), :, :, bass.ds(first, WIN_C)],
                           src[h:h + 1, :, :, bass.ds(off, WIN_C)]).then_inc(laid, 16)

    half = WIN_C // 2
    last = GRID - WIN_C
    with pool.Fori(0, half) as c:
        one(c, 0, WIN_C - 1 - c)
    with pool.Fori(half, last + half) as c:
        one(c, c - half, half - 1)
    with pool.Fori(last + half, GRID) as c:
        one(c, last, last - c + WIN_C - 1)
    pool.wait_ge(laid, 16 * (2 * GRID + 3))


def neighbourhood_phase(nc, k, proj, dst, consts):
    Q0, K0, V0, O0 = 3 * 512, 4 * 512, 5 * 512, 512
    QC = 4 * DB_H
    with ExitStack() as stack:
        s = Scope(nc, "na", stack)
        bias = s.sb("bias", [P, 2, OFFS, GRID])
        raw = [s.sb(f"raw{i}", [P, NT, QC]) for i in range(2)]
        v_even = s.sb("v_even", [P, NT, QC])
        v_odd = s.sb("v_odd", [P, NT - 1, QC])
        qd = s.sb("qd", [P, ROWS, 4, GRID])
        kT = s.sb("kT", [P, SEQ])
        sc = [[s.sb(f"sc{a}{b}", [P, CH]) for b in range(2)] for a in range(2)]
        e = [[s.sb(f"e{a}{b}", [P, CH]) for b in range(2)] for a in range(2)]
        eT = [s.sb(f"eT{b}", [P, CH]) for b in range(2)]
        neg_max = [[s.sb(f"neg_max{a}{b}", [P, 1]) for b in range(2)] for a in range(2)]
        total = [s.sb(f"total{a}", [P, 2]) for a in range(2)]
        inv = [s.sb(f"inv{a}", [P, 2]) for a in range(2)]
        o1 = [s.sb(f"o1{a}", [P, QC]) for a in range(2)]
        o2 = [s.sb(f"o2{a}", [P, QC]) for a in range(2)]
        own = s.sb("own", [P, QC])
        fold = s.sb("fold", [P, GRID])
        rows = s.sb("rows", [P, NT, QC])
        spare = s.sb("spare", [P, 3])
        psS = [[k.ps[:, 2 * a + b, :] for b in range(2)] for a in range(2)]
        psT = [k.ps[:, 4 + b, :] for b in range(2)]
        psO = [k.ps[:, 6, a * QC:(a + 1) * QC] for a in range(2)]
        psR = k.ps[:, 7, 0:QC]

        consts_loaded, loaded, stored = s.sem("consts_loaded"), s.sems("loaded", 4), s.sem("stored")
        spared = s.sem("spared")
        cleared, turned, taken, bias_loaded = (s.sem(n) for n in ("cleared", "turned", "taken", "bias_loaded"))
        scored, biased, exped, e_turned, eT_ready = (s.sem(n) for n in ("scored", "biased", "exped", "e_turned", "eT_ready"))
        multiplied, inverted, scaled, masked, folded, row_out = (s.sem(n) for n in (
            "multiplied", "inverted", "scaled", "masked", "folded", "row_out"))
        block = s.block()

        def first_row(r):
            return min(max(r - WIN_R // 2, 0), ROWS - WIN_R)

        @block.sync
        def _(sp):
            sp.dma_start(own[:], consts[:, 0:QC]).then_inc(consts_loaded, 16)
            sp.dma_start(fold[:], consts[:, QC:QC + GRID]).then_inc(consts_loaded, 16)

            def load(first, pair):
                sp.dma_start(bias[:], k.bias_rows[:, bass.ds(pair, 2), :, :]).then_inc(bias_loaded, 16)
                for i, to in enumerate((raw[0], raw[1], v_even)):
                    sp.dma_start(to[:], proj[:, bass.ds(first[i], QC)].rearrange("(t p) d -> p t d", p=P)).then_inc(loaded[i], 16)
                sp.dma_start(v_odd[:], proj[GRID:SEQ - GRID, bass.ds(first[2], QC)].rearrange("(t p) d -> p t d", p=P)
                             ).then_inc(loaded[3], 16)

            def store(col):
                sp.dma_start(dst[:, bass.ds(col, QC)].rearrange("(t p) d -> p t d", p=P), rows[:]).then_inc(stored, 16)

            load([Q0, K0, V0], 0)
            with sp.Fori(1, QUADS) as q:
                first = [sp.snap(c0 + q * QC) for c0 in (Q0, K0, V0)]
                pair, col = sp.snap(2 * q), sp.snap(O0 + q * QC - QC)
                sp.wait_ge(row_out, ROWS * q)
                load(first, pair)
                store(col)
            sp.wait_ge(row_out, ROWS * QUADS)
            store(O0 + (QUADS - 1) * QC)
            sp.wait_ge(stored, 16 * QUADS)

        @block.gpsimd
        def _(pool):
            pool.memset(qd[:], 0.0).then_inc(cleared, 1)

        @block.tensor
        def _(pe):
            def score(g, r):
                a = r % 2
                if r >= 2:
                    pe.wait_ge(biased, 2 * (g - 1))
                else:
                    pe.wait_ge(biased, 2 * (g - r))
                for b in range(2):
                    last = pe.matmul(psS[a][b], qd[:, r, 2 * b:2 * b + 2, :].rearrange("p h c -> p (h c)"),
                                     kT[:, first_row(r) * GRID:first_row(r) * GRID + CH], start=True, stop=True)
                last.then_inc(scored, 1)

            pe.wait_ge(consts_loaded, 32)
            with pe.Fori(0, QUADS) as q:
                for i in range(2):
                    pe.wait_ge(loaded[i], 16 * (q + 1))
                    for b in range(2):
                        pe.wait_ge(eT_ready, 2 * ROWS * q)
                        pe.wait_ge(taken, 4 * q + 2 * i)
                        for n in range(4):
                            last = pe.transpose(psT[b][:, n * P:(n + 1) * P], raw[i][:, 4 * b + n, :], k.ident[:])
                        last.then_inc(turned, 1)
                pe.wait_ge(taken, 4 * q + 4)
                pe.wait_ge(loaded[2], 16 * (q + 1))
                pe.wait_ge(loaded[3], 16 * (q + 1))
                g0 = pe.snap(ROWS * q)
                score(g0, 0)
                score(g0 + 1, 1)
                for r in range(ROWS):
                    g, a = g0 + r, r % 2
                    for b in range(2):
                        pe.wait_ge(exped, 2 * g + b + 1)
                        for n in range(4):
                            last = pe.transpose(psT[b][:, n * P:(n + 1) * P], e[a][b][:, n * P:(n + 1) * P], k.ident[:])
                        last.then_inc(e_turned, 1)
                    if r + 2 < ROWS:
                        score(g + 2, r + 2)
                    if r >= 1:
                        pe.wait_ge(masked, g)
                        pe.wait_ge(row_out, g - 1)
                        half = slice(((r - 1) % 2) * GRID, ((r - 1) % 2 + 1) * GRID)
                        pe.matmul(psR[half, :], fold[:], o2[1 - a][:], start=True, stop=True).then_inc(folded, 1)
                    for b in range(2):
                        pe.wait_ge(eT_ready, 2 * g + b + 1)
                        for n in range(4):
                            row = first_row(r) + 2 * n
                            vv = (v_even if row % 2 == 0 else v_odd)[:, row // 2, b * 2 * DB_H:(b + 1) * 2 * DB_H]
                            last = pe.matmul(psO[a][:, b * 2 * DB_H:(b + 1) * 2 * DB_H], eT[b][:, n * P:(n + 1) * P], vv,
                                             start=(n == 0), stop=(n == 3))
                    last.then_inc(multiplied, 1)
                pe.wait_ge(masked, g0 + ROWS)
                pe.wait_ge(row_out, g0 + ROWS - 1)
                pe.matmul(psR[GRID:2 * GRID, :], fold[:], o2[1][:], start=True, stop=True).then_inc(folded, 1)

        @block.scalar
        def _(act):
            act.preload_act_table(ACT.Exp)
            with act.Fori(0, QUADS) as q:
                g0 = act.snap(ROWS * q)
                for b in range(2):
                    act.wait_ge(turned, 4 * q + b + 1)
                    if b == 0:
                        act.wait_ge(cleared, 1)
                    for h in range(4):
                        part = slice(h * DB_H, (h + 1) * DB_H)
                        last = act.activation(qd[part, 8 * b:8 * b + 8, h, :], psT[b][part, :].rearrange("p (r c) -> p r c", c=GRID),
                                              ACT.Copy, scale=-(DB_H ** -0.5))
                    last.then_inc(taken, 1)
                for b in range(2):
                    act.wait_ge(turned, 4 * q + b + 3)
                    act.copy(kT[:, b * CH:(b + 1) * CH], psT[b]).then_inc(taken, 1)

                def exps(g, a, before):
                    act.wait_ge(inverted, before)
                    for b in range(2):
                        act.wait_ge(biased, 2 * g + b + 1)
                        act.activation(e[a][b][:], sc[a][b][:], ACT.Exp, scale=-1.0, bias=neg_max[a][b][:],
                                       accum_out=total[a][:, b:b + 1]).then_inc(exped, 1)

                def take(g):
                    act.wait_ge(e_turned, 2 * g + 1)
                    act.wait_ge(multiplied, g)
                    act.copy(eT[0][:], psT[0]).then_inc(eT_ready, 1)

                exps(g0, 0, g0)
                with act.Fori(0, ROWS // 2 - 1) as j:
                    for a in range(2):
                        g = g0 + 2 * j + a
                        take(g)
                        exps(g + 1, 1 - a, g)
                take(g0 + ROWS - 2)
                exps(g0 + ROWS - 1, 1, g0 + ROWS - 2)
                take(g0 + ROWS - 1)

        @block.vector
        def _(dve):
            def add_bias(g, a, off):
                for b in range(2):
                    nb = bias[:, b, off:off + WIN_R, :].rearrange("p r c -> p (r c)")
                    dve.tensor_tensor_reduce(sc[a][b][:], psS[a][b], nb, 1.0, BIG, ALU.add, ALU.min,
                                             neg_max[a][b][:]).then_inc(biased, 1)

            def take(g):
                dve.wait_ge(e_turned, 2 * g + 2)
                dve.wait_ge(eT_ready, 2 * g + 1)
                dve.tensor_copy(eT[1][:], psT[1]).then_inc(eT_ready, 1)

            def rows_of(g, a):
                dve.wait_ge(exped, 2 * g + 2)
                dve.reciprocal(inv[a][:], total[a][:]).then_inc(inverted, 1)
                dve.wait_ge(inverted, g + 1)
                dve.wait_ge(multiplied, g + 1)
                dve.tensor_tensor(o1[a][:].rearrange("p (b c) -> p b c", b=2), psO[a].rearrange("p (b c) -> p b c", b=2),
                                  inv[a][:].rearrange("p (b o) -> p b o", o=1).to_broadcast([P, 2, 2 * DB_H]),
                                  ALU.mult).then_inc(scaled, 1)
                dve.wait_ge(scaled, g + 1)
                dve.tensor_tensor(o2[a][:], o1[a][:], own[:], ALU.mult).then_inc(masked, 1)

            def clear_spare(col):
                dve.memset(spare[:, col:col + 1], 0.0).then_inc(spared, 1)

            def out_of(g, t, a):
                dve.wait_ge(folded, g + 1)
                half = slice(a * GRID, (a + 1) * GRID)
                dve.tensor_copy(rows[half, t, :], psR[half, :]).then_inc(row_out, 1)

            dve.wait_ge(consts_loaded, 32)
            with dve.Fori(0, QUADS) as q:
                g0 = dve.snap(ROWS * q)
                dve.wait_ge(bias_loaded, 16 * (q + 1))

                def off(r):
                    return first_row(r) - r + WIN_R - 1

                dve.wait_ge(spared, 3 * q)
                dve.wait_ge(scored, g0 + 1)
                clear_spare(0)
                add_bias(g0, 0, off(0))
                dve.wait_ge(scored, g0 + 2)
                clear_spare(1)
                add_bias(g0 + 1, 1, off(1))
                dve.wait_ge(stored, 16 * q)
                for r in range(ROWS):
                    g, a = g0 + r, r % 2
                    take(g)
                    if r + 2 < ROWS:
                        dve.wait_ge(scored, g + 3)
                    if r >= 1:
                        out_of(g - 1, (r - 1) // 2, 1 - a)
                    else:
                        clear_spare(2)
                    if r + 2 < ROWS:
                        add_bias(g + 2, a, off(r + 2))
                    rows_of(g, a)
                out_of(g0 + ROWS - 1, NT - 1, 1)


D_PLE = 256


def ple_phase(nc, k, src, w, gain, dst):
    KP = D_PLE // P
    with ExitStack() as stack:
        s = Scope(nc, "ple", stack)
        x = [s.sb(f"x{p}", [P, D_PLE]) for p in range(2)]
        xT = [s.sb(f"xT{p}", [P, D_PLE]) for p in range(2)]
        w_sb = s.sb("w", [P, KP, DM])
        gain_b = s.sb("gain", [P, DM])
        out = [s.sb(f"out{p}", [P, DM]) for p in range(2)]
        junk = s.sb("junk", [P, DM], BF)
        ss, ms, sd, rs = (s.sb(n, [P, NT]) for n in ("ss", "ms", "sd", "rs"))
        psT = [k.ps[:, p, 0:D_PLE] for p in range(2)]
        psY = [k.ps[:, 2 + 2 * p:4 + 2 * p, :].rearrange("p b n -> p (b n)") for p in range(2)]
        x_loaded, stored, consts_loaded = s.sems("x_loaded", 2), s.sems("stored", 2), s.sem("consts_loaded")
        turned, taken, product, squared, meaned, rooted, inverted, ready = (s.sem(n) for n in (
            "turned", "taken", "product", "squared", "meaned", "rooted", "inverted", "ready"))
        block = s.block()

        @block.sync
        def _(sp):
            for p in range(2):
                sp.dma_start(x[p][:], src[p * P:(p + 1) * P, :]).then_inc(x_loaded[p], 16)
            sp.dma_start(w_sb[:], w.rearrange("(k p) n -> p k n", p=P)).then_inc(consts_loaded, 16)
            sp.dma_start(gain_b[:], row_to_all(gain, DM)).then_inc(consts_loaded, 16)

            def store(t, p):
                sp.wait_ge(ready, t + 1)
                sp.dma_start(dst[bass.ds(t * P, P), :], out[p][:]).then_inc(stored[p], 16)

            with sp.Fori(0, NT // 2 - 1) as j:
                for p in range(2):
                    store(2 * j + p, p)
                    sp.dma_start(x[p][:], src[bass.ds((2 * j + p + 2) * P, P), :]).then_inc(x_loaded[p], 16)
            for p in range(2):
                store(NT - 2 + p, p)
            for p in range(2):
                sp.wait_ge(stored[p], 16 * NT // 2)

        @block.tensor
        def _(pe):
            pe.wait_ge(consts_loaded, 32)
            with pe.Fori(0, NT // 2) as j:
                for p in range(2):
                    t = 2 * j + p
                    pe.wait_ge(x_loaded[p], 16 * (j + 1))
                    for kt in range(KP):
                        last = pe.transpose(psT[p][:, kt * P:(kt + 1) * P], x[p][:, kt * P:(kt + 1) * P], k.ident[:])
                    last.then_inc(turned, 1)
                for p in range(2):
                    t = 2 * j + p
                    pe.wait_ge(taken, t + 1)
                    pe.wait_ge(ready, 2 * j)
                    for half in range(2):
                        for kt in range(KP):
                            last = pe.matmul(psY[p][:, half * CH:(half + 1) * CH], xT[p][:, kt * P:(kt + 1) * P],
                                             w_sb[:, kt, half * CH:(half + 1) * CH], start=(kt == 0), stop=(kt == KP - 1))
                    last.then_inc(product, 1)

        @block.scalar
        def _(act):
            act.preload_act_table(ACT.Sqrt)
            with act.Fori(0, NT // 2) as j:
                for p in range(2):
                    act.wait_ge(turned, 2 * j + p + 1)
                    act.copy(xT[p][:], psT[p]).then_inc(taken, 1)
                for p in range(2):
                    t = 2 * j + p
                    act.wait_ge(product, t + 1)
                    act.activation(junk[:], psY[p], ACT.Square, accum_out=ss[:, bass.ds(t, 1)]).then_inc(squared, 1)
                    act.wait_ge(meaned, t + 1)
                    act.activation(sd[:, bass.ds(t, 1)], ms[:, bass.ds(t, 1)], ACT.Sqrt).then_inc(rooted, 1)

        @block.vector
        def _(dve):
            dve.wait_ge(consts_loaded, 32)
            with dve.Fori(0, NT // 2) as j:
                for p in range(2):
                    t = 2 * j + p
                    one = bass.ds(t, 1)
                    dve.wait_ge(squared, t + 1)
                    dve.tensor_scalar(ms[:, one], ss[:, one], 1.0 / DM, EPS, ALU.mult, ALU.add).then_inc(meaned, 1)
                    dve.wait_ge(rooted, t + 1)
                    dve.reciprocal(rs[:, one], sd[:, one]).then_inc(inverted, 1)
                    dve.wait_ge(inverted, t + 1)
                    dve.wait_ge(stored[p], 16 * j)
                    dve.scalar_tensor_tensor(out=out[p][:], in0=psY[p], scalar=rs[:, one], in1=gain_b[:],
                                             op0=ALU.mult, op1=ALU.mult).then_inc(ready, 1)


LAYERS = 2


def ada_phase(nc, k, c, w, b, norm_g, mod):
    N = 3 * DM
    NB = N // CH
    with ExitStack() as stack:
        s = Scope(nc, "ada", stack)
        wb = [s.sb(f"w{i}", [P, N]) for i in range(4)]
        c_raw, c_act = s.sb("c_raw", [P, KT]), s.sb("c_act", [P, KT])
        bias = s.sb("bias", [1, LAYERS, N])
        g = s.sb("g", [1, LAYERS, DM])
        row = s.sb("row", [1, LAYERS, N])
        gained = s.sb("gained", [1, LAYERS, DM])
        ps = k.ps[0:1, 0:NB, :].rearrange("p b n -> p (b n)")
        loaded, consts_loaded, c_loaded, c_done = s.sems("loaded", 4), s.sem("consts_loaded"), s.sem("c_loaded"), s.sem("c_done")
        used, rows_done, gain_done, stored = (s.sem(n) for n in ("used", "rows_done", "gain_done", "stored"))
        block = s.block()

        @block.sync
        def _(sp):
            sp.dma_start(c_raw[:], c.rearrange("(k p) -> p k", p=P), allow_slow_non_contiguous=True).then_inc(c_loaded, 16)

            def load(i, l, kt):
                sp.dma_start(wb[i][:], w[bass.ds(l * DM + kt * P, P), :]).then_inc(loaded[i], 16)

            for i in range(4):
                load(i, 0, i)
            sp.dma_start(bias[:], b.rearrange("(o l) n -> o l n", o=1)).then_inc(consts_loaded, 16)
            sp.dma_start(g[:], norm_g.rearrange("(o l) n -> o l n", o=1)).then_inc(consts_loaded, 16)
            with sp.Fori(1, LAYERS * KT // 4) as j:
                for i in range(4):
                    sp.wait_ge(used, 4 * j + i - 3)
                    load(i, 0, 4 * j + i)
            for l in range(LAYERS):
                sp.wait_ge(gain_done, l + 1)
                sp.wait_ge(rows_done, l + 1)
                sp.dma_start(mod[l, 0:1, :], row[:, l, 0:DM]).then_inc(stored, 16)
                sp.dma_start(mod[l, 1:2, :], gained[:, l, :]).then_inc(stored, 16)
                sp.dma_start(mod[l, 2:3, :], row[:, l, 2 * DM:]).then_inc(stored, 16)
            sp.wait_ge(stored, 16 * 3 * LAYERS)

        @block.scalar
        def _(act):
            act.preload_act_table(ACT.Silu)
            act.wait_ge(c_loaded, 16)
            act.activation(c_act[:], c_raw[:], ACT.Silu).then_inc(c_done, 1)

        @block.tensor
        def _(pe):
            pe.wait_ge(c_done, 1)
            with pe.Fori(0, LAYERS) as l:
                for kt in range(KT):
                    pe.wait_ge(loaded[kt % 4], 16 * (2 * l + kt // 4 + 1))
                    if kt == 0:
                        pe.wait_ge(rows_done, l)
                    for n in range(NB):
                        last = pe.matmul(ps[:, n * CH:(n + 1) * CH], c_act[:, kt:kt + 1], wb[kt % 4][:, n * CH:(n + 1) * CH],
                                         start=(kt == 0), stop=(kt == KT - 1))
                    last.then_inc(used, 1)

        @block.vector
        def _(dve):
            dve.wait_ge(consts_loaded, 32)
            with dve.Fori(0, LAYERS) as l:
                one = bass.ds(l, 1)
                dve.wait_ge(used, KT * (l + 1))
                dve.tensor_tensor(row[:, one, :].rearrange("p o n -> p (o n)"), ps,
                                  bias[:, one, :].rearrange("p o n -> p (o n)"), ALU.add).then_inc(rows_done, 1)
                dve.wait_ge(rows_done, l + 1)
                dve.scalar_tensor_tensor(out=gained[:, one, :], in0=row[:, one, DM:2 * DM], scalar=1.0, in1=g[:, one, :],
                                         op0=ALU.add, op1=ALU.mult).then_inc(gain_done, 1)


HR, DR = 4, 128


def retention_phase(nc, k, tag, proj, dst, decay, q_decay, k_decay, tile_decay):
    RET = HR * DR
    with ExitStack() as stack:
        s = Scope(nc, tag, stack)
        raw = [s.sb(f"raw{i}", [P, NT, DR]) for i in range(2)]
        v, g = s.sb("v", [P, NT, RET]), s.sb("g", [P, NT, RET])
        qT, kT, qTd = (s.sb(n, [P, SEQ]) for n in ("qT", "kT", "qTd"))
        kd = s.sb("kd", [P, NT, DR])
        sm = s.sb("sm", [P, SEQ])
        state = s.sb("state", [P, NT, DR])
        cen, sq, nrm = (s.sb(n, [P, NT, DR]) for n in ("cen", "sq", "nrm"))
        sums, mu, var_sum, ms, sd, rs = (s.sb(n, [P, NT]) for n in ("sums", "mu", "var_sum", "ms", "sd", "rs"))
        y = s.sb("y", [P, NT, RET])
        dec = s.sb("dec", [P, HR, P])
        q_dec = s.sb("q_dec", [P, HR, P])
        k_dec, t_dec = s.sb("k_dec", [P, HR]), s.sb("t_dec", [P, HR])
        psT = [k.ps[:, i, :] for i in range(2)]
        two = [k.ps[:, b:b + 2, :].rearrange("p b n -> p (b n)") for b in (2, 4, 6)]
        psS, psKV, psO = two
        loaded, g_loaded, consts_loaded, stored = s.sems("loaded", 3), s.sem("g_loaded"), s.sem("consts_loaded"), s.sem("stored")
        turned, taken, kd_done, scored, kv_done, qd_done, sm_done, state_done, product = (s.sem(n) for n in (
            "turned", "taken", "kd_done", "scored", "kv_done", "qd_done", "sm_done", "state_done", "product"))
        did, meaned, rooted, y_done = (s.sem(n) for n in ("did", "meaned", "rooted", "y_done"))
        block = s.block()
        LINKS = 7

        def part(ap):
            return ap.rearrange("(t p) d -> p t d", p=P)

        @block.sync
        def _(sp):
            for i in range(2):
                sp.dma_start(raw[i][:], part(proj[:, i * RET:i * RET + DR])).then_inc(loaded[i], 16)
            sp.dma_start(dec[:], decay).then_inc(consts_loaded, 16)
            sp.dma_start(k_dec[:], k_decay).then_inc(consts_loaded, 16)
            sp.dma_start(t_dec[:], tile_decay).then_inc(consts_loaded, 16)
            sp.dma_start(q_dec[:].rearrange("p h n -> p (h n)"), row_to_all(q_decay, HR * P)).then_inc(consts_loaded, 16)
            sp.dma_start(v[:], part(proj[:, 2 * RET:3 * RET])).then_inc(loaded[2], 16)
            sp.dma_start(g[:], part(proj[:, 3 * RET:4 * RET])).then_inc(g_loaded, 16)
            with sp.Fori(1, HR) as h:
                first = [sp.snap(h * DR + i * RET) for i in range(2)]
                sp.wait_ge(kd_done, h)
                for i in range(2):
                    sp.dma_start(raw[i][:], part(proj[:, bass.ds(first[i], DR)])).then_inc(loaded[i], 16)
            sp.wait_ge(y_done, HR)
            sp.dma_start(part(dst[:, 0:RET]), y[:]).then_inc(stored, 16)
            sp.wait_ge(stored, 16)

        @block.tensor
        def _(pe):
            pe.wait_ge(loaded[2], 16)
            with pe.Fori(0, HR) as h:
                for i in range(2):
                    pe.wait_ge(loaded[i], 16 * (h + 1))
                    for b in range(2):
                        pe.wait_ge(taken, 4 * h + 2 * i)
                        for n in range(4):
                            last = pe.transpose(psT[b][:, n * P:(n + 1) * P], raw[i][:, 4 * b + n, :], k.ident[:])
                        last.then_inc(turned, 1)
                pe.wait_ge(taken, 4 * h + 4)
                pe.wait_ge(sm_done, 2 * h)
                for t in range(NT):
                    tok = slice(t * P, (t + 1) * P)
                    last = pe.matmul(psS[:, tok], kT[:, tok], qT[:, tok], start=True, stop=True)
                    if t % 4 == 3:
                        last.then_inc(scored, 1)
                pe.wait_ge(kd_done, h + 1)
                pe.wait_ge(state_done, (NT - 1) * h)
                for t in range(NT - 1):
                    pe.matmul(psKV[:, t * P:(t + 1) * P], kd[:, t, :], v[:, t, bass.ds(h * DR, DR)],
                              start=True, stop=True).then_inc(kv_done, 1)
                pe.wait_ge(qd_done, h + 1)
                pe.wait_ge(did, LINKS * h)
                for t in range(NT):
                    tok = slice(t * P, (t + 1) * P)
                    if t % 4 == 0:
                        pe.wait_ge(sm_done, 2 * h + t // 4 + 1)
                    pe.matmul(psO[:, tok], sm[:, tok], v[:, t, bass.ds(h * DR, DR)], start=True, stop=(t == 0))
                    if t:
                        pe.wait_ge(state_done, (NT - 1) * h + t)
                        last = pe.matmul(psO[:, tok], qTd[:, tok], state[:, t, :], start=False, stop=True)
                last.then_inc(product, 1)

        @block.scalar
        def _(act):
            def take(h):
                for i in range(4):
                    act.wait_ge(turned, 4 * h + i + 1)
                    if i == 0 and not isinstance(h, int):
                        act.wait_ge(scored, 2 * h)
                        act.wait_ge(qd_done, h)
                    act.copy((qT, kT)[i // 2][:, (i % 2) * CH:(i % 2 + 1) * CH], psT[i % 2]).then_inc(taken, 1)
                if not isinstance(h, int):
                    act.wait_ge(kv_done, (NT - 1) * h)
                act.activation(kd[:], raw[1][:], ACT.Copy, scale=k_dec[:, bass.ds(h, 1)]).then_inc(kd_done, 1)

            def root(h):
                act.wait_ge(meaned, h + 1)
                act.activation(sd[:], ms[:], ACT.Sqrt).then_inc(rooted, 1)

            act.preload_act_table(ACT.Sqrt)
            act.wait_ge(consts_loaded, 16 * 4)
            take(0)
            with act.Fori(0, HR - 1) as h:
                take(h + 1)
                root(h)
            root(HR - 1)

        @block.vector
        def _(dve):
            dve.wait_ge(consts_loaded, 16 * 4)
            dve.wait_ge(g_loaded, 16)
            with dve.Fori(0, HR) as h:
                one = bass.ds(h, 1)

                def over_tiles(ap, n):
                    return ap.to_broadcast([P, n, P])

                def each(ap):
                    return ap.rearrange("p (t o) -> p t o", o=1).to_broadcast([P, NT, DR])

                dve.wait_ge(taken, 4 * h + 4)
                dve.wait_ge(product, h)
                dve.tensor_tensor(qTd[:].rearrange("p (t n) -> p t n", n=P), qT[:].rearrange("p (t n) -> p t n", n=P),
                                  over_tiles(q_dec[:, one, :], NT), ALU.mult).then_inc(qd_done, 1)
                for b in range(2):
                    cols = slice(b * CH, (b + 1) * CH)
                    dve.wait_ge(scored, 2 * h + b + 1)
                    dve.tensor_tensor(sm[:, cols].rearrange("p (t n) -> p t n", n=P), psS[:, cols].rearrange("p (t n) -> p t n", n=P),
                                      over_tiles(dec[:, one, :], 4), ALU.mult).then_inc(sm_done, 1)
                for t in range(1, NT):
                    dve.wait_ge(kv_done, (NT - 1) * h + (4 if t <= 4 else NT - 1))
                    kv = psKV[:, (t - 1) * P:t * P]
                    if t == 1:
                        dve.tensor_copy(state[:, 1, :], kv).then_inc(state_done, 1)
                    else:
                        dve.wait_ge(state_done, (NT - 1) * h + t - 1)
                        dve.scalar_tensor_tensor(out=state[:, t, :], in0=state[:, t - 1, :], scalar=t_dec[:, one], in1=kv,
                                                 op0=ALU.mult, op1=ALU.add).then_inc(state_done, 1)
                n = [0]

                def link(ins):
                    n[0] += 1
                    ins.then_inc(did, 1)
                    dve.wait_ge(did, LINKS * h + n[0])

                o = psO.rearrange("p (t d) -> p t d", d=DR)
                dve.wait_ge(product, h + 1)
                link(dve.tensor_reduce(sums[:], o, X, ALU.add))
                link(dve.tensor_scalar(mu[:], sums[:], 1.0 / DR, None, ALU.mult))
                link(dve.tensor_tensor(cen[:], o, each(mu[:]), ALU.subtract))
                link(dve.tensor_tensor(sq[:], cen[:], cen[:], ALU.mult))
                link(dve.tensor_reduce(var_sum[:], sq[:], X, ALU.add))
                dve.tensor_scalar(ms[:], var_sum[:], 1.0 / DR, EPS, ALU.mult, ALU.add).then_inc(meaned, 1)
                dve.wait_ge(rooted, h + 1)
                link(dve.reciprocal(rs[:], sd[:]))
                link(dve.tensor_tensor(nrm[:], cen[:], each(rs[:]), ALU.mult))
                cols = bass.ds(h * DR, DR)
                dve.tensor_tensor(y[:, :, cols], nrm[:], g[:, :, cols], ALU.mult).then_inc(y_done, 1)


HS, DS = 8, 64
Z_TOP = 40.0


def stick_breaking_phase(nc, k, tag, proj, dst, mask):
    S0, SB, Y0 = 4 * HR * DR, HS * DS, HR * DR
    STEPS = 2 * NT
    with ExitStack() as stack:
        s = Scope(nc, tag, stack)
        raw = [s.sb(f"raw{i}", [P, NT, 2 * DS]) for i in range(2)]
        v, g = s.sb("v", [P, NT, SB]), s.sb("g", [P, NT, SB])
        qT, kT = ([s.sb(f"{n}{p}", [P, SEQ]) for p in range(2)] for n in ("qT", "kT"))
        z = [s.sb(f"z{p}", [P, 2, SEQ]) for p in range(3)]
        soft, T, w = ([s.sb(f"{n}{p}", [P, 2, SEQ]) for p in range(2)] for n in ("soft", "T", "w"))
        wT = [s.sb(f"wT{a}", [P, SEQ]) for a in range(2)]
        y = s.sb("y", [P, NT, SB])
        mask_raw, mask_r, ident_r = s.sb("mask_raw", [P, P]), s.sb("mask_r", [P, P], R), s.sb("ident_r", [P, P], R)
        psZ = k.ps[:, 0:2, :].rearrange("p b n -> p (b n)")
        psT = [[k.ps[:, 2 + 2 * a + i, :] for i in range(2)] for a in range(2)]
        psO = [k.ps[:, 6 + p, 0:2 * DS] for p in range(2)]
        psQ = [psT[a][1] for a in range(2)]
        loaded, v_loaded, mask_loaded, mask_done, stored = s.sems("loaded", 2), s.sem("v_loaded"), s.sem("mask_loaded"), s.sem("mask_done"), s.sem("stored")
        turned, taken, scored, copied, capped, exped, logged, softed, summed, weighed, w_done, w_turned, wT0, wT1, product, y_done = (
            s.sem(n) for n in ("turned", "taken", "scored", "copied", "capped", "exped", "logged", "softed", "summed",
                               "weighed", "w_done", "w_turned", "wT0", "wT1", "product", "y_done"))
        block = s.block()

        def part(ap):
            return ap.rearrange("(t p) d -> p t d", p=P)

        def wide(m):
            return (m % NT + 1) * P

        def second(m):
            return sum(2 * (wide(n) > CH) for n in range(m))

        ROUND_SECOND = second(STEPS)

        def turn_step(m):
            return m - 1 if 1 <= m <= 4 else None

        @block.sync
        def _(sp):
            def load(first):
                for i in range(2):
                    sp.dma_start(raw[i][:], part(proj[:, bass.ds(first[i], 2 * DS)])).then_inc(loaded[i], 16)

            load([S0 + i * SB for i in range(2)])
            sp.dma_start(mask_raw[:], mask).then_inc(mask_loaded, 16)
            sp.dma_start(v[:], part(proj[:, S0 + 2 * SB:S0 + 3 * SB])).then_inc(v_loaded, 16)
            sp.dma_start(g[:], part(proj[:, S0 + 3 * SB:S0 + 4 * SB])).then_inc(v_loaded, 16)
            with sp.Fori(1, HS // 2) as h:
                first = [sp.snap(h * 2 * DS + S0 + i * SB) for i in range(2)]
                sp.wait_ge(turned, 4 * h)
                load(first)
            sp.wait_ge(y_done, STEPS * HS // 4)
            sp.dma_start(part(dst[:, Y0:Y0 + SB]), y[:]).then_inc(stored, 16)
            sp.wait_ge(stored, 16)

        @block.tensor
        def _(pe):
            pe.wait_ge(mask_done, 2)
            pe.wait_ge(v_loaded, 32)
            with pe.Fori(0, HS // 4) as r:
                i0 = pe.snap(STEPS * r)

                def turn_qk(pair, group, bank):
                    i, b = group // 2, group % 2
                    pe.wait_ge(loaded[i], 16 * (2 * r + pair + 1))
                    for q in range(4):
                        last = pe.transpose(bank[:, q * P:(q + 1) * P], raw[i][:, 4 * b + q, :], k.ident[:])
                    last.then_inc(turned, 1)

                def score(m, a):
                    if m >= STEPS:
                        return
                    pair, t, half = m // NT, m % NT, slice(a * DS, (a + 1) * DS)
                    if m == NT and a == 0:
                        pe.wait_ge(taken, 8 * r + 8)
                    if m or a:
                        pe.wait_ge(copied, 2 * i0 + 2 * m + a)
                    for c in range(0, wide(m), CH):
                        end = min(c + CH, wide(m))
                        pe.matmul(psZ[:, c:end], qT[pair][half, t * P:(t + 1) * P], kT[pair][half, c:end],
                                  start=True, stop=(end < wide(m)))
                    pe.matmul(psZ[:, t * P:(t + 1) * P], ident_r[:], mask_r[:], start=False, stop=True).then_inc(scored, 1)

                def turn(m, a):
                    pe.wait_ge(w_done, i0 + m + 1)
                    if m == 4:
                        pe.wait_ge(taken, 8 * r + 8)
                    for kt in range(m % NT + 1):
                        last = pe.transpose(psT[a][kt // 4][:, kt % 4 * P:(kt % 4 + 1) * P], w[m % 2][:, a, kt * P:(kt + 1) * P], k.ident[:])
                    last.then_inc(w_turned, 1)

                def multiply(m, a):
                    pe.wait_ge(wT0, 2 * i0 + 2 * m + a + 1)
                    if m >= 2 and a == 0:
                        pe.wait_ge(y_done, i0 + m - 1)
                    for kt in range(m % NT + 1):
                        if kt == 4:
                            pe.wait_ge(wT1, ROUND_SECOND * r + second(m) + a + 1)
                        last = pe.matmul(psO[m % 2][:, a * DS:(a + 1) * DS], wT[a][:, kt * P:(kt + 1) * P],
                                         v[:, kt, bass.ds(r * 4 * DS + (m // NT * 2 + a) * DS, DS)],
                                         start=(kt == 0), stop=(kt == m % NT))
                    if a:
                        last.then_inc(product, 1)

                pe.wait_ge(y_done, i0)
                for group in range(4):
                    if group >= 2:
                        pe.wait_ge(taken, 8 * r + group - 1)
                    turn_qk(0, group, psQ[group % 2])
                pe.wait_ge(taken, 8 * r + 4)
                for m in range(2):
                    for a in range(2):
                        score(m, a)
                for m in range(STEPS + 1):
                    score(m + 2, 0)
                    if m >= 1:
                        turn(m - 1, 0)
                        turn(m - 1, 1)
                    score(m + 2, 1)
                    if m >= 1:
                        multiply(m - 1, 0)
                        multiply(m - 1, 1)
                    if turn_step(m) is not None:
                        pe.wait_ge(taken, 8 * r + 4 + turn_step(m))
                        turn_qk(1, turn_step(m), psQ[turn_step(m) % 2])

        @block.scalar
        def _(act):
            act.wait_ge(mask_loaded, 16)
            act.copy(mask_r[:], mask_raw[:]).then_inc(mask_done, 1)
            act.copy(ident_r[:], k.ident[:]).then_inc(mask_done, 1)
            act.preload_act_table_set("natural_log_exp_and_others")
            with act.Fori(0, HS // 4) as r:
                i0 = act.snap(STEPS * r)

                def take_qk(pair, group, bank):
                    act.wait_ge(turned, 8 * r + 4 * pair + group + 1)
                    act.activation((qT, kT)[group // 2][pair][:, (group % 2) * CH:(group % 2 + 1) * CH], bank, ACT.Copy,
                                   scale=DS ** -0.5 if group < 2 else 1.0).then_inc(taken, 1)

                def copy_z(m, a):
                    if m < STEPS:
                        act.wait_ge(scored, 2 * i0 + 2 * m + a + 1)
                        if m >= 3 and a == 0:
                            act.wait_ge(weighed, i0 + m - 2)
                        act.copy(z[m % 3][:, a, 0:wide(m)], psZ[:, 0:wide(m)]).then_inc(copied, 1)

                def exp(m):
                    if m < STEPS:
                        ap = soft[m % 2][:, :, 0:wide(m)]
                        act.wait_ge(capped, i0 + m + 1)
                        act.activation(ap, ap, ACT.Exp).then_inc(exped, 1)

                def log(m):
                    if m < STEPS:
                        ap = soft[m % 2][:, :, 0:wide(m)]
                        act.wait_ge(exped, i0 + m + 1)
                        act.activation(ap, ap, ACT.Ln, bias=1.0).then_inc(logged, 1)

                def weights(m):
                    if m < STEPS:
                        ap = w[m % 2][:, :, 0:wide(m)]
                        act.wait_ge(weighed, i0 + m + 1)
                        act.activation(ap, ap, ACT.Exp).then_inc(w_done, 1)

                def take(m, a):
                    cols = slice(0, min(wide(m), CH))
                    act.wait_ge(w_turned, 2 * i0 + 2 * m + a + 1)
                    if m:
                        act.wait_ge(product, i0 + m)
                    act.copy(wT[a][:, cols], psT[a][0][:, cols]).then_inc(wT0, 1)

                for group in range(4):
                    take_qk(0, group, psQ[group % 2])
                for m in range(2):
                    for a in range(2):
                        copy_z(m, a)
                exp(0)
                log(0)
                for m in range(STEPS + 1):
                    exp(m + 1)
                    log(m + 1)
                    copy_z(m + 2, 0)
                    if m >= 1:
                        take(m - 1, 0)
                        take(m - 1, 1)
                    copy_z(m + 2, 1)
                    if turn_step(m) is not None:
                        take_qk(1, turn_step(m), psQ[turn_step(m) % 2])
                    weights(m)

        @block.vector
        def _(dve):
            with dve.Fori(0, HS // 4) as r:
                i0 = dve.snap(STEPS * r)

                def cap(m):
                    if m < STEPS:
                        dve.wait_ge(copied, 2 * i0 + 2 * m + 2)
                        dve.tensor_scalar(soft[m % 2][:, :, 0:wide(m)], z[m % 3][:, :, 0:wide(m)], Z_TOP, None,
                                          ALU.min).then_inc(capped, 1)

                def soften(m):
                    p, cols = m % 2, slice(0, wide(m))
                    dve.wait_ge(logged, i0 + m + 1)
                    dve.tensor_tensor(soft[p][:, :, cols], z[m % 3][:, :, cols], soft[p][:, :, cols], ALU.max).then_inc(softed, 1)
                    dve.wait_ge(softed, i0 + m + 1)
                    for a in range(2):
                        back = soft[p][:, a, cols][:, ::-1]
                        dve.tensor_tensor_scan(T[p][:, a, cols][:, ::-1], back, back, 0.0, ALU.add, ALU.bypass).then_inc(summed, 1)

                def weigh(m):
                    p, cols = m % 2, slice(0, wide(m))
                    dve.wait_ge(summed, 2 * i0 + 2 * m + 2)
                    if m >= 2:
                        dve.wait_ge(w_turned, 2 * i0 + 2 * m - 2)
                    dve.tensor_tensor(w[p][:, :, cols], z[m % 3][:, :, cols], T[p][:, :, cols], ALU.subtract).then_inc(weighed, 1)

                def take(m, a):
                    if wide(m) > CH:
                        dve.wait_ge(w_turned, 2 * i0 + 2 * m + a + 1)
                        if m:
                            dve.wait_ge(product, i0 + m)
                        dve.tensor_copy(wT[a][:, CH:wide(m)], psT[a][1][:, 0:wide(m) - CH]).then_inc(wT1, 1)

                def rows(m):
                    dve.wait_ge(product, i0 + m + 1)
                    cols = bass.ds(r * 4 * DS + m // NT * 2 * DS, 2 * DS)
                    dve.tensor_tensor(y[:, m % NT, cols], psO[m % 2], g[:, m % NT, cols], ALU.mult).then_inc(y_done, 1)

                cap(0)
                for m in range(STEPS + 1):
                    cap(m + 1)
                    if m < STEPS:
                        soften(m)
                    if m >= 1:
                        take(m - 1, 0)
                        take(m - 1, 1)
                    if m < STEPS:
                        weigh(m)
                    if m >= 2:
                        rows(m - 2)
                rows(STEPS - 1)


def norm_phase(nc, k, src, gain, dst):
    with ExitStack() as stack:
        s = Scope(nc, "fin", stack)
        x = s.sb("x", [P, NT, DM])
        out = s.sb("out", [P, NT, DM])
        gain_b, junk = s.sb("gain", [P, DM]), s.sb("junk", [P, DM], BF)
        ss, ms, sd, rs = (s.sb(n, [P, NT]) for n in ("ss", "ms", "sd", "rs"))
        loaded, gain_loaded = s.sems("loaded", NT), s.sem("gain_loaded")
        squared, meaned, rooted, inverted, ready, stored = (s.sem(n) for n in (
            "squared", "meaned", "rooted", "inverted", "ready", "stored"))
        block = s.block()

        @block.sync
        def _(sp):
            sp.dma_start(gain_b[:], row_to_all(gain, DM)).then_inc(gain_loaded, 16)
            for t in range(NT):
                sp.dma_start(x[:, t, :], src[t * P:(t + 1) * P, :]).then_inc(loaded[t], 16)
            for t in range(NT):
                sp.wait_ge(ready, t + 1)
                sp.dma_start(dst[t * P:(t + 1) * P, :], out[:, t, :]).then_inc(stored, 16)
            sp.wait_ge(stored, 16 * NT)

        @block.scalar
        def _(act):
            act.preload_act_table(ACT.Sqrt)
            for t in range(NT):
                act.wait_ge(loaded[t], 16)
                act.activation(junk[:], x[:, t, :], ACT.Square, accum_out=ss[:, t:t + 1]).then_inc(squared, 1)
                act.wait_ge(meaned, t + 1)
                act.activation(sd[:, t:t + 1], ms[:, t:t + 1], ACT.Sqrt).then_inc(rooted, 1)

        @block.vector
        def _(dve):
            dve.wait_ge(gain_loaded, 16)
            for t in range(NT):
                one = slice(t, t + 1)
                dve.wait_ge(squared, t + 1)
                dve.tensor_scalar(ms[:, one], ss[:, one], 1.0 / DM, EPS, ALU.mult, ALU.add).then_inc(meaned, 1)
                dve.wait_ge(rooted, t + 1)
                dve.reciprocal(rs[:, one], sd[:, one]).then_inc(inverted, 1)
                dve.wait_ge(inverted, t + 1)
                dve.scalar_tensor_tensor(out=out[:, t, :], in0=x[:, t, :], scalar=rs[:, one], in1=gain_b[:],
                                         op0=ALU.mult, op1=ALU.mult).then_inc(ready, 1)


class Shared:
    pass


def build(nc, a, out):
    with ExitStack() as stack:
        k = Shared()
        k.ps = stack.enter_context(nc.psum_tensor("ps", [P, 8, CH], F))
        k.ident = stack.enter_context(nc.sbuf_tensor("ident", [P, P], F))
        k.slot_w = stack.enter_context(nc.sbuf_tensor("slot_w", [P, TOP_K, NT], F))
        k.block_expert = stack.enter_context(nc.sbuf_tensor("block_expert", [P, MAX_BLOCKS + 1], I32))
        ident_loaded = stack.enter_context(nc.semaphore("ident_loaded"))

        def scratch(name, shape, dt=F):
            return nc.dram_tensor(name, shape, dt).ap()

        k.tri_dram = a["triangle"]
        k.xn, k.slot_y = scratch("xn", [SEQ, DM]), scratch("slot_y", [SEQ * TOP_K + P, DM])
        k.slot_rows = scratch("slot_rows", [MAX_BLOCKS * P, 2], I32)
        k.bias_rows = scratch("bias_rows", [P, PAIRS, OFFS, GRID])
        k.neg_rpb = scratch("neg_rpb", [HB, OFFS, 2 * WIN_C - 1])
        proj, att, h1, h2, h3, h4, h5 = (scratch(n, [SEQ, w]) for n, w in (
            ("proj", 6 * CH), ("att", DM), ("h1", DM), ("h2", DM), ("h3", DM), ("h4", DM), ("h5", DM)))
        ple, proj2, y, mod = scratch("ple", [SEQ, DM]), scratch("proj2", [SEQ, 8 * CH]), scratch("y", [SEQ, DM]), scratch("mod", [LAYERS, 3, DM])

        with ExitStack() as first:
            block = first.enter_context(nc.Block())

            @block.sync
            def _(sp):
                sp.dma_start(k.ident[:], a["ident"]).then_inc(ident_loaded, 16)
                sp.wait_ge(ident_loaded, 16)

        x = a["x"][0]
        dense_phase(nc, k, "mix_in", x, a["w_in"][0], proj, ["normrope", "normrope", "copy", "norm", "norm", "copy"],
                    gain=a["g_mix"][0], rope=(a["cos_64"], a["sin_64"], DQK), head=[DQK, DQK, 0, DB_H, DB_H, 0],
                    head_gain={0: a["g_qa"][0], 1: a["g_ka"][0], 3: a["g_qb"][0], 4: a["g_kb"][0]})
        diff_attention_phase(nc, k, proj, att, [a[n][0] for n in ("lam_q1", "lam_k1", "lam_q2", "lam_k2")],
                             a["g_sub"][0], a["rpb"][0])
        neighbourhood_phase(nc, k, proj, att, a["neighbour"])
        dense_phase(nc, k, "mix_out", att, a["w_out"][0], h1, ["resid"] * 2, resid=x)
        router_phase(nc, k, h1, a["g_ffn"][0], a["w_rg"][0], a["w_re"][0], a["router"], a["token_ids"])
        expert_phase(nc, k, a["w1"][0], a["w3"][0], a["w2"][0])
        combine_phase(nc, k, h1, h2)
        ple_phase(nc, k, a["p"][0, 0], a["w_ple"][0], a["g_ple"][0], ple)
        dense_phase(nc, k, "ple_gate", h2, a["w_plg"][0], h3, ["gated"] * 2, gain=a["g_plg"][0], resid=h2, times=ple)
        ada_phase(nc, k, a["c_2"][0], a["w_ada_2"].rearrange("l k n -> (l k) n"), a["b_ada_2"], a["norm_g_2"], mod)
        for l, (h_in, h_out) in enumerate(((h3, h4), (h4, h5))):
            dense_phase(nc, k, f"in{l}", h_in, a["w_in_2"][l], proj2,
                        ["rope", "rope", "copy", "silu", "copy", "copy", "copy", "silu"],
                        gain=mod[l, 1], shift=mod[l, 0], rope=(a["cos_128"], a["sin_128"], DR))
            retention_phase(nc, k, f"ret{l}", proj2, y, a["decay"], a["q_decay"], a["k_decay"], a["tile_decay"])
            stick_breaking_phase(nc, k, f"stick{l}", proj2, y, a["stick_mask"])
            dense_phase(nc, k, f"out{l}", y, a["w_out_2"][l], h_out, ["resid"] * 2, resid=h_in, gate=mod[l, 2])
        norm_phase(nc, k, h5, a["final_g_2"], out[0])


def rope_table(dim):
    inv = (10000.0 ** (-np.arange(0, dim, 2, dtype=np.float32) / dim)).astype(np.float32)
    angle = (np.arange(SEQ, dtype=np.float32)[:, None] * inv[None, :]).astype(np.float32)
    return np.cos(angle), np.concatenate([-np.sin(angle), np.sin(angle)], axis=1)


def shape_constants():
    f = np.float32
    c = {"ident": np.eye(P, dtype=f), "triangle": np.triu(np.ones((P, P), f), 1)}
    c["router"] = np.concatenate([np.arange(8, 0, -1), np.arange(NT) * P, np.arange(MAX_BLOCKS)]).astype(f)
    slots, spare = SEQ * TOP_K, MAX_BLOCKS * P
    c["token_ids"] = np.concatenate([np.stack([np.tile(np.arange(SEQ), TOP_K), np.arange(slots)], 1),
                                     np.stack([np.zeros(spare, int), slots + np.arange(spare) % P], 1)]).astype(np.int32)
    p, col = np.arange(P)[:, None], np.arange(P)[None, :]
    c["neighbour"] = np.concatenate([(col % 64 // DB_H == p // GRID).astype(f), np.tile(np.eye(GRID, dtype=f), (2, 1))], axis=1)
    c["cos_64"], c["sin_64"] = rope_table(DQK)
    c["cos_128"], c["sin_128"] = rope_table(DR)
    log_gamma = np.log1p(-2.0 ** (-5.0 - np.arange(HR)))
    n = np.arange(P)
    allowed = n[:, None] // 64 <= n[None, :] // 64
    decay = np.exp(np.abs(n[None, :] - n[:, None])[:, None, :] * log_gamma[None, :, None]) * allowed[:, None, :]
    c["decay"] = (decay * DR ** -0.5).astype(f)
    c["q_decay"] = np.exp((n + 1)[None, :] * log_gamma[:, None]).astype(f).reshape(-1)
    c["k_decay"] = (np.exp((P - 1 - n)[:, None] * log_gamma[None, :]) * DR ** -0.5).astype(f)
    c["tile_decay"] = np.tile(np.exp(P * log_gamma), (P, 1)).astype(f)
    c["stick_mask"] = np.where(col >= p, -BIG, 0.0).astype(f)
    return c


def kernel(**inputs):
    import concourse.bacc as bacc
    from concourse.bass_utils import run_bass_kernel_spmd

    nc = bacc.Bacc("TRN2", target_bir_lowering=False, num_devices=1)
    arrays, aps = {}, {}
    for name, array in (*inputs.items(), *shape_constants().items()):
        array = np.ascontiguousarray(array)
        arrays[f"in_{name}_dram"] = array
        aps[name] = nc.dram_tensor(f"in_{name}_dram", array.shape, mybir.dt.from_np(array.dtype), kind="ExternalInput").ap()
    out = nc.dram_tensor("out_0_dram", (1, SEQ, DM), F, kind="ExternalOutput").ap()
    build(nc, aps, out)
    result = run_bass_kernel_spmd(nc, [arrays], core_ids=[0])
    return result.results[0]["out_0_dram"]
```

```python
import concourse.bass as bass
import numpy as np
from concourse import mybir
from contextlib import ExitStack

F = mybir.dt.float32
R = mybir.dt.float32r
BF = mybir.dt.bfloat16
I32 = mybir.dt.int32
ACT = mybir.ActivationFunctionType
ALU = mybir.AluOpType
X = mybir.AxisListType.X

P = 128
SEQ = 1024
DM = 1024
NT = SEQ // P
KT = DM // P
CH = 512
EPS = 1e-6
BIG = 1e30


class Scope:

    def __init__(self, nc, tag, stack):
        self.nc, self.tag, self.stack = nc, tag, stack
        self.handles = []
        stack.callback(self.finish)

    def finish(self):
        self.nc.clear_and_free_semaphores(self.handles)
        self.nc.all_engine_barrier()

    def sb(self, name, shape, dt=F):
        return self.stack.enter_context(self.nc.sbuf_tensor(f"{self.tag}_{name}", shape, dt))

    def sem(self, name):
        self.handles.append(self.nc.alloc_semaphore(name=f"{self.tag}_{name}"))
        return self.handles[-1]

    def pool_sem(self, name):
        return self.nc.alloc_semaphore(name=f"{self.tag}_{name}")

    def sems(self, name, n):
        return [self.sem(f"{name}{i}") for i in range(n)]

    def pool_sems(self, name, n):
        return [self.pool_sem(f"{name}{i}") for i in range(n)]

    def block(self):
        return self.stack.enter_context(self.nc.Block())


def row_to_all(row, n):
    return row.rearrange("(a n) -> a n", a=1).to_broadcast([P, n])


def dense_phase(nc, k, tag, src, w, dst, kinds, gain=None, shift=None, rope=None, head=None,
                head_gain=None, resid=None, gate=None, times=None, order=None):
    C = len(kinds)
    order = order or list(range(C))
    kinds = [kinds[o] for o in order]
    head = head and [head[o] for o in order]
    head_gain = {c: head_gain[o] for c, o in enumerate(order) if head_gain and o in head_gain}
    norm = gain is not None
    has_norm = [q in ("norm", "normrope") for q in kinds]
    has_rope = [q in ("normrope", "rope") for q in kinds]
    is_head = [a or b for a, b in zip(has_norm, has_rope)]
    extras = resid is not None

    def before(flags, c):
        return NT * sum(flags[:c])

    def columns(c):
        return slice(order[c] * CH, (order[c] + 1) * CH)

    with ExitStack() as stack:
        s = Scope(nc, tag, stack)
        x = [s.sb(f"x{p}", [P, DM]) for p in range(2)]
        xh = s.sb("xh", [P, KT, SEQ], R)
        xl = s.sb("xl", [P, KT, SEQ], R)
        raw = s.sb("raw", [P, 2, KT, CH])
        wh = s.sb("wh", [P, 2, KT, CH], R)
        wl = s.sb("wl", [P, 2, KT, CH], R)
        out = [s.sb(f"out{p}", [P, CH]) for p in range(2)]
        psT = [k.ps[:, b:b + 2, :].rearrange("p b n -> p (b n)") for b in (0, 4)]

        x_loaded = s.pool_sems("x_loaded", 2)
        raw_loaded, stored, extra_loaded = (s.sems(n, 2) for n in ("raw_loaded", "stored", "extra_loaded"))
        rows_loaded, consts_loaded, first_loaded = s.sem("rows_loaded"), s.sem("consts_loaded"), s.sems("first_loaded", 4)
        x_ss, x_ms, x_sd, x_rs, x_scaled, x_ready, x_turned, x_hi, x_lo = (s.sem(n) for n in (
            "x_ss", "x_ms", "x_sd", "x_rs", "x_scaled", "x_ready", "x_turned", "x_hi", "x_lo"))
        w_hi, w_lo, product, out_ready = (s.sem(n) for n in ("w_hi", "w_lo", "product", "out_ready"))

        rows, consts = [], []
        if norm:
            junk = s.sb("junk", [P, DM], BF)
            ss, ms, sd, rs = (s.sb(n, [P, NT]) for n in ("ss", "ms", "sd", "rs"))
            gain_b = s.sb("gain", [P, DM])
            rows.append((gain_b[:], row_to_all(gain, DM)))
            if shift is not None:
                shift_b = s.sb("shift", [P, DM])
                rows.append((shift_b[:], row_to_all(shift, DM)))
        if any(is_head):
            y = [s.sb(f"y{p}", [P, CH]) for p in range(2)]
            y2 = [s.sb(f"sq{p}", [P, CH]) for p in range(2)]
            z = [s.sb(f"z{p}", [P, CH]) for p in range(2)]
            hss, hms, hsd, hrs = (s.sb(n, [P, 16]) for n in ("hss", "hms", "hsd", "hrs"))
            h_val, hd_sq, hd_ss, hd_ms, hd_sd, hd_rs, hd_scaled, hd_gained, hd_cos, hd_sin = (
                s.sem(n) for n in ("h_val", "hd_sq", "hd_ss", "hd_ms", "hd_sd", "hd_rs", "hd_scaled",
                                   "hd_gained", "hd_cos", "hd_sin"))
            if any(has_rope):
                RD = rope[2]
                cos_t = s.sb("cos", [P, NT, RD // 2])
                sin_t = s.sb("sin", [P, NT, RD])
                consts.append((cos_t[:], rope[0].rearrange("(t p) d -> p t d", p=P)))
                consts.append((sin_t[:], rope[1].rearrange("(t p) d -> p t d", p=P)))
            hg = {}
            for c, row in head_gain.items():
                hg[c] = s.sb(f"hg{c}", [P, head[c]])
                consts.append((hg[c][:], row_to_all(row, head[c])))
        if extras:
            rt = [s.sb(f"rt{p}", [P, CH]) for p in range(2)]
            mid = [s.sb(f"mid{p}", [P, CH]) for p in range(2)]
            mid_done = s.sem("mid_done")
            if times is not None:
                tt = [s.sb(f"tt{p}", [P, CH]) for p in range(2)]
                sg = s.sb("sg", [P, CH])
                sg_done = s.sem("sg_done")
            if gate is not None:
                gate_b = s.sb("gate", [P, DM])
                consts.append((gate_b[:], row_to_all(gate, DM)))
        n_extra = 32 if times is not None else 16
        block = s.block()
        w_v = w.rearrange("(k p) n -> p k n", p=P)

        @block.sync
        def _(sp):
            for to, of in rows:
                sp.dma_start(to, of).then_inc(rows_loaded, 16)
            for i in range(4):
                kts = slice(i * KT // 4, (i + 1) * KT // 4)
                sp.dma_start(raw[:, 0, kts, :], w_v[:, kts, columns(0)]).then_inc(first_loaded[i], 16)
            for to, of in consts:
                sp.dma_start(to, of).then_inc(consts_loaded, 16)
            sp.dma_start(raw[:, 1, :, :], w_v[:, :, columns(1)]).then_inc(raw_loaded[1], 16)

            def load_extra(c, t, p):
                rows = bass.ds(t * P, P)
                sp.dma_start(rt[p][:], resid[rows, columns(c)]).then_inc(extra_loaded[p], 16)
                if times is not None:
                    sp.dma_start(tt[p][:], times[rows, columns(c)]).then_inc(extra_loaded[p], 16)

            def tile(c, t, p, ahead):
                sp.wait_ge(out_ready, c * NT + t + 1)
                sp.dma_start(dst[bass.ds(t * P, P), columns(c)], out[p][:]).then_inc(stored[p], 16)
                if extras and ahead is not None:
                    load_extra(*ahead, p)

            if extras:
                for p in range(2):
                    load_extra(0, p, p)
            for c in range(C):
                if c + 2 < C:
                    sp.wait_ge(w_lo, KT * (c + 1))
                    sp.dma_start(raw[:, c % 2, :, :], w_v[:, :, columns(c + 2)]).then_inc(raw_loaded[c % 2], 16)
                with sp.Fori(0, NT // 2 - 1) as j:
                    for p in range(2):
                        tile(c, 2 * j + p, p, (c, 2 * j + p + 2))
                for p in range(2):
                    tile(c, NT - 2 + p, p, (c + 1, p) if c + 1 < C else None)
            for p in range(2):
                sp.wait_ge(stored[p], 16 * C * NT // 2)

        @block.gpsimd
        def _(pool):
            for p in range(2):
                pool.dma_start(x[p][:], src[p * P:(p + 1) * P, :]).then_inc(x_loaded[p], 16)
            with pool.Fori(0, NT // 2 - 1) as j:
                for p in range(2):
                    pool.wait_ge(x_turned, 2 * j + p + 1)
                    pool.dma_start(x[p][:], src[bass.ds((2 * j + p + 2) * P, P), :]).then_inc(x_loaded[p], 16)

        @block.scalar
        def _(act):
            def split(c, kt):
                act.copy(wh[:, c % 2, bass.ds(kt, 1), :], raw[:, c % 2, bass.ds(kt, 1), :]).then_inc(w_hi, 1)

            def scale(t, p, j):
                if norm:
                    act.wait_ge(x_loaded[p], 16 * (j + 1))
                    act.activation(junk[:], x[p][:], ACT.Square, accum_out=ss[:, bass.ds(t, 1)]).then_inc(x_ss, 1)
                    act.wait_ge(x_ms, t + 1)
                    act.activation(sd[:, bass.ds(t, 1)], ms[:, bass.ds(t, 1)], ACT.Sqrt).then_inc(x_sd, 1)

            def take(t, p):
                act.wait_ge(x_turned, t + 1)
                act.copy(xh[:, :, bass.ds(t * P, P)], psT[p].rearrange("p (k n) -> p k n", k=KT)).then_inc(x_hi, 1)

            def post(c, t, p, j):
                kind = kinds[c]
                act.wait_ge(product, c * NT + t + 1)
                if kind in ("copy", "silu"):
                    act.wait_ge(stored[p], 16 * (c * NT // 2 + j))
                    if kind == "copy":
                        act.copy(out[p][:], k.ps[:, 2 + p, :]).then_inc(out_ready, 1)
                    else:
                        act.activation(out[p][:], k.ps[:, 2 + p, :], ACT.Silu).then_inc(out_ready, 1)
                elif is_head[c]:
                    act.copy(y[p][:], k.ps[:, 2 + p, :]).then_inc(h_val, 1)
                    if has_norm[c]:
                        act.activation(y2[p][:], k.ps[:, 2 + p, :], ACT.Square).then_inc(hd_sq, 1)
                        n = before(has_norm, c) + t
                        act.wait_ge(hd_ms, n + 1)
                        G = CH // head[c]
                        act.activation(hsd[:, 0:G], hms[:, 0:G], ACT.Sqrt).then_inc(hd_sd, 1)
                elif kind == "gated":
                    if not isinstance(t, int) or c * NT + t > 0:
                        act.wait_ge(mid_done, c * NT + t)
                    act.activation(sg[:], k.ps[:, 2 + p, :], ACT.Sigmoid).then_inc(sg_done, 1)

            act.preload_act_table(ACT.Sqrt if norm or any(has_norm) else ACT.Sigmoid if times is not None else ACT.Copy)
            scale(0, 0, 0)
            scale(1, 1, 0)
            take(0, 0)
            for kt in range(KT):
                act.wait_ge(first_loaded[kt * 4 // KT], 16)
                split(0, kt)
            for c in range(C):
                if kinds[c] == "silu":
                    act.preload_act_table(ACT.Silu)
                if c + 1 < C:
                    act.wait_ge(raw_loaded[(c + 1) % 2], 16 * ((c + 2) // 2))
                if c == 0:
                    with act.Fori(0, NT // 2 - 1) as j:
                        for p in range(2):
                            take(2 * j + p + 1, 1 - p)
                            scale(2 * j + p + 2, p, j + 1)
                            post(c, 2 * j + p, p, j)
                            if c + 1 < C:
                                split(c + 1, 2 * j + p)
                    take(NT - 1, 1)
                    for p in range(2):
                        post(c, NT - 2 + p, p, NT // 2 - 1)
                        if c + 1 < C:
                            split(c + 1, NT - 2 + p)
                else:
                    with act.Fori(0, NT // 2) as j:
                        for p in range(2):
                            post(c, 2 * j + p, p, j)
                            if c + 1 < C:
                                split(c + 1, 2 * j + p)

        @block.vector
        def _(dve):
            def split(c, kt):
                dve.wait_ge(w_hi, c * KT + kt + 1)
                dve.tensor_tensor(wl[:, c % 2, bass.ds(kt, 1), :], raw[:, c % 2, bass.ds(kt, 1), :],
                                  wh[:, c % 2, bass.ds(kt, 1), :].bitcast(F), ALU.subtract).then_inc(w_lo, 1)

            def scale(t, p):
                one = bass.ds(t, 1)
                if norm:
                    dve.wait_ge(x_ss, t + 1)
                    dve.tensor_scalar(ms[:, one], ss[:, one], 1.0 / DM, EPS, ALU.mult, ALU.add).then_inc(x_ms, 1)
                    dve.wait_ge(x_sd, t + 1)
                    dve.reciprocal(rs[:, one], sd[:, one]).then_inc(x_rs, 1)
                    dve.wait_ge(x_rs, t + 1)
                    last = dve.scalar_tensor_tensor(out=x[p][:], in0=x[p][:], scalar=rs[:, one], in1=gain_b[:],
                                                    op0=ALU.mult, op1=ALU.mult)
                    if shift is not None:
                        last.then_inc(x_scaled, 1)
                        dve.wait_ge(x_scaled, t + 1)
                        last = dve.tensor_tensor(x[p][:], x[p][:], shift_b[:], ALU.add)
                    last.then_inc(x_ready, 1)

            def take(t, p):
                dve.wait_ge(x_hi, t + 1)
                cols = bass.ds(t * P, P)
                dve.tensor_tensor(xl[:, :, cols], psT[p].rearrange("p (k n) -> p k n", k=KT),
                                  xh[:, :, cols].bitcast(F), ALU.subtract).then_inc(x_lo, 1)

            def post(c, t, p, j):
                g = c * NT + t
                if is_head[c]:
                    n, r, h = before(has_norm, c) + t, before(has_rope, c) + t, before(is_head, c) + t
                    dve.wait_ge(h_val, h + 1)
                    if has_norm[c]:
                        D = head[c]
                        G = CH // D
                        yv = y[p][:].rearrange("p (g d) -> p g d", d=D)
                        dve.wait_ge(hd_sq, n + 1)
                        dve.tensor_reduce(hss[:, 0:G], y2[p][:].rearrange("p (g d) -> p g d", d=D), X,
                                          ALU.add).then_inc(hd_ss, 1)
                        dve.wait_ge(hd_ss, n + 1)
                        dve.tensor_scalar(hms[:, 0:G], hss[:, 0:G], 1.0 / D, EPS, ALU.mult, ALU.add).then_inc(hd_ms, 1)
                        dve.wait_ge(hd_sd, n + 1)
                        dve.reciprocal(hrs[:, 0:G], hsd[:, 0:G]).then_inc(hd_rs, 1)
                        dve.wait_ge(hd_rs, n + 1)
                        dve.tensor_tensor(yv, yv, hrs[:, 0:G].rearrange("p (g o) -> p g o", o=1).to_broadcast([P, G, D]),
                                          ALU.mult).then_inc(hd_scaled, 1)
                        dve.wait_ge(hd_scaled, n + 1)
                        gb = hg[c][:].rearrange("p (o d) -> p o d", o=1).to_broadcast([P, G, D])
                        if not has_rope[c]:
                            dve.wait_ge(stored[p], 16 * (c * NT // 2 + j))
                            dve.tensor_tensor(out[p][:].rearrange("p (g d) -> p g d", d=D), yv, gb,
                                              ALU.mult).then_inc(out_ready, 1)
                        else:
                            dve.tensor_tensor(yv, yv, gb, ALU.mult).then_inc(hd_gained, 1)
                            dve.wait_ge(hd_gained, r + 1)
                    if has_rope[c]:
                        dve.wait_ge(stored[p], 16 * (c * NT // 2 + j))
                        G, Hf = CH // RD, RD // 2
                        y4 = y[p][:].rearrange("p (g a d) -> p g a d", a=2, d=Hf)
                        c4 = cos_t[:, bass.ds(t, 1), :].rearrange("p o (a d) -> p o a d", a=1).to_broadcast([P, G, 2, Hf])
                        dve.tensor_tensor(y2[p][:].rearrange("p (g a d) -> p g a d", a=2, d=Hf), y4, c4,
                                          ALU.mult).then_inc(hd_cos, 1)
                        s4 = sin_t[:, bass.ds(t, 1), :].rearrange("p o (a d) -> p o a d", a=2).to_broadcast([P, G, 2, Hf])
                        dve.tensor_tensor(z[p][:].rearrange("p (g a d) -> p g a d", a=2, d=Hf), y4[:, :, ::-1, :], s4,
                                          ALU.mult).then_inc(hd_sin, 1)
                        dve.wait_ge(hd_cos, r + 1)
                        dve.wait_ge(hd_sin, r + 1)
                        dve.tensor_tensor(out[p][:], y2[p][:], z[p][:], ALU.add).then_inc(out_ready, 1)
                elif kinds[c] == "resid":
                    dve.wait_ge(extra_loaded[p], n_extra * (c * NT // 2 + j + 1))
                    dve.wait_ge(product, g + 1)
                    dve.wait_ge(stored[p], 16 * (c * NT // 2 + j))
                    if gate is None:
                        dve.tensor_tensor(out[p][:], k.ps[:, 2 + p, :], rt[p][:], ALU.add).then_inc(out_ready, 1)
                    else:
                        dve.tensor_tensor(mid[p][:], k.ps[:, 2 + p, :], gate_b[:, columns(c)],
                                          ALU.mult).then_inc(mid_done, 1)
                        dve.wait_ge(mid_done, g + 1)
                        dve.tensor_tensor(out[p][:], mid[p][:], rt[p][:], ALU.add).then_inc(out_ready, 1)
                elif kinds[c] == "gated":
                    dve.wait_ge(extra_loaded[p], n_extra * (c * NT // 2 + j + 1))
                    dve.wait_ge(sg_done, g + 1)
                    dve.wait_ge(stored[p], 16 * (c * NT // 2 + j))
                    dve.tensor_tensor(mid[p][:], sg[:], tt[p][:], ALU.mult).then_inc(mid_done, 1)
                    dve.wait_ge(mid_done, g + 1)
                    dve.tensor_tensor(out[p][:], mid[p][:], rt[p][:], ALU.add).then_inc(out_ready, 1)

            if rows:
                dve.wait_ge(rows_loaded, 16 * len(rows))
            scale(0, 0)
            scale(1, 1)
            take(0, 0)
            with dve.Fori(0, KT) as kt:
                split(0, kt)
            if consts:
                dve.wait_ge(consts_loaded, 16 * len(consts))
            for c in range(C):
                if c > 0 and c + 1 < C:
                    dve.wait_ge(product, c * NT)
                if c == 0:
                    with dve.Fori(0, NT // 2 - 1) as j:
                        for p in range(2):
                            take(2 * j + p + 1, 1 - p)
                            scale(2 * j + p + 2, p)
                            post(c, 2 * j + p, p, j)
                            if c + 1 < C:
                                split(c + 1, 2 * j + p)
                    take(NT - 1, 1)
                    for p in range(2):
                        post(c, NT - 2 + p, p, NT // 2 - 1)
                        if c + 1 < C:
                            split(c + 1, NT - 2 + p)
                else:
                    with dve.Fori(0, NT // 2) as j:
                        for p in range(2):
                            post(c, 2 * j + p, p, j)
                            if c + 1 < C:
                                split(c + 1, 2 * j + p)

        @block.tensor
        def _(pe):
            def turn(t):
                p = t % 2
                if norm:
                    pe.wait_ge(x_ready, t + 1)
                else:
                    pe.wait_ge(x_loaded[p], 16 * (t // 2 + 1))
                if t >= 2:
                    pe.wait_ge(x_lo, t - 1)
                for kt in range(KT):
                    last = pe.transpose(psT[p][:, kt * P:(kt + 1) * P], x[p][:, kt * P:(kt + 1) * P], k.ident[:])
                last.then_inc(x_turned, 1)

            def multiply(c, b, t):
                p = t % 2
                for kt in range(KT):
                    if isinstance(c, int) and t == 0:
                        pe.wait_ge(w_lo, kt + 1)
                    tok = slice(t * P, (t + 1) * P)
                    o = k.ps[:, 2 + p, :]
                    wb = [v[:, bass.ds(b, 1), kt, :].rearrange("p o n -> p (o n)") for v in (wh, wl)]
                    pe.matmul(o, xh[:, kt, tok], wb[0], start=(kt == 0), stop=False)
                    pe.matmul(o, xh[:, kt, tok], wb[1], start=False, stop=False)
                    last = pe.matmul(o, xl[:, kt, tok], wb[0], start=False, stop=(kt == KT - 1))
                last.then_inc(product, 1)

            turn(0)
            for t in range(NT):
                if t + 1 < NT:
                    turn(t + 1)
                pe.wait_ge(x_lo, t + 1)
                if t >= 2:
                    pe.wait_ge(out_ready, t - 1)
                multiply(0, 0, t)
            with pe.Fori(1, C) as c:
                pe.wait_ge(w_lo, c * KT + KT)
                b = pe.snap(c % 2)
                for t in range(NT):
                    pe.wait_ge(out_ready, c * NT + t - 1)
                    multiply(c, b, t)


N_GROUPS, PER_GROUP, TOP_K, D_EXPERT = 4, 8, 2, 512
N_EXPERTS = N_GROUPS * PER_GROUP
MAX_BLOCKS = SEQ * TOP_K // P + N_EXPERTS
LEAST_BLOCKS = SEQ * TOP_K // P


def router_phase(nc, k, src, gain, w_rg, w_re, consts, token_ids):
    NL = N_GROUPS + N_EXPERTS
    XB = 4
    rev, thresholds, block_no = consts[0:8], consts[8:16], consts[16:16 + MAX_BLOCKS]
    with ExitStack() as stack:
        s = Scope(nc, "rt", stack)
        x = [s.sb(f"x{q}", [P, DM]) for q in range(XB)]
        junk = s.sb("junk", [P, DM], BF)
        gain_b = s.sb("gain", [P, DM])
        xt = [s.sb(f"xt{p}", [P, DM]) for p in range(2)]
        wr = s.sb("wr", [P, KT, NL])
        ss, ms, sd, rs = (s.sb(n, [P, NT]) for n in ("ss", "ms", "sd", "rs"))
        L = s.sb("L", [P, NT, NL])
        tri, ones = s.sb("tri", [P, P]), s.sb("ones", [P, P])
        tok = s.sb("tok", [P, TOP_K, NT, 2], I32)
        spare = s.sb("spare", [P, MAX_BLOCKS, 2], I32)
        slot = s.sb("slot", [P, TOP_K, NT], I32)
        rev_b, thr_b, no_b = s.sb("rev", [P, 8]), s.sb("thr", [P, 8]), s.sb("no", [P, MAX_BLOCKS])
        gmax, gsum, gate, kmax = (s.sb(n, [P, NT]) for n in ("gmax", "gsum", "gate", "kmax"))
        gd, gexp, gkey, goh = (s.sb(n, [P, NT, N_GROUPS]) for n in ("gd", "gexp", "gkey", "goh"))
        grouped = s.sb("grouped", [P, NT, N_EXPERTS])
        sel, d1, key, low = (s.sb(n, [P, NT, PER_GROUP]) for n in ("sel", "d1", "key", "low"))
        oh = [s.sb(f"oh{i}", [P, NT, PER_GROUP]) for i in range(2)]
        top = [s.sb(f"top{i}", [P, NT]) for i in range(2)]
        dtop, etop, den, rden = (s.sb(n, [P, NT]) for n in ("dtop", "etop", "den", "rden"))
        M = [s.sb(f"M{i}", [P, NT, N_EXPERTS]) for i in range(2)]
        both = s.sb("both", [P, NT, N_EXPERTS])
        ahead = s.sb("ahead", [P, NT + 1, N_EXPERTS])
        more = s.sb("more", [P, N_EXPERTS, 8])
        blocks, upto, first = (s.sb(n, [P, N_EXPERTS]) for n in ("blocks", "upto", "first"))
        place, mine = (s.sb(n, [P, NT, N_EXPERTS]) for n in ("place", "mine"))
        slot_f = s.sb("slot_f", [P, NT])
        past = s.sb("past", [P, MAX_BLOCKS, N_EXPERTS])
        be_f = s.sb("be_f", [P, MAX_BLOCKS])
        psT = [k.ps[:, b:b + 2, :].rearrange("p b n -> p (b n)") for b in (0, 6)]
        ps_logit = k.ps[:, 2, 0:NT * NL]
        ps_rank = k.ps[:, 3, 0:NT * N_EXPERTS]
        ps_count = k.ps[:, 4, 0:N_EXPERTS]

        x_loaded, x_stored = s.pool_sems("x_loaded", XB), s.sems("x_stored", XB)
        gain_loaded, weights_loaded = s.sem("gain_loaded"), s.sem("weights_loaded")
        consts_loaded, cleared, spare_written = (s.sem(n) for n in ("consts_loaded", "cleared", "spare_written"))
        scattered = s.pool_sem("scattered")
        x_ss, x_ms, x_sd, x_rs, x_ready, x_turned, x_out, logits = (s.sem(n) for n in (
            "x_ss", "x_ms", "x_sd", "x_rs", "x_ready", "x_turned", "x_out", "logits"))
        did, gd_done, gexp_done, dtop_done, etop_done, ahead_done, ranked, slots_done = (s.sem(n) for n in (
            "did", "gd_done", "gexp_done", "dtop_done", "etop_done", "ahead_done", "ranked", "slots_done"))
        block = s.block()

        @block.sync
        def _(sp):
            sp.dma_start(gain_b[:], row_to_all(gain, DM)).then_inc(gain_loaded, 16)
            sp.dma_start(wr[:, :, 0:N_GROUPS], w_rg.rearrange("(k p) n -> p k n", p=P)).then_inc(weights_loaded, 16)
            sp.dma_start(wr[:, :, N_GROUPS:NL], w_re.rearrange("(k p) n -> p k n", p=P)).then_inc(weights_loaded, 16)
            with sp.Fori(0, NT // XB) as j:
                for q in range(XB):
                    t = XB * j + q
                    sp.wait_ge(x_ready, t + 1)
                    sp.dma_start(k.xn[bass.ds(t * P, P), :], x[q][:]).then_inc(x_stored[q], 16)
            for q in range(XB):
                sp.wait_ge(x_stored[q], 16 * NT // XB)

        @block.gpsimd
        def _(pool):
            for q in range(XB):
                pool.dma_start(x[q][:], src[q * P:(q + 1) * P, :]).then_inc(x_loaded[q], 16)
            pool.memset(ones[:], 1.0).then_inc(cleared, 1)
            pool.memset(ahead[:, 0, :], 0.0).then_inc(cleared, 1)
            for t in range(XB, NT):
                q = t % XB
                pool.wait_ge(x_turned, t - XB + 1)
                pool.wait_ge(x_stored[q], 16 * (t // XB))
                pool.dma_start(x[q][:], src[t * P:(t + 1) * P, :]).then_inc(x_loaded[q], 16)
            pool.wait_ge(spare_written, 16)
            pool.wait_ge(consts_loaded, 16 * 6)
            pool.wait_ge(slots_done, 2)
            for i in range(TOP_K):
                for t in range(NT):
                    pool.indirect_dma_start(
                        out=k.slot_rows[:, :], out_offset=bass.IndirectOffsetOnAxis(ap=slot[:, i, t:t + 1], axis=0),
                        in_=tok[:, i, t, :], in_offset=None).then_inc(scattered, 16)
            pool.wait_ge(scattered, 16 * TOP_K * NT)

        @block.scalar
        def _(act):
            def square(t, q, j):
                one = bass.ds(t, 1)
                act.wait_ge(x_loaded[q], 16 * (j + 1))
                act.activation(junk[:], x[q][:], ACT.Square, accum_out=ss[:, one]).then_inc(x_ss, 1)
                act.wait_ge(x_ms, t + 1)
                act.activation(sd[:, one], ms[:, one], ACT.Sqrt).then_inc(x_sd, 1)

            def take(t, p):
                act.wait_ge(x_turned, t + 1)
                if t >= 2:
                    act.wait_ge(logits, t - 1)
                act.copy(xt[p][:], psT[p]).then_inc(x_out, 1)

            for to, of in ((tri[:], k.tri_dram), (tok[:], token_ids[0:TOP_K * SEQ, :].rearrange("(i t p) a -> p i t a", p=P, i=TOP_K)),
                           (spare[:], token_ids[TOP_K * SEQ:, :].rearrange("(b p) a -> p b a", p=P)),
                           (rev_b[:], row_to_all(rev, 8)), (thr_b[:], row_to_all(thresholds, 8)),
                           (no_b[:], row_to_all(block_no, MAX_BLOCKS))):
                act.dma_start(to, of, allow_slow_non_contiguous=True).then_inc(consts_loaded, 16)
            act.preload_act_table(ACT.Sqrt)
            square(0, 0, 0)
            for t in range(NT):
                if t + 1 < NT:
                    square(t + 1, (t + 1) % XB, (t + 1) // XB)
                take(t, t % 2)
            act.wait_ge(consts_loaded, 16 * 6)
            act.dma_start(k.slot_rows.rearrange("(b p) a -> p b a", p=P), spare[:],
                          allow_slow_non_contiguous=True).then_inc(spare_written, 16)
            act.preload_act_table(ACT.Exp)
            act.wait_ge(gd_done, 1)
            act.activation(gexp[:], gd[:], ACT.Exp).then_inc(gexp_done, 1)
            act.wait_ge(dtop_done, 1)
            act.activation(etop[:], dtop[:], ACT.Exp).then_inc(etop_done, 1)

        @block.tensor
        def _(pe):
            def turn(t):
                pe.wait_ge(x_ready, t + 1)
                if t >= 2:
                    pe.wait_ge(x_out, t - 1)
                for kt in range(KT):
                    last = pe.transpose(psT[t % 2][:, kt * P:(kt + 1) * P], x[t % XB][:, kt * P:(kt + 1) * P], k.ident[:])
                last.then_inc(x_turned, 1)

            turn(0)
            pe.wait_ge(weights_loaded, 32)
            for t in range(NT):
                if t + 1 < NT:
                    turn(t + 1)
                pe.wait_ge(x_out, t + 1)
                for kt in range(KT):
                    last = pe.matmul(ps_logit[:, t * NL:(t + 1) * NL], xt[t % 2][:, kt * P:(kt + 1) * P], wr[:, kt, :],
                                     start=(kt == 0), stop=(kt == KT - 1))
                last.then_inc(logits, 1)
            pe.wait_ge(consts_loaded, 16 * 6)
            pe.wait_ge(cleared, 2)
            pe.wait_ge(ahead_done, NT + 1)
            pe.matmul(ps_rank, tri[:], both[:].rearrange("p t e -> p (t e)"), start=True, stop=False)
            pe.matmul(ps_rank, ones[:], ahead[:, 0:NT, :].rearrange("p t e -> p (t e)"), start=False, stop=True)
            pe.matmul(ps_count, ones[:], ahead[:, NT, :], start=True, stop=True).then_inc(ranked, 1)

        @block.vector
        def _(dve):
            dve.wait_ge(gain_loaded, 16)
            with dve.Fori(0, NT // XB) as j:
                for q in range(XB):
                    t = XB * j + q
                    one = bass.ds(t, 1)
                    dve.wait_ge(x_ss, t + 1)
                    dve.tensor_scalar(ms[:, one], ss[:, one], 1.0 / DM, EPS, ALU.mult, ALU.add).then_inc(x_ms, 1)
                    dve.wait_ge(x_sd, t + 1)
                    dve.reciprocal(rs[:, one], sd[:, one]).then_inc(x_rs, 1)
                    dve.wait_ge(x_rs, t + 1)
                    dve.scalar_tensor_tensor(out=x[q][:], in0=x[q][:], scalar=rs[:, one], in1=gain_b[:],
                                             op0=ALU.mult, op1=ALU.mult).then_inc(x_ready, 1)
            dve.wait_ge(consts_loaded, 16 * 6)
            n = [0]

            def link(ins):
                n[0] += 1
                ins.then_inc(did, 1)
                dve.wait_ge(did, n[0])

            def spread(row, width):
                return row.rearrange("p (t o) -> p t o", o=1).to_broadcast([P, NT, width])

            def each(row, width):
                return row.rearrange("p (o n) -> p o n", o=1).to_broadcast([P, NT, width])

            def first_of(values, largest, hot, width, keys):
                link(dve.tensor_tensor(keys, values, spread(largest, width), ALU.is_ge))
                link(dve.tensor_tensor(keys, keys, each(rev_b[:, 8 - width:8], width), ALU.mult))
                link(dve.tensor_reduce(kmax[:], keys, X, ALU.max))
                link(dve.tensor_tensor(hot, keys, spread(kmax[:], width), ALU.is_equal))

            dve.wait_ge(logits, NT)
            link(dve.tensor_copy(L[:], ps_logit.rearrange("p (t n) -> p t n", n=NL)))
            gl = L[:, :, 0:N_GROUPS]
            link(dve.tensor_reduce(gmax[:], gl, X, ALU.max))
            dve.tensor_tensor(gd[:], gl, spread(gmax[:], N_GROUPS), ALU.subtract).then_inc(gd_done, 1)
            first_of(gl, gmax[:], goh[:], N_GROUPS, gkey[:])
            link(dve.tensor_tensor(grouped[:].rearrange("p t (g e) -> p t g e", g=N_GROUPS),
                                   L[:, :, N_GROUPS:NL].rearrange("p t (g e) -> p t g e", g=N_GROUPS),
                                   goh[:].rearrange("p t (g o) -> p t g o", o=1).to_broadcast([P, NT, N_GROUPS, PER_GROUP]),
                                   ALU.mult))
            link(dve.tensor_reduce(sel[:], grouped[:].rearrange("p t (g e) -> p t e g", g=N_GROUPS), X, ALU.add))
            link(dve.tensor_reduce(top[0][:], sel[:], X, ALU.max))
            first_of(sel[:], top[0][:], oh[0][:], PER_GROUP, key[:])
            link(dve.scalar_tensor_tensor(out=low[:], in0=oh[0][:], scalar=-BIG, in1=sel[:], op0=ALU.mult, op1=ALU.add))
            link(dve.tensor_reduce(top[1][:], low[:], X, ALU.max))
            dve.tensor_tensor(dtop[:], top[1][:], top[0][:], ALU.subtract).then_inc(dtop_done, 1)
            first_of(low[:], top[1][:], oh[1][:], PER_GROUP, key[:])
            for i in range(2):
                link(dve.tensor_tensor(M[i][:].rearrange("p t (g e) -> p t g e", g=N_GROUPS),
                                       goh[:].rearrange("p t (g o) -> p t g o", o=1).to_broadcast([P, NT, N_GROUPS, PER_GROUP]),
                                       oh[i][:].rearrange("p t (o e) -> p t o e", o=1).to_broadcast([P, NT, N_GROUPS, PER_GROUP]),
                                       ALU.mult))
            dve.tensor_tensor(both[:], M[0][:], M[1][:], ALU.add).then_inc(ahead_done, 1)
            dve.wait_ge(cleared, 2)
            for t in range(NT):
                dve.wait_ge(ahead_done, t + 1)
                dve.tensor_tensor(ahead[:, t + 1, :], ahead[:, t, :], both[:, t, :], ALU.add).then_inc(ahead_done, 1)
            dve.wait_ge(gexp_done, 1)
            link(dve.tensor_reduce(gsum[:], gexp[:], X, ALU.add))
            link(dve.reciprocal(gate[:], gsum[:]))
            dve.wait_ge(etop_done, 1)
            link(dve.tensor_scalar(den[:], etop[:], 1.0, None, ALU.add))
            link(dve.reciprocal(rden[:], den[:]))
            link(dve.tensor_tensor(k.slot_w[:, 0, :], gate[:], rden[:], ALU.mult))
            link(dve.tensor_tensor(k.slot_w[:, 1, :], k.slot_w[:, 0, :], etop[:], ALU.mult))
            dve.wait_ge(ranked, 1)
            link(dve.tensor_copy(blocks[:], ps_count))
            link(dve.tensor_tensor(more[:], blocks[:].rearrange("p (e o) -> p e o", o=1).to_broadcast([P, N_EXPERTS, 8]),
                                   thr_b[:].rearrange("p (o i) -> p o i", o=1).to_broadcast([P, N_EXPERTS, 8]), ALU.is_gt))
            link(dve.tensor_reduce(blocks[:], more[:], X, ALU.add))
            link(dve.tensor_tensor_scan(upto[:], blocks[:], blocks[:], 0.0, ALU.add, ALU.bypass))
            link(dve.tensor_tensor(first[:], upto[:], blocks[:], ALU.subtract))
            link(dve.tensor_scalar(first[:], first[:], float(P), None, ALU.mult))
            link(dve.tensor_tensor(place[:], ps_rank.rearrange("p (t e) -> p t e", e=N_EXPERTS),
                                   each(first[:], N_EXPERTS), ALU.add))
            for i in range(TOP_K):
                link(dve.tensor_tensor(mine[:], place[:], M[i][:], ALU.mult))
                link(dve.tensor_reduce(slot_f[:], mine[:], X, ALU.add))
                dve.tensor_copy(slot[:, i, :], slot_f[:]).then_inc(slots_done, 1)
                dve.wait_ge(slots_done, i + 1)
            link(dve.tensor_tensor(past[:], upto[:].rearrange("p (o e) -> p o e", o=1).to_broadcast([P, MAX_BLOCKS, N_EXPERTS]),
                                   no_b[:].rearrange("p (b o) -> p b o", o=1).to_broadcast([P, MAX_BLOCKS, N_EXPERTS]), ALU.is_le))
            link(dve.tensor_reduce(be_f[:], past[:], X, ALU.add))
            link(dve.tensor_copy(k.block_expert[:, 0:MAX_BLOCKS], be_f[:]))
            link(dve.tensor_scalar(k.block_expert[:, MAX_BLOCKS:MAX_BLOCKS + 1], upto[:, N_EXPERTS - 1:N_EXPERTS],
                                   -2.0, None, ALU.add))


def expert_phase(nc, k, w1, w3, w2):
    HK = KT // 2
    YK = D_EXPERT // P
    with ExitStack() as stack:
        s = Scope(nc, "ex", stack)
        names = ["w1a", "w1b", "w3a", "w3b"]
        raw_h, hi_h, lo_h = ([s.sb(f"{v}_{n}", [P, HK, CH], dt) for n in names]
                             for v, dt in (("raw", F), ("hi", R), ("lo", R)))
        raw_y, hi_y, lo_y = ([s.sb(f"{v}_w2{n}", [P, YK, CH], dt) for n in "ab"]
                             for v, dt in (("raw", F), ("hi", R), ("lo", R)))
        idx = s.sb("idx", [P, 2], I32)
        row = s.sb("row", [P, 2], I32)
        idx_own, row_own = s.sb("idx_own", [P, 2], I32), s.sb("row_own", [P, 2], I32)
        nothing = s.sb("nothing", [P, 2], I32)
        copied = s.sem("copied")
        xg = s.sb("xg", [P, DM])
        xh, xl = s.sb("xh", [P, KT, P], R), s.sb("xl", [P, KT, P], R)
        act1, hid = s.sb("act1", [P, CH]), s.sb("hid", [P, CH])
        hh, hl = s.sb("hh", [P, YK, P], R), s.sb("hl", [P, YK, P], R)
        y = s.sb("y", [P, DM])
        psX = k.ps[:, 0:2, :].rearrange("p b n -> p (b n)")
        psH = [k.ps[:, 2, :], k.ps[:, 3, :]]
        psHT = k.ps[:, 4, :]
        psY = [k.ps[:, 5, :], k.ps[:, 6, :]]

        h_loaded, y_loaded = s.sems("h_loaded", 4), s.sems("y_loaded", 2)
        idx_loaded, row_loaded, gathered, stored = (s.pool_sem(n) for n in ("idx_loaded", "row_loaded", "gathered", "stored"))
        h_hi, h_lo, h_used, y_hi, y_lo, y_used = (s.sem(n) for n in (
            "h_hi", "h_lo", "h_used", "y_hi", "y_lo", "y_used"))
        x_turned, x_hi, x_lo, silu_done, hid_ready, hid_turned, hid_hi, hid_lo, y_out = (s.sem(n) for n in (
            "x_turned", "x_hi", "x_lo", "silu_done", "hid_ready", "hid_turned", "hid_hi", "hid_lo", "y_out"))
        block = s.block()

        def blocks_less_2(eng):
            return eng.value_load(k.block_expert[0:1, MAX_BLOCKS:MAX_BLOCKS + 1], min_val=LEAST_BLOCKS - 2,
                                  max_val=MAX_BLOCKS - 3)

        @block.sync
        def _(sp):
            def expert(n):
                return sp.value_load(k.block_expert[0:1, bass.ds(n, 1)], min_val=0, max_val=N_EXPERTS - 1)

            def load_h(n):
                e = bass.ds(expert(n), 1)
                for i, w in enumerate((w1, w3)):
                    for half in range(2):
                        j = 2 * i + half
                        if not isinstance(n, int) or n > 0:
                            sp.wait_ge(h_lo, 4 * (n - 1) + j + 1)
                        rows = slice(half * HK * P, (half + 1) * HK * P)
                        sp.dma_start(raw_h[j][:], w[e, rows, :].rearrange("o (k p) n -> p (o k) n", p=P)).then_inc(h_loaded[j], 16)

            def load_y(n):
                e = bass.ds(expert(n), 1)
                for j in range(2):
                    if not isinstance(n, int) or n > 0:
                        sp.wait_ge(y_lo, 2 * (n - 1) + j + 1)
                    sp.dma_start(raw_y[j][:], w2[e, :, j * CH:(j + 1) * CH].rearrange("o (k p) n -> p (o k) n", p=P)).then_inc(y_loaded[j], 16)

            N2 = blocks_less_2(sp)
            load_h(0)
            load_y(0)
            load_h(1)
            with sp.Fori(0, N2) as n:
                load_h(n + 2)
                load_y(n + 1)
            load_y(N2 + 1)

        @block.gpsimd
        def _(pool):
            def hand_over(of, to):
                pool.tensor_tensor(to[:], of[:], nothing[:], ALU.add).then_inc(copied, 1)
                pool.wait_ge(copied, 1)
                pool.sem_clear(copied)

            def load_idx(n):
                pool.dma_start(idx[:], k.slot_rows[bass.ds(n * P, P), :]).then_inc(idx_loaded, 16)

            def load_row(n):
                pool.dma_start(row[:], k.slot_rows[bass.ds(n * P, P), :]).then_inc(row_loaded, 16)

            def gather(n):
                pool.wait_ge(idx_loaded, 16 * (n + 1))
                if not isinstance(n, int) or n > 0:
                    pool.wait_ge(gathered, 16 * n)
                hand_over(idx, idx_own)
                pool.indirect_dma_start(out=xg[:], out_offset=None, in_=k.xn[:, :],
                                        in_offset=bass.IndirectOffsetOnAxis(ap=idx_own[:, 0:1], axis=0)).then_inc(gathered, 16)

            def scatter(n):
                pool.wait_ge(row_loaded, 16 * (n + 1))
                pool.wait_ge(stored, 16 * n)
                pool.wait_ge(y_out, 2 * n + 2)
                hand_over(row, row_own)
                pool.indirect_dma_start(out=k.slot_y[:, :], out_offset=bass.IndirectOffsetOnAxis(ap=row_own[:, 1:2], axis=0),
                                        in_=y[:], in_offset=None).then_inc(stored, 16)

            N2 = blocks_less_2(pool)
            pool.memset(nothing[:], 0).then_inc(copied, 1)
            pool.wait_ge(copied, 1)
            pool.sem_clear(copied)
            load_idx(0)
            load_row(0)
            gather(0)
            load_idx(1)
            pool.wait_ge(x_turned, 1)
            gather(1)
            load_idx(2)
            with pool.Fori(1, N2 + 1) as n:
                pool.wait_ge(x_turned, n + 1)
                gather(n + 1)
                load_idx(n + 2)
                scatter(n - 1)
                load_row(n)
            pool.wait_ge(x_turned, N2 + 2)
            gather(N2 + 2)
            scatter(N2)
            load_row(N2 + 1)
            scatter(N2 + 1)
            pool.wait_ge(gathered, 16 * (N2 + 3))
            pool.wait_ge(stored, 16 * (N2 + 2))

        @block.scalar
        def _(act):
            def split_h(n, j):
                act.wait_ge(h_loaded[j], 16 * (n + 1))
                if not isinstance(n, int) or n > 0:
                    act.wait_ge(h_used, 4 * (n - 1) + j + 1)
                act.copy(hi_h[j][:], raw_h[j][:]).then_inc(h_hi, 1)

            def split_y(n, j):
                act.wait_ge(y_loaded[j], 16 * (n + 1))
                if not isinstance(n, int) or n > 0:
                    act.wait_ge(y_used, 2 * (n - 1) + j + 1)
                act.copy(hi_y[j][:], raw_y[j][:]).then_inc(y_hi, 1)

            def take_x(n):
                act.wait_ge(x_turned, n + 1)
                if not isinstance(n, int) or n > 0:
                    act.wait_ge(h_used, 4 * n)
                act.copy(xh[:].rearrange("p k n -> p (k n)"), psX).then_inc(x_hi, 1)

            def block_n(n, first, last):
                for j in range(4):
                    if not last:
                        split_h(n + 1, j)
                    if j == 1:
                        if last:
                            act.wait_ge(h_used, 4 * n + 2)
                        act.activation(act1[:], psH[0], ACT.Silu).then_inc(silu_done, 1)
                take_x(n + 1)
                for j in range(2):
                    if not first:
                        act.wait_ge(y_used, 2 * (n - 1) + j + 1)
                        act.wait_ge(stored, 16 * (n - 1))
                        act.copy(y[:, j * CH:(j + 1) * CH], psY[j]).then_inc(y_out, 1)
                    split_y(n, j)
                act.wait_ge(hid_turned, n + 1)
                act.copy(hh[:].rearrange("p k n -> p (k n)"), psHT).then_inc(hid_hi, 1)

            N2 = blocks_less_2(act)
            act.preload_act_table(ACT.Silu)
            take_x(0)
            for j in range(4):
                split_h(0, j)
            block_n(0, True, False)
            with act.Fori(1, N2 + 1) as n:
                block_n(n, False, False)
            block_n(N2 + 1, False, True)
            for j in range(2):
                act.wait_ge(y_used, 2 * (N2 + 1) + j + 1)
                act.wait_ge(stored, 16 * (N2 + 1))
                act.copy(y[:, j * CH:(j + 1) * CH], psY[j]).then_inc(y_out, 1)

        @block.vector
        def _(dve):
            def split_h(n, j):
                dve.wait_ge(h_hi, 4 * n + j + 1)
                dve.tensor_tensor(lo_h[j][:], raw_h[j][:], hi_h[j][:].bitcast(F), ALU.subtract).then_inc(h_lo, 1)

            def split_y(n, j):
                dve.wait_ge(y_hi, 2 * n + j + 1)
                dve.tensor_tensor(lo_y[j][:], raw_y[j][:], hi_y[j][:].bitcast(F), ALU.subtract).then_inc(y_lo, 1)

            def take_x(n):
                dve.wait_ge(x_hi, n + 1)
                dve.tensor_tensor(xl[:].rearrange("p k n -> p (k n)"), psX,
                                  xh[:].rearrange("p k n -> p (k n)").bitcast(F), ALU.subtract).then_inc(x_lo, 1)

            def block_n(n, last):
                for j in range(4):
                    if j == 3:
                        dve.wait_ge(silu_done, n + 1)
                        dve.wait_ge(h_used, 4 * n + 4)
                        dve.tensor_tensor(hid[:], psH[1], act1[:], ALU.mult).then_inc(hid_ready, 1)
                    if not last:
                        split_h(n + 1, j)
                take_x(n + 1)
                for j in range(2):
                    split_y(n, j)
                dve.wait_ge(hid_hi, n + 1)
                dve.tensor_tensor(hl[:].rearrange("p k n -> p (k n)"), psHT,
                                  hh[:].rearrange("p k n -> p (k n)").bitcast(F), ALU.subtract).then_inc(hid_lo, 1)

            N2 = blocks_less_2(dve)
            take_x(0)
            for j in range(4):
                split_h(0, j)
            block_n(0, False)
            with dve.Fori(1, N2 + 1) as n:
                block_n(n, False)
            block_n(N2 + 1, True)

        @block.tensor
        def _(pe):
            def turn_x(n):
                pe.wait_ge(gathered, 16 * (n + 1))
                if not isinstance(n, int) or n > 0:
                    pe.wait_ge(x_lo, n)
                for kt in range(KT):
                    last = pe.transpose(psX[:, kt * P:(kt + 1) * P], xg[:, kt * P:(kt + 1) * P], k.ident[:])
                last.then_inc(x_turned, 1)

            def up(n):
                pe.wait_ge(x_lo, n + 1)
                if not isinstance(n, int) or n > 0:
                    pe.wait_ge(hid_ready, n)
                for j in range(4):
                    pe.wait_ge(h_lo, 4 * n + j + 1)
                    for q in range(HK):
                        kt = (j % 2) * HK + q
                        pe.matmul(psH[j // 2], xh[:, kt, :], hi_h[j][:, q, :], start=(kt == 0), stop=False)
                        pe.matmul(psH[j // 2], xh[:, kt, :], lo_h[j][:, q, :], start=False, stop=False)
                        last = pe.matmul(psH[j // 2], xl[:, kt, :], hi_h[j][:, q, :], start=False, stop=(kt == KT - 1))
                    last.then_inc(h_used, 1)

            def turn_hid(n):
                pe.wait_ge(hid_ready, n + 1)
                for q in range(YK):
                    last = pe.transpose(psHT[:, q * P:(q + 1) * P], hid[:, q * P:(q + 1) * P], k.ident[:])
                last.then_inc(hid_turned, 1)

            def down(n):
                pe.wait_ge(hid_lo, n + 1)
                pe.wait_ge(y_out, 2 * n)
                for j in range(2):
                    pe.wait_ge(y_lo, 2 * n + j + 1)
                    for q in range(YK):
                        pe.matmul(psY[j], hh[:, q, :], hi_y[j][:, q, :], start=(q == 0), stop=False)
                        pe.matmul(psY[j], hh[:, q, :], lo_y[j][:, q, :], start=False, stop=False)
                        last = pe.matmul(psY[j], hl[:, q, :], hi_y[j][:, q, :], start=False, stop=(q == YK - 1))
                    last.then_inc(y_used, 1)

            N2 = blocks_less_2(pe)
            turn_x(0)
            up(0)
            turn_x(1)
            turn_hid(0)
            with pe.Fori(1, N2 + 2) as n:
                up(n)
                turn_x(n + 1)
                down(n - 1)
                turn_hid(n)
            down(N2 + 1)


HA, DQK, DV = 4, 64, 128
LAM_INIT = 0.8 - 0.6


def diff_attention_phase(nc, k, proj, dst, lams, g_sub, rpb):
    TILES = HA * NT
    with ExitStack() as stack:
        s = Scope(nc, "da", stack)
        qk_raw = [s.sb(f"raw{i}", [P, NT, DV]) for i in range(2)]
        v = s.sb("v", [P, NT, DV])
        q_hi, q_lo, k_hi, k_lo = (s.sb(n, [P, SEQ], R) for n in ("q_hi", "q_lo", "k_hi", "k_lo"))
        e = [s.sb(f"e{c}", [P, SEQ]) for c in range(2)]
        w = s.sb("w", [P, SEQ])
        wT = s.sb("wT", [P, SEQ])
        o_all = s.sb("o_all", [P, NT, HA * DV])
        junk = s.sb("junk", [P, DV])
        neg_max = [s.sb(f"neg_max{c}", [P, 1]) for c in range(2)]
        total = [s.sb(f"total{c}", [P, 1]) for c in range(2)]
        inv = [s.sb(f"inv{c}", [P, 1]) for c in range(2)]
        coef = s.sb("coef", [P, 1])
        sq, ms, sd, rs = (s.sb(n, [P, TILES]) for n in ("sq", "ms", "sd", "rs"))
        lam_b = [s.sb(f"lam{i}", [P, DQK]) for i in range(4)]
        dots, edots, neg_lam = s.sb("dots", [P, 2]), s.sb("edots", [P, 2]), s.sb("neg_lam", [P, 1])
        prod = [s.sb(f"prod{i}", [P, DQK]) for i in range(2)]
        gs = s.sb("gs", [P, DV])
        psS = [k.ps[:, 2 * c:2 * c + 2, :].rearrange("p b n -> p (b n)") for c in range(2)]
        psT = [k.ps[:, 4 + i, :] for i in range(2)]
        psO = k.ps[:, 6, 0:DV]

        consts_loaded, loaded = s.sem("consts_loaded"), s.sems("loaded", 3)
        turned, taken, lowered = s.sem("turned"), s.sem("taken"), s.sem("lowered")
        scored, maxed, exped, inverted = (s.sems(n, 2) for n in ("scored", "maxed", "exped", "inverted"))
        coef_done, w_ready, w_turned, wT_ready, pv_done, o_out, sq_done = (s.sem(n) for n in (
            "coef_done", "w_ready", "w_turned", "wT_ready", "pv_done", "o_out", "sq_done"))
        did, dots_done, edots_done, ms_done, sd_done, final, stored = (s.sem(n) for n in (
            "did", "dots_done", "edots_done", "ms_done", "sd_done", "final", "stored"))
        cleared, bias_laid, squared = s.sem("cleared"), s.pool_sem("bias_laid"), s.sem("squared")
        bias = s.sb("bias", [P, PAIRS, OFFS, GRID])
        rpb_sb = s.sb("rpb", [HB, OFFS * (2 * WIN_C - 1)])
        block = s.block()

        @block.sync
        def _(sp):
            for to, row in list(zip(lam_b, lams)):
                sp.dma_start(to[:], row_to_all(row, DQK)).then_inc(consts_loaded, 16)
            sp.dma_start(gs[:], row_to_all(g_sub, DV)).then_inc(consts_loaded, 16)

            def load(i, first):
                sp.dma_start((qk_raw[0], qk_raw[1], v)[i][:], proj[:, bass.ds(first[i], DV)].rearrange("(t p) d -> p t d", p=P)
                             ).then_inc(loaded[i], 16)

            for i in range(3):
                load(i, [c * HA * DV for c in range(3)])
            with sp.Fori(1, HA) as h:
                first = [sp.snap(i * HA * DV + h * DV) for i in range(3)]
                sp.wait_ge(turned, 4 * h)
                load(0, first)
                load(1, first)
                sp.wait_ge(pv_done, NT * h)
                load(2, first)
            for t in range(NT):
                sp.wait_ge(final, HA * (t + 1))
                sp.dma_start(dst[t * P:(t + 1) * P, 0:HA * DV], o_all[:, t, :]).then_inc(stored, 16)
            sp.wait_ge(stored, 16 * NT)

        @block.gpsimd
        def _(pool):
            lay_bias(pool, k, bias, rpb_sb, rpb, cleared, bias_laid)

        @block.tensor
        def _(pe):
            def score(i, t):
                for c in range(2):
                    half = slice(c * DQK, (c + 1) * DQK)
                    if not isinstance(i, int) or i > 0:
                        pe.wait_ge(exped[c], i)
                    for n in range(2):
                        for i_pass, (q, kk) in enumerate(((q_hi, k_hi), (q_lo, k_hi), (q_hi, k_lo))):
                            last = pe.matmul(psS[c][:, n * CH:(n + 1) * CH], q[half, t * P:(t + 1) * P],
                                             kk[half, n * CH:(n + 1) * CH], start=(i_pass == 0), stop=(i_pass == 2))
                    last.then_inc(scored[c], 1)

            with pe.Fori(0, HA) as h:
                for i in range(2):
                    pe.wait_ge(loaded[i], 16 * (h + 1))
                    for b in range(2):
                        pe.wait_ge(wT_ready, 2 * NT * h)
                        pe.wait_ge(lowered, 4 * h + 2 * i)
                        for q in range(4):
                            last = pe.transpose(psT[b][:, q * P:(q + 1) * P], qk_raw[i][:, 4 * b + q, :], k.ident[:])
                        last.then_inc(turned, 1)
                pe.wait_ge(lowered, 4 * h + 4)
                pe.wait_ge(loaded[2], 16 * (h + 1))
                score(NT * h, 0)
                for t in range(NT):
                    i = NT * h + t
                    if t + 1 < NT:
                        score(i + 1, t + 1)
                    pe.wait_ge(w_ready, i + 1)
                    for b in range(2):
                        for q in range(4):
                            kt = 4 * b + q
                            last = pe.transpose(psT[b][:, q * P:(q + 1) * P], w[:, kt * P:(kt + 1) * P], k.ident[:])
                        last.then_inc(w_turned, 1)
                    pe.wait_ge(o_out, i)
                    for b in range(2):
                        pe.wait_ge(wT_ready, 2 * i + b + 1)
                        for q in range(4):
                            kt = 4 * b + q
                            last = pe.matmul(psO, wT[:, kt * P:(kt + 1) * P], v[:, kt, :], start=(kt == 0), stop=(kt == NT - 1))
                    last.then_inc(pv_done, 1)

        @block.scalar
        def _(act):
            def exps(i, c):
                act.wait_ge(maxed[c], i + 1)
                if not isinstance(i, int) or i > 0:
                    act.wait_ge(w_ready, i)
                act.activation(e[c][:], psS[c], ACT.Exp, bias=neg_max[c][:], accum_out=total[c][:]).then_inc(exped[c], 1)

            def take_turned(i):
                for b in range(2):
                    act.wait_ge(w_turned, 2 * i + b + 1)
                    if b == 0 and (not isinstance(i, int) or i > 0):
                        act.wait_ge(pv_done, i)
                    act.copy(wT[:, b * CH:(b + 1) * CH], psT[b]).then_inc(wT_ready, 1)

            def take_rows(i, h, t):
                act.wait_ge(pv_done, i + 1)
                act.wait_ge(inverted[0], i + 1)
                act.activation(o_all[:, bass.ds(t, 1), bass.ds(h * DV, DV)], psO, ACT.Copy, scale=inv[0][:]).then_inc(o_out, 1)

            act.preload_act_table(ACT.Exp)
            act.wait_ge(dots_done, 2)
            act.activation(edots[:], dots[:], ACT.Exp).then_inc(edots_done, 1)
            with act.Fori(0, HA) as h:
                for g in range(4):
                    act.wait_ge(turned, 4 * h + g + 1)
                    to = (q_hi, k_hi)[g // 2][:, (g % 2) * CH:(g % 2 + 1) * CH]
                    act.activation(to, psT[g % 2], ACT.Copy, scale=DQK ** -0.5 if g < 2 else 1.0).then_inc(taken, 1)
                i0 = act.snap(NT * h)
                for c in range(2):
                    exps(i0, c)
                with act.Fori(0, NT - 1) as t:
                    i = i0 + t
                    take_turned(i)
                    exps(i + 1, 0)
                    exps(i + 1, 1)
                    take_rows(i, h, t)
                take_turned(i0 + NT - 1)
                take_rows(i0 + NT - 1, h, NT - 1)
            act.preload_act_table(ACT.Sqrt)
            act.wait_ge(ms_done, 1)
            act.activation(sd[:], ms[:], ACT.Sqrt).then_inc(sd_done, 1)

        @block.vector
        def _(dve):
            n = [0]

            def link(ins):
                n[0] += 1
                ins.then_inc(did, 1)
                dve.wait_ge(did, n[0])

            dve.wait_ge(consts_loaded, 16 * 5)
            for i in range(2):
                link(dve.tensor_tensor(prod[i][:], lam_b[2 * i][:], lam_b[2 * i + 1][:], ALU.mult))
                dve.tensor_reduce(dots[:, i:i + 1], prod[i][:], X, ALU.add).then_inc(dots_done, 1)
            link(dve.tensor_scalar(gs[:], gs[:], 1.0 - LAM_INIT, None, ALU.mult))
            dve.wait_ge(edots_done, 1)
            link(dve.tensor_tensor(neg_lam[:], edots[:, 1:2], edots[:, 0:1], ALU.subtract))
            link(dve.tensor_scalar(neg_lam[:], neg_lam[:], -LAM_INIT, None, ALU.add))

            def maxima(i):
                for c in range(2):
                    dve.wait_ge(scored[c], i + 1)
                    if not isinstance(i, int) or i > 0:
                        dve.wait_ge(exped[c], i)
                    dve.tensor_reduce(neg_max[c][:], psS[c], X, ALU.max, negate=True).then_inc(maxed[c], 1)

            def combine(i):
                dve.wait_ge(exped[1], i + 1)
                dve.wait_ge(exped[0], i + 1)
                if not isinstance(i, int) or i > 0:
                    dve.wait_ge(w_turned, 2 * i)
                dve.reciprocal(inv[1][:], total[1][:]).then_inc(inverted[1], 1)
                dve.wait_ge(inverted[1], i + 1)
                dve.scalar_tensor_tensor(out=coef[:], in0=inv[1][:], scalar=total[0][:], in1=neg_lam[:],
                                         op0=ALU.mult, op1=ALU.mult).then_inc(coef_done, 1)
                dve.wait_ge(coef_done, i + 1)
                dve.scalar_tensor_tensor(out=w[:], in0=e[1][:], scalar=coef[:], in1=e[0][:],
                                         op0=ALU.mult, op1=ALU.add).then_inc(w_ready, 1)

            def invert(i):
                if not isinstance(i, int) or i > 0:
                    dve.wait_ge(o_out, i)
                dve.reciprocal(inv[0][:], total[0][:]).then_inc(inverted[0], 1)

            def squares(i, h, t):
                dve.wait_ge(o_out, i + 1)
                if not isinstance(i, int) or i > 0:
                    dve.wait_ge(sq_done, i)
                o = o_all[:, bass.ds(t, 1), bass.ds(h * DV, DV)].rearrange("p o d -> p (o d)")
                dve.tensor_tensor(junk[:], o, o, ALU.mult).then_inc(squared, 1)
                dve.wait_ge(squared, i + 1)
                dve.tensor_reduce(sq[:, bass.ds(i, 1)], junk[:], X, ALU.add).then_inc(sq_done, 1)

            with dve.Fori(0, HA) as h:
                i0 = dve.snap(NT * h)
                for g in range(4):
                    dve.wait_ge(taken, 4 * h + g + 1)
                    cols = slice((g % 2) * CH, (g % 2 + 1) * CH)
                    dve.scalar_tensor_tensor(out=(q_lo, k_lo)[g // 2][:, cols], in0=psT[g % 2],
                                             scalar=DQK ** -0.5 if g < 2 else 1.0,
                                             in1=(q_hi, k_hi)[g // 2][:, cols].bitcast(F),
                                             op0=ALU.mult, op1=ALU.subtract).then_inc(lowered, 1)
                maxima(i0)
                combine(i0)
                invert(i0)
                with dve.Fori(0, NT - 1) as t:
                    i = i0 + t
                    maxima(i + 1)
                    combine(i + 1)
                    squares(i, h, t)
                    invert(i + 1)
                squares(i0 + NT - 1, h, NT - 1)
            dve.wait_ge(sq_done, TILES)
            dve.tensor_scalar(ms[:], sq[:], 1.0 / DV, EPS, ALU.mult, ALU.add).then_inc(ms_done, 1)
            dve.wait_ge(sd_done, 1)
            link(dve.reciprocal(rs[:], sd[:]))
            for t in range(NT):
                for h in range(HA):
                    o = o_all[:, t, h * DV:(h + 1) * DV]
                    i = NT * h + t
                    dve.scalar_tensor_tensor(out=o, in0=o, scalar=rs[:, i:i + 1], in1=gs[:],
                                             op0=ALU.mult, op1=ALU.mult).then_inc(final, 1)


HB, DB_H, GRID, ROWS, WIN_R, WIN_C = 16, 32, 64, 16, 8, 16
OFFS = 2 * WIN_R - 1
PAIRS = HB // 2
QUADS = HB // 4


def lay_bias(pool, k, bias, rpb_sb, rpb, cleared, laid):
    pool.memset(bias[:], BIG).then_inc(cleared, 1)
    pool.dma_start(rpb_sb[:], rpb.rearrange("h r w -> h (r w)")).then_inc(laid, 16)
    pool.wait_ge(laid, 16)
    pool.tensor_scalar(rpb_sb[:], rpb_sb[:], -1.0, None, ALU.mult).then_inc(cleared, 1)
    pool.wait_ge(cleared, 2)
    pool.dma_start(k.neg_rpb.rearrange("h r w -> h (r w)"), rpb_sb[:]).then_inc(laid, 16)
    pool.wait_ge(laid, 32)
    pool.dma_start(k.bias_rows, bias[:]).then_inc(laid, 16)
    pool.wait_ge(laid, 48)
    src = k.neg_rpb.rearrange("(p h) r w -> h p r w", h=2)

    def one(c, first, off):
        for h in range(2):
            pool.dma_start(k.bias_rows[bass.ds(c + h * GRID, 1), :, :, bass.ds(first, WIN_C)],
                           src[h:h + 1, :, :, bass.ds(off, WIN_C)]).then_inc(laid, 16)

    half = WIN_C // 2
    last = GRID - WIN_C
    with pool.Fori(0, half) as c:
        one(c, 0, WIN_C - 1 - c)
    with pool.Fori(half, last + half) as c:
        one(c, c - half, half - 1)
    with pool.Fori(last + half, GRID) as c:
        one(c, last, last - c + WIN_C - 1)
    pool.wait_ge(laid, 16 * (2 * GRID + 3))


def neighbourhood_phase(nc, k, proj, dst, consts):
    Q0, K0, V0, O0 = 3 * 512, 4 * 512, 5 * 512, 512
    QC = 4 * DB_H
    with ExitStack() as stack:
        s = Scope(nc, "na", stack)
        bias = s.sb("bias", [P, 2, OFFS, GRID])
        raw = [s.sb(f"raw{i}", [P, NT, QC]) for i in range(2)]
        v_even = s.sb("v_even", [P, NT, QC])
        v_odd = s.sb("v_odd", [P, NT - 1, QC])
        q_hi, q_lo = (s.sb(n, [P, ROWS, 4, GRID], R) for n in ("q_hi", "q_lo"))
        k_hi, k_lo = s.sb("k_hi", [P, SEQ], R), s.sb("k_lo", [P, SEQ], R)
        sc = [[s.sb(f"sc{a}{b}", [P, CH]) for b in range(2)] for a in range(2)]
        e = [[s.sb(f"e{a}{b}", [P, CH]) for b in range(2)] for a in range(2)]
        eT = [s.sb(f"eT{b}", [P, CH]) for b in range(2)]
        neg_max = [[s.sb(f"neg_max{a}{b}", [P, 1]) for b in range(2)] for a in range(2)]
        total = [s.sb(f"total{a}", [P, 2]) for a in range(2)]
        inv = [s.sb(f"inv{a}", [P, 2]) for a in range(2)]
        o1 = [s.sb(f"o1{a}", [P, QC]) for a in range(2)]
        o2 = [s.sb(f"o2{a}", [P, QC]) for a in range(2)]
        own = s.sb("own", [P, QC])
        fold = s.sb("fold", [P, GRID])
        rows = s.sb("rows", [P, NT, QC])
        spare = s.sb("spare", [P, 3])
        psS = [[k.ps[:, 2 * a + b, :] for b in range(2)] for a in range(2)]
        psT = [k.ps[:, 4 + b, :] for b in range(2)]
        psO = [k.ps[:, 6, a * QC:(a + 1) * QC] for a in range(2)]
        psR = k.ps[:, 7, 0:QC]

        consts_loaded, loaded, stored = s.sem("consts_loaded"), s.sems("loaded", 4), s.sem("stored")
        spared, lowered = s.sem("spared"), s.sem("lowered")
        cleared, turned, taken, bias_loaded = (s.sem(n) for n in ("cleared", "turned", "taken", "bias_loaded"))
        scored, biased, exped, e_turned, eT_ready = (s.sem(n) for n in ("scored", "biased", "exped", "e_turned", "eT_ready"))
        multiplied, inverted, scaled, masked, folded, row_out = (s.sem(n) for n in (
            "multiplied", "inverted", "scaled", "masked", "folded", "row_out"))
        block = s.block()

        def first_row(r):
            return min(max(r - WIN_R // 2, 0), ROWS - WIN_R)

        @block.sync
        def _(sp):
            sp.dma_start(own[:], consts[:, 0:QC]).then_inc(consts_loaded, 16)
            sp.dma_start(fold[:], consts[:, QC:QC + GRID]).then_inc(consts_loaded, 16)

            def load_qk(first):
                for i in range(2):
                    sp.dma_start(raw[i][:], proj[:, bass.ds(first[i], QC)].rearrange("(t p) d -> p t d", p=P)).then_inc(loaded[i], 16)

            def load_bias(pair):
                sp.dma_start(bias[:], k.bias_rows[:, bass.ds(pair, 2), :, :]).then_inc(bias_loaded, 16)

            def load_v(first):
                sp.dma_start(v_even[:], proj[:, bass.ds(first[2], QC)].rearrange("(t p) d -> p t d", p=P)).then_inc(loaded[2], 16)
                sp.dma_start(v_odd[:], proj[GRID:SEQ - GRID, bass.ds(first[2], QC)].rearrange("(t p) d -> p t d", p=P)
                             ).then_inc(loaded[3], 16)

            def store(col):
                sp.dma_start(dst[:, bass.ds(col, QC)].rearrange("(t p) d -> p t d", p=P), rows[:]).then_inc(stored, 16)

            load_qk([Q0, K0, V0])
            load_bias(0)
            load_v([Q0, K0, V0])
            with sp.Fori(1, QUADS) as q:
                first = [sp.snap(c0 + q * QC) for c0 in (Q0, K0, V0)]
                pair, col = sp.snap(2 * q), sp.snap(O0 + q * QC - QC)
                sp.wait_ge(turned, 4 * q)
                load_qk(first)
                sp.wait_ge(biased, 2 * ROWS * q)
                load_bias(pair)
                sp.wait_ge(multiplied, ROWS * q)
                load_v(first)
                sp.wait_ge(row_out, ROWS * q)
                store(col)
            sp.wait_ge(row_out, ROWS * QUADS)
            store(O0 + (QUADS - 1) * QC)
            sp.wait_ge(stored, 16 * QUADS)

        @block.gpsimd
        def _(pool):
            pool.memset(q_hi[:].bitcast(F), 0.0).then_inc(cleared, 1)

        @block.tensor
        def _(pe):
            def score(g, r):
                a = r % 2
                if r >= 2:
                    pe.wait_ge(biased, 2 * (g - 1))
                else:
                    pe.wait_ge(biased, 2 * (g - r))
                for b in range(2):
                    for i_pass, (qq, kk) in enumerate(((q_hi, k_hi), (q_lo, k_hi), (q_hi, k_lo))):
                        last = pe.matmul(psS[a][b], qq[:, r, 2 * b:2 * b + 2, :].rearrange("p h c -> p (h c)"),
                                         kk[:, first_row(r) * GRID:first_row(r) * GRID + CH],
                                         start=(i_pass == 0), stop=(i_pass == 2))
                last.then_inc(scored, 1)

            pe.wait_ge(consts_loaded, 32)
            with pe.Fori(0, QUADS) as q:
                for i in range(2):
                    pe.wait_ge(loaded[i], 16 * (q + 1))
                    for b in range(2):
                        pe.wait_ge(eT_ready, 2 * ROWS * q)
                        pe.wait_ge(lowered, 4 * q + 2 * i)
                        for n in range(4):
                            last = pe.transpose(psT[b][:, n * P:(n + 1) * P], raw[i][:, 4 * b + n, :], k.ident[:])
                        last.then_inc(turned, 1)
                pe.wait_ge(lowered, 4 * q + 4)
                pe.wait_ge(loaded[2], 16 * (q + 1))
                pe.wait_ge(loaded[3], 16 * (q + 1))
                g0 = pe.snap(ROWS * q)
                score(g0, 0)
                score(g0 + 1, 1)
                for r in range(ROWS):
                    g, a = g0 + r, r % 2
                    for b in range(2):
                        pe.wait_ge(exped, 2 * g + b + 1)
                        for n in range(4):
                            last = pe.transpose(psT[b][:, n * P:(n + 1) * P], e[a][b][:, n * P:(n + 1) * P], k.ident[:])
                        last.then_inc(e_turned, 1)
                    if r + 2 < ROWS:
                        score(g + 2, r + 2)
                    if r >= 1:
                        pe.wait_ge(masked, g)
                        pe.wait_ge(row_out, g - 1)
                        half = slice(((r - 1) % 2) * GRID, ((r - 1) % 2 + 1) * GRID)
                        pe.matmul(psR[half, :], fold[:], o2[1 - a][:], start=True, stop=True).then_inc(folded, 1)
                    for b in range(2):
                        pe.wait_ge(eT_ready, 2 * g + b + 1)
                        for n in range(4):
                            row = first_row(r) + 2 * n
                            vv = (v_even if row % 2 == 0 else v_odd)[:, row // 2, b * 2 * DB_H:(b + 1) * 2 * DB_H]
                            last = pe.matmul(psO[a][:, b * 2 * DB_H:(b + 1) * 2 * DB_H], eT[b][:, n * P:(n + 1) * P], vv,
                                             start=(n == 0), stop=(n == 3))
                    last.then_inc(multiplied, 1)
                pe.wait_ge(masked, g0 + ROWS)
                pe.wait_ge(row_out, g0 + ROWS - 1)
                pe.matmul(psR[GRID:2 * GRID, :], fold[:], o2[1][:], start=True, stop=True).then_inc(folded, 1)

        @block.scalar
        def _(act):
            act.preload_act_table(ACT.Exp)
            with act.Fori(0, QUADS) as q:
                g0 = act.snap(ROWS * q)
                for b in range(2):
                    act.wait_ge(turned, 4 * q + b + 1)
                    if b == 0:
                        act.wait_ge(cleared, 2)
                    for h in range(4):
                        part = slice(h * DB_H, (h + 1) * DB_H)
                        last = act.activation(q_hi[part, 8 * b:8 * b + 8, h, :], psT[b][part, :].rearrange("p (r c) -> p r c", c=GRID),
                                              ACT.Copy, scale=-(DB_H ** -0.5))
                    last.then_inc(taken, 1)
                for b in range(2):
                    act.wait_ge(turned, 4 * q + b + 3)
                    act.copy(k_hi[:, b * CH:(b + 1) * CH], psT[b]).then_inc(taken, 1)

                def exps(g, a, before):
                    act.wait_ge(inverted, before)
                    for b in range(2):
                        act.wait_ge(biased, 2 * g + b + 1)
                        act.activation(e[a][b][:], sc[a][b][:], ACT.Exp, scale=-1.0, bias=neg_max[a][b][:],
                                       accum_out=total[a][:, b:b + 1]).then_inc(exped, 1)

                def take(g):
                    act.wait_ge(e_turned, 2 * g + 1)
                    act.wait_ge(multiplied, g)
                    act.copy(eT[0][:], psT[0]).then_inc(eT_ready, 1)

                exps(g0, 0, g0)
                with act.Fori(0, ROWS // 2 - 1) as j:
                    for a in range(2):
                        g = g0 + 2 * j + a
                        take(g)
                        exps(g + 1, 1 - a, g)
                take(g0 + ROWS - 2)
                exps(g0 + ROWS - 1, 1, g0 + ROWS - 2)
                take(g0 + ROWS - 1)

        @block.vector
        def _(dve):
            def add_bias(g, a, off):
                for b in range(2):
                    nb = bias[:, b, off:off + WIN_R, :].rearrange("p r c -> p (r c)")
                    dve.tensor_tensor_reduce(sc[a][b][:], psS[a][b], nb, 1.0, BIG, ALU.add, ALU.min,
                                             neg_max[a][b][:]).then_inc(biased, 1)

            def take(g):
                dve.wait_ge(e_turned, 2 * g + 2)
                dve.wait_ge(eT_ready, 2 * g + 1)
                dve.tensor_copy(eT[1][:], psT[1]).then_inc(eT_ready, 1)

            def rows_of(g, a):
                dve.wait_ge(exped, 2 * g + 2)
                dve.reciprocal(inv[a][:], total[a][:]).then_inc(inverted, 1)
                dve.wait_ge(inverted, g + 1)
                dve.wait_ge(multiplied, g + 1)
                dve.tensor_tensor(o1[a][:].rearrange("p (b c) -> p b c", b=2), psO[a].rearrange("p (b c) -> p b c", b=2),
                                  inv[a][:].rearrange("p (b o) -> p b o", o=1).to_broadcast([P, 2, 2 * DB_H]),
                                  ALU.mult).then_inc(scaled, 1)
                dve.wait_ge(scaled, g + 1)
                dve.tensor_tensor(o2[a][:], o1[a][:], own[:], ALU.mult).then_inc(masked, 1)

            def clear_spare(col):
                dve.memset(spare[:, col:col + 1], 0.0).then_inc(spared, 1)

            def out_of(g, t, a):
                dve.wait_ge(folded, g + 1)
                half = slice(a * GRID, (a + 1) * GRID)
                dve.tensor_copy(rows[half, t, :], psR[half, :]).then_inc(row_out, 1)

            dve.memset(q_lo[:].bitcast(F), 0.0).then_inc(cleared, 1)
            dve.wait_ge(consts_loaded, 32)
            with dve.Fori(0, QUADS) as q:
                g0 = dve.snap(ROWS * q)
                for b in range(2):
                    dve.wait_ge(taken, 4 * q + b + 1)
                    for h in range(4):
                        part = slice(h * DB_H, (h + 1) * DB_H)
                        last = dve.scalar_tensor_tensor(out=q_lo[part, 8 * b:8 * b + 8, h, :], in0=psT[b][part, :].rearrange("p (r c) -> p r c", c=GRID),
                                                        scalar=-(DB_H ** -0.5), in1=q_hi[part, 8 * b:8 * b + 8, h, :].bitcast(F),
                                                        op0=ALU.mult, op1=ALU.subtract)
                    last.then_inc(lowered, 1)
                for b in range(2):
                    dve.wait_ge(taken, 4 * q + b + 3)
                    cols = slice(b * CH, (b + 1) * CH)
                    dve.tensor_tensor(k_lo[:, cols], psT[b], k_hi[:, cols].bitcast(F), ALU.subtract).then_inc(lowered, 1)
                dve.wait_ge(bias_loaded, 16 * (q + 1))

                def off(r):
                    return first_row(r) - r + WIN_R - 1

                dve.wait_ge(spared, 3 * q)
                dve.wait_ge(scored, g0 + 1)
                clear_spare(0)
                add_bias(g0, 0, off(0))
                dve.wait_ge(scored, g0 + 2)
                clear_spare(1)
                add_bias(g0 + 1, 1, off(1))
                dve.wait_ge(stored, 16 * q)
                for r in range(ROWS):
                    g, a = g0 + r, r % 2
                    take(g)
                    if r + 2 < ROWS:
                        dve.wait_ge(scored, g + 3)
                    if r >= 1:
                        out_of(g - 1, (r - 1) // 2, 1 - a)
                    else:
                        clear_spare(2)
                    if r + 2 < ROWS:
                        add_bias(g + 2, a, off(r + 2))
                    rows_of(g, a)
                out_of(g0 + ROWS - 1, NT - 1, 1)


D_PLE, LAYERS = 256, 2


def between_phase(nc, k, src, dst, p_src, w_ple, g_ple, ple, c, w_ada, b_ada, norm_g, mod):
    KP, N = D_PLE // P, 3 * DM
    NB = N // CH
    PER_LAYER = NT // LAYERS
    with ExitStack() as stack:
        s = Scope(nc, "bt", stack)
        h, mid, out = ([s.sb(f"{n}{p}", [P, DM]) for p in range(2)] for n in ("h", "mid", "out"))
        expert = [[s.sb(f"expert{i}{p}", [P, DM]) for p in range(2)] for i in range(TOP_K)]
        h_loaded, h_stored, expert_loaded = s.sems("h_loaded", 2), s.sems("h_stored", 2), s.pool_sems("expert_loaded", 2)
        mid_done, out_ready = s.sem("mid_done"), s.sem("out_ready")
        x, xT = ([s.sb(f"{n}{p}", [P, D_PLE]) for p in range(2)] for n in ("x", "xT"))
        prod, factor = ([s.sb(f"{n}{p}", [P, DM]) for p in range(2)] for n in ("prod", "factor"))
        w_sb, gain_b, junk = s.sb("w", [P, KP, DM]), s.sb("gain", [P, DM]), s.sb("junk", [P, DM], BF)
        ss, ms, sd, rs = (s.sb(n, [P, NT]) for n in ("ss", "ms", "sd", "rs"))
        psT, psY = k.ps[:, 6, 0:D_PLE], k.ps[:, 7, :]
        x_loaded, w_loaded, factor_stored = s.pool_sems("x_loaded", 2), s.sem("w_loaded"), s.sems("factor_stored", 2)
        turned, taken, product, prod_out, squared, meaned, rooted, inverted, factor_ready = (s.sem(n) for n in (
            "turned", "taken", "product", "prod_out", "squared", "meaned", "rooted", "inverted", "factor_ready"))
        wb = [s.sb(f"w_ada{i}", [P, N]) for i in range(4)]
        c_raw, c_act = s.sb("c_raw", [P, KT]), s.sb("c_act", [P, KT])
        bias, row = s.sb("bias", [1, LAYERS, N]), s.sb("row", [1, LAYERS, N])
        g, gained = s.sb("g", [1, LAYERS, DM]), s.sb("gained", [1, LAYERS, DM])
        psM = k.ps[0:1, 0:NB, :].rearrange("p b n -> p (b n)")
        ada_loaded, ada_consts_loaded, c_loaded, c_done = s.sems("ada_loaded", 4), s.sem("ada_consts_loaded"), s.sem("c_loaded"), s.sem("c_done")
        used, rows_done, gain_done, mod_stored = (s.sem(n) for n in ("used", "rows_done", "gain_done", "mod_stored"))
        block = s.block()

        @block.sync
        def _(sp):
            sp.dma_start(c_raw[:], c.rearrange("(k p) -> p k", p=P), allow_slow_non_contiguous=True).then_inc(c_loaded, 16)
            for i in range(LAYERS * KT):
                if i >= 4:
                    sp.wait_ge(used, i - 3)
                sp.dma_start(wb[i % 4][:], w_ada[i * P:(i + 1) * P, :]).then_inc(ada_loaded[i % 4], 16)
                if i == 0:
                    sp.dma_start(w_sb[:], w_ple.rearrange("(k p) n -> p k n", p=P)).then_inc(w_loaded, 16)
                    sp.dma_start(gain_b[:], row_to_all(g_ple, DM)).then_inc(w_loaded, 16)
                if i == 3:
                    sp.dma_start(bias[:], b_ada.rearrange("(o l) n -> o l n", o=1)).then_inc(ada_consts_loaded, 16)
                    sp.dma_start(g[:], norm_g.rearrange("(o l) n -> o l n", o=1)).then_inc(ada_consts_loaded, 16)
                if i % 2 == 0:
                    t = i // 2
                    if t >= 2:
                        sp.wait_ge(out_ready, t - 1)
                    sp.dma_start(h[t % 2][:], src[t * P:(t + 1) * P, :]).then_inc(h_loaded[t % 2], 16)
            for l in range(LAYERS):
                sp.wait_ge(gain_done, l + 1)
                sp.dma_start(mod[l, 0:1, :], row[:, l, 0:DM]).then_inc(mod_stored, 16)
                sp.dma_start(mod[l, 1:2, :], gained[:, l, :]).then_inc(mod_stored, 16)
                sp.dma_start(mod[l, 2:3, :], row[:, l, 2 * DM:]).then_inc(mod_stored, 16)
            sp.wait_ge(mod_stored, 16 * 3 * LAYERS)

        @block.gpsimd
        def _(pool):
            for t in range(NT):
                p = t % 2
                if t >= 2:
                    pool.wait_ge(turned, t - 1)
                pool.dma_start(x[p][:], p_src[t * P:(t + 1) * P, :]).then_inc(x_loaded[p], 16)
                if t >= 2:
                    pool.wait_ge(out_ready, t - 1)
                for i in range(TOP_K):
                    pool.dma_start(expert[i][p][:], k.slot_y[i * SEQ + t * P:i * SEQ + (t + 1) * P, :]).then_inc(expert_loaded[p], 16)

        @block.tensor
        def _(pe):
            pe.wait_ge(c_done, 1)
            with pe.Fori(0, LAYERS) as l:
                for kt in range(KT):
                    i, half = kt // 2, kt % 2
                    t, p = PER_LAYER * l + i, i % 2
                    if half == 0:
                        pe.wait_ge(x_loaded[p], 16 * (2 * l + i // 2 + 1))
                        pe.wait_ge(taken, t)
                        for q in range(KP):
                            last = pe.transpose(psT[:, q * P:(q + 1) * P], x[p][:, q * P:(q + 1) * P], k.ident[:])
                        last.then_inc(turned, 1)
                    pe.wait_ge(ada_loaded[kt % 4], 16 * (2 * l + kt // 4 + 1))
                    if kt == 0:
                        pe.wait_ge(rows_done, l)
                    for n in range(NB):
                        last = pe.matmul(psM[:, n * CH:(n + 1) * CH], c_act[:, kt:kt + 1], wb[kt % 4][:, n * CH:(n + 1) * CH],
                                         start=(kt == 0), stop=(kt == KT - 1))
                    last.then_inc(used, 1)
                    if kt == 0:
                        pe.wait_ge(w_loaded, 32)
                    if half == 0:
                        pe.wait_ge(taken, t + 1)
                    pe.wait_ge(prod_out, 2 * t + half)
                    for q in range(KP):
                        last = pe.matmul(psY, xT[p][:, q * P:(q + 1) * P], w_sb[:, q, half * CH:(half + 1) * CH],
                                         start=(q == 0), stop=(q == KP - 1))
                    last.then_inc(product, 1)

        @block.scalar
        def _(act):
            act.preload_act_table(ACT.Silu)
            act.wait_ge(c_loaded, 16)
            act.activation(c_act[:], c_raw[:], ACT.Silu).then_inc(c_done, 1)
            act.preload_act_table(ACT.Sqrt)
            with act.Fori(0, NT // 2) as j:
                for p in range(2):
                    t = 2 * j + p
                    act.wait_ge(turned, t + 1)
                    act.copy(xT[p][:], psT).then_inc(taken, 1)
                    act.wait_ge(factor_ready, 2 * j)
                    for half in range(2):
                        act.wait_ge(product, 2 * t + half + 1)
                        act.copy(prod[p][:, half * CH:(half + 1) * CH], psY).then_inc(prod_out, 1)
                    act.wait_ge(prod_out, 2 * t + 2)
                    act.activation(junk[:], prod[p][:], ACT.Square, accum_out=ss[:, bass.ds(t, 1)]).then_inc(squared, 1)
                    act.wait_ge(meaned, t + 1)
                    act.activation(sd[:, bass.ds(t, 1)], ms[:, bass.ds(t, 1)], ACT.Sqrt).then_inc(rooted, 1)
                    act.wait_ge(factor_ready, t + 1)
                    act.dma_start(ple[bass.ds(t * P, P), :], factor[p][:]).then_inc(factor_stored[p], 16)
                    act.wait_ge(out_ready, t + 1)
                    act.dma_start(dst[bass.ds(t * P, P), :], out[p][:]).then_inc(h_stored[p], 16)
            for p in range(2):
                act.wait_ge(factor_stored[p], 16 * NT // 2)
                act.wait_ge(h_stored[p], 16 * NT // 2)

        @block.vector
        def _(dve):
            dve.wait_ge(w_loaded, 32)
            with dve.Fori(0, LAYERS) as l:
                for i in range(PER_LAYER):
                    t, p = PER_LAYER * l + i, i % 2
                    one, before = bass.ds(t, 1), 2 * l + i // 2
                    dve.wait_ge(h_loaded[p], 16 * (before + 1))
                    dve.wait_ge(expert_loaded[p], 32 * (before + 1))
                    dve.wait_ge(out_ready, t)
                    dve.scalar_tensor_tensor(out=mid[p][:], in0=expert[0][p][:], scalar=k.slot_w[:, 0, one], in1=h[p][:],
                                             op0=ALU.mult, op1=ALU.add).then_inc(mid_done, 1)
                    dve.wait_ge(mid_done, t + 1)
                    dve.wait_ge(h_stored[p], 16 * before)
                    dve.scalar_tensor_tensor(out=out[p][:], in0=expert[1][p][:], scalar=k.slot_w[:, 1, one], in1=mid[p][:],
                                             op0=ALU.mult, op1=ALU.add).then_inc(out_ready, 1)
                    dve.wait_ge(squared, t + 1)
                    dve.tensor_scalar(ms[:, one], ss[:, one], 1.0 / DM, EPS, ALU.mult, ALU.add).then_inc(meaned, 1)
                    dve.wait_ge(rooted, t + 1)
                    dve.reciprocal(rs[:, one], sd[:, one]).then_inc(inverted, 1)
                    dve.wait_ge(inverted, t + 1)
                    dve.wait_ge(factor_stored[p], 16 * before)
                    dve.scalar_tensor_tensor(out=factor[p][:], in0=prod[p][:], scalar=rs[:, one], in1=gain_b[:],
                                             op0=ALU.mult, op1=ALU.mult).then_inc(factor_ready, 1)
                layer = bass.ds(l, 1)
                dve.wait_ge(ada_consts_loaded, 32)
                dve.wait_ge(used, KT * (l + 1))
                dve.tensor_tensor(row[:, layer, :].rearrange("p o n -> p (o n)"), psM,
                                  bias[:, layer, :].rearrange("p o n -> p (o n)"), ALU.add).then_inc(rows_done, 1)
                dve.wait_ge(rows_done, l + 1)
                dve.scalar_tensor_tensor(out=gained[:, layer, :], in0=row[:, layer, DM:2 * DM], scalar=1.0, in1=g[:, layer, :],
                                         op0=ALU.add, op1=ALU.mult).then_inc(gain_done, 1)


HR, DR = 4, 128


def retention_phase(nc, k, tag, proj, dst, decay, q_decay, k_decay, tile_decay):
    RET = HR * DR
    with ExitStack() as stack:
        s = Scope(nc, tag, stack)
        raw = [s.sb(f"raw{i}", [P, NT, DR]) for i in range(2)]
        v, g = s.sb("v", [P, NT, RET]), s.sb("g", [P, NT, RET])
        qT, kT, qTd = (s.sb(n, [P, SEQ]) for n in ("qT", "kT", "qTd"))
        kd = s.sb("kd", [P, NT, DR])
        sm = s.sb("sm", [P, SEQ])
        state = s.sb("state", [P, NT, DR])
        cen, sq, nrm = (s.sb(n, [P, NT, DR]) for n in ("cen", "sq", "nrm"))
        sums, mu, var_sum, ms, sd, rs = (s.sb(n, [P, NT]) for n in ("sums", "mu", "var_sum", "ms", "sd", "rs"))
        y = s.sb("y", [P, NT, RET])
        dec = s.sb("dec", [P, HR, P])
        q_dec = s.sb("q_dec", [P, HR, P])
        k_dec, t_dec = s.sb("k_dec", [P, HR]), s.sb("t_dec", [P, HR])
        psT = [k.ps[:, i, :] for i in range(2)]
        two = [k.ps[:, b:b + 2, :].rearrange("p b n -> p (b n)") for b in (2, 4, 6)]
        psS, psKV, psO = two
        loaded, g_loaded, consts_loaded, stored = s.sems("loaded", 3), s.sem("g_loaded"), s.sem("consts_loaded"), s.sem("stored")
        turned, taken, kd_done, scored, kv_done, qd_done, sm_done, state_done, product = (s.sem(n) for n in (
            "turned", "taken", "kd_done", "scored", "kv_done", "qd_done", "sm_done", "state_done", "product"))
        did, meaned, rooted, y_done = (s.sem(n) for n in ("did", "meaned", "rooted", "y_done"))
        block = s.block()
        LINKS = 7

        def part(ap):
            return ap.rearrange("(t p) d -> p t d", p=P)

        @block.sync
        def _(sp):
            for i in range(2):
                sp.dma_start(raw[i][:], part(proj[:, i * RET:i * RET + DR])).then_inc(loaded[i], 16)
            sp.dma_start(dec[:], decay).then_inc(consts_loaded, 16)
            sp.dma_start(k_dec[:], k_decay).then_inc(consts_loaded, 16)
            sp.dma_start(t_dec[:], tile_decay).then_inc(consts_loaded, 16)
            sp.dma_start(q_dec[:].rearrange("p h n -> p (h n)"), row_to_all(q_decay, HR * P)).then_inc(consts_loaded, 16)
            sp.dma_start(v[:], part(proj[:, 2 * RET:3 * RET])).then_inc(loaded[2], 16)
            sp.dma_start(g[:], part(proj[:, 3 * RET:4 * RET])).then_inc(g_loaded, 16)
            with sp.Fori(1, HR) as h:
                first = [sp.snap(h * DR + i * RET) for i in range(2)]
                sp.wait_ge(kd_done, h)
                for i in range(2):
                    sp.dma_start(raw[i][:], part(proj[:, bass.ds(first[i], DR)])).then_inc(loaded[i], 16)
            for h in range(HR):
                sp.wait_ge(y_done, h + 1)
                sp.dma_start(part(dst[:, h * DR:(h + 1) * DR]), y[:, :, h * DR:(h + 1) * DR]).then_inc(stored, 16)
            sp.wait_ge(stored, 16 * HR)

        @block.tensor
        def _(pe):
            with pe.Fori(0, HR) as h:
                for i in range(2):
                    pe.wait_ge(loaded[i], 16 * (h + 1))
                    for b in range(2):
                        pe.wait_ge(taken, 4 * h + 2 * i)
                        for n in range(4):
                            last = pe.transpose(psT[b][:, n * P:(n + 1) * P], raw[i][:, 4 * b + n, :], k.ident[:])
                        last.then_inc(turned, 1)
                pe.wait_ge(taken, 4 * h + 4)
                pe.wait_ge(sm_done, 2 * h)
                for t in range(NT):
                    tok = slice(t * P, (t + 1) * P)
                    last = pe.matmul(psS[:, tok], kT[:, tok], qT[:, tok], start=True, stop=True)
                    if t % 4 == 3:
                        last.then_inc(scored, 1)
                pe.wait_ge(loaded[2], 16)
                pe.wait_ge(kd_done, h + 1)
                pe.wait_ge(state_done, (NT - 1) * h)
                for t in range(NT - 1):
                    pe.matmul(psKV[:, t * P:(t + 1) * P], kd[:, t, :], v[:, t, bass.ds(h * DR, DR)],
                              start=True, stop=True).then_inc(kv_done, 1)
                pe.wait_ge(qd_done, h + 1)
                pe.wait_ge(did, LINKS * h)
                for t in range(NT):
                    tok = slice(t * P, (t + 1) * P)
                    if t % 4 == 0:
                        pe.wait_ge(sm_done, 2 * h + t // 4 + 1)
                    pe.matmul(psO[:, tok], sm[:, tok], v[:, t, bass.ds(h * DR, DR)], start=True, stop=(t == 0))
                    if t:
                        pe.wait_ge(state_done, (NT - 1) * h + t)
                        last = pe.matmul(psO[:, tok], qTd[:, tok], state[:, t, :], start=False, stop=True)
                last.then_inc(product, 1)

        @block.scalar
        def _(act):
            def take(h):
                for i in range(4):
                    act.wait_ge(turned, 4 * h + i + 1)
                    if i == 0 and not isinstance(h, int):
                        act.wait_ge(scored, 2 * h)
                        act.wait_ge(qd_done, h)
                    act.copy((qT, kT)[i // 2][:, (i % 2) * CH:(i % 2 + 1) * CH], psT[i % 2]).then_inc(taken, 1)
                if not isinstance(h, int):
                    act.wait_ge(kv_done, (NT - 1) * h)
                act.activation(kd[:], raw[1][:], ACT.Copy, scale=k_dec[:, bass.ds(h, 1)]).then_inc(kd_done, 1)

            def root(h):
                act.wait_ge(meaned, h + 1)
                act.activation(sd[:], ms[:], ACT.Sqrt).then_inc(rooted, 1)

            act.preload_act_table(ACT.Sqrt)
            act.wait_ge(consts_loaded, 16 * 4)
            take(0)
            with act.Fori(0, HR - 1) as h:
                take(h + 1)
                root(h)
            root(HR - 1)

        @block.vector
        def _(dve):
            dve.wait_ge(consts_loaded, 16 * 4)
            with dve.Fori(0, HR) as h:
                one = bass.ds(h, 1)

                def over_tiles(ap, n):
                    return ap.to_broadcast([P, n, P])

                def each(ap):
                    return ap.rearrange("p (t o) -> p t o", o=1).to_broadcast([P, NT, DR])

                dve.wait_ge(taken, 4 * h + 4)
                dve.wait_ge(product, h)
                dve.tensor_tensor(qTd[:].rearrange("p (t n) -> p t n", n=P), qT[:].rearrange("p (t n) -> p t n", n=P),
                                  over_tiles(q_dec[:, one, :], NT), ALU.mult).then_inc(qd_done, 1)
                for b in range(2):
                    cols = slice(b * CH, (b + 1) * CH)
                    dve.wait_ge(scored, 2 * h + b + 1)
                    dve.tensor_tensor(sm[:, cols].rearrange("p (t n) -> p t n", n=P), psS[:, cols].rearrange("p (t n) -> p t n", n=P),
                                      over_tiles(dec[:, one, :], 4), ALU.mult).then_inc(sm_done, 1)
                for t in range(1, NT):
                    dve.wait_ge(kv_done, (NT - 1) * h + (4 if t <= 4 else NT - 1))
                    kv = psKV[:, (t - 1) * P:t * P]
                    if t == 1:
                        dve.tensor_copy(state[:, 1, :], kv).then_inc(state_done, 1)
                    else:
                        dve.wait_ge(state_done, (NT - 1) * h + t - 1)
                        dve.scalar_tensor_tensor(out=state[:, t, :], in0=state[:, t - 1, :], scalar=t_dec[:, one], in1=kv,
                                                 op0=ALU.mult, op1=ALU.add).then_inc(state_done, 1)
                n = [0]

                def link(ins):
                    n[0] += 1
                    ins.then_inc(did, 1)
                    dve.wait_ge(did, LINKS * h + n[0])

                o = psO.rearrange("p (t d) -> p t d", d=DR)
                dve.wait_ge(product, h + 1)
                link(dve.tensor_reduce(sums[:], o, X, ALU.add))
                link(dve.tensor_scalar(mu[:], sums[:], 1.0 / DR, None, ALU.mult))
                link(dve.tensor_tensor(cen[:], o, each(mu[:]), ALU.subtract))
                link(dve.tensor_tensor(sq[:], cen[:], cen[:], ALU.mult))
                link(dve.tensor_reduce(var_sum[:], sq[:], X, ALU.add))
                dve.tensor_scalar(ms[:], var_sum[:], 1.0 / DR, EPS, ALU.mult, ALU.add).then_inc(meaned, 1)
                dve.wait_ge(rooted, h + 1)
                link(dve.reciprocal(rs[:], sd[:]))
                link(dve.tensor_tensor(nrm[:], cen[:], each(rs[:]), ALU.mult))
                cols = bass.ds(h * DR, DR)
                dve.wait_ge(g_loaded, 16)
                dve.tensor_tensor(y[:, :, cols], nrm[:], g[:, :, cols], ALU.mult).then_inc(y_done, 1)


HS, DS = 8, 64
Z_TOP = 40.0


def stick_breaking_phase(nc, k, tag, proj, dst, mask):
    S0, SB, Y0 = 4 * HR * DR, HS * DS, HR * DR
    ORDER = [*range(NT), *reversed(range(NT))]
    STEPS = 2 * NT
    with ExitStack() as stack:
        s = Scope(nc, tag, stack)
        raw = [s.sb(f"raw{i}", [P, NT, 2 * DS]) for i in range(2)]
        v, g = s.sb("v", [P, NT, SB]), s.sb("g", [P, NT, SB])
        q_hi, k_lo = ([s.sb(f"{n}{p}", [P, SEQ], R) for p in range(2)] for n in ("q_hi", "k_lo"))
        q_lo, k_hi = s.sb("q_lo", [P, SEQ], R), s.sb("k_hi", [P, SEQ], R)
        q_both, k_both = ([[s.sb(f"{n}{p}{a}", [P, SEQ], R) for a in range(2)] for p in range(2)] for n in ("q_both", "k_both"))
        z = [s.sb(f"z{p}", [P, 2, SEQ]) for p in range(3)]
        soft, T, w = ([s.sb(f"{n}{p}", [P, 2, SEQ]) for p in range(2)] for n in ("soft", "T", "w"))
        wT = [s.sb(f"wT{a}", [P, SEQ]) for a in range(2)]
        y = s.sb("y", [P, NT, SB])
        mask_raw, mask_r, ident_r = s.sb("mask_raw", [P, P]), s.sb("mask_r", [P, P], R), s.sb("ident_r", [P, P], R)
        psZ = k.ps[:, 0:2, :].rearrange("p b n -> p (b n)")
        psT = [[k.ps[:, 2 + 2 * a + i, :] for i in range(2)] for a in range(2)]
        psO = [k.ps[:, 6 + p, 0:2 * DS] for p in range(2)]
        psQ = [psT[a][1] for a in range(2)]
        loaded, v_loaded, mask_loaded, mask_done, stored = s.sems("loaded", 2), s.sem("v_loaded"), s.sem("mask_loaded"), s.sem("mask_done"), s.sem("stored")
        stacked, lowered = s.sems("stacked", 2), s.sem("lowered")
        turned, taken, scored, copied, capped, exped, logged, softed, summed, weighed, w_done, w_turned, wT0, wT1, product, y_done = (
            s.sem(n) for n in ("turned", "taken", "scored", "copied", "capped", "exped", "logged", "softed", "summed",
                               "weighed", "w_done", "w_turned", "wT0", "wT1", "product", "y_done"))
        block = s.block()

        def part(ap):
            return ap.rearrange("(t p) d -> p t d", p=P)

        def tile_of(m):
            return ORDER[m]

        def wide(m):
            return (tile_of(m) + 1) * P

        def second(m):
            return sum(2 * (wide(n) > CH) for n in range(m))

        ROUND_SECOND = second(STEPS)

        def turn_step(m):
            return m - 1 if 1 <= m <= 4 else None

        @block.sync
        def _(sp):
            def load(first):
                for i in range(2):
                    sp.dma_start(raw[i][:], part(proj[:, bass.ds(first[i], 2 * DS)])).then_inc(loaded[i], 16)

            load([S0 + i * SB for i in range(2)])
            sp.dma_start(mask_raw[:], mask).then_inc(mask_loaded, 16)
            sp.dma_start(v[:], part(proj[:, S0 + 2 * SB:S0 + 3 * SB])).then_inc(v_loaded, 16)
            sp.dma_start(g[:], part(proj[:, S0 + 3 * SB:S0 + 4 * SB])).then_inc(v_loaded, 16)
            for h in range(HS // 2):
                sp.wait_ge(lowered, 4 * (h + 1))
                for a in range(2):
                    half = slice(a * DS, (a + 1) * DS)
                    for to, of in ((q_both, (q_hi[h % 2], q_lo)), (k_both, (k_hi, k_hi))):
                        for i in range(2):
                            sp.dma_start(to[h % 2][a][i * DS:(i + 1) * DS, :].bitcast(F), of[i][half, :].bitcast(F)).then_inc(stacked[h % 2], 16)
                if h + 1 < HS // 2:
                    load([S0 + i * SB + (h + 1) * 2 * DS for i in range(2)])
            for r in range(2):
                for pair in range(2):
                    cols = slice((r * 2 + pair) * 2 * DS, (r * 2 + pair + 1) * 2 * DS)
                    sp.wait_ge(y_done, STEPS * r + NT * (pair + 1))
                    sp.dma_start(part(dst[:, Y0:Y0 + SB])[:, :, cols], y[:, :, cols]).then_inc(stored, 16)
            sp.wait_ge(stored, 64)

        @block.tensor
        def _(pe):
            pe.wait_ge(mask_done, 2)
            with pe.Fori(0, HS // 4) as r:
                i0 = pe.snap(STEPS * r)

                def turn_qk(pair, group, bank):
                    i, b = group // 2, group % 2
                    pe.wait_ge(loaded[i], 16 * (2 * r + pair + 1))
                    for q in range(4):
                        last = pe.transpose(bank[:, q * P:(q + 1) * P], raw[i][:, 4 * b + q, :], k.ident[:])
                    last.then_inc(turned, 1)

                def score(m, a):
                    if m >= STEPS:
                        return
                    pair, t, half = m // NT, tile_of(m), slice(a * DS, (a + 1) * DS)
                    if m % NT == 0 and a == 0:
                        pe.wait_ge(stacked[pair], 128 * (r + 1))
                    pe.wait_ge(copied, 2 * i0 + 2 * m + a)
                    for c in range(0, wide(m), CH):
                        end = min(c + CH, wide(m))
                        tok = slice(t * P, (t + 1) * P)
                        pe.matmul(psZ[:, c:end], q_both[pair][a][:, tok], k_both[pair][a][:, c:end], start=True, stop=False)
                        pe.matmul(psZ[:, c:end], q_hi[pair][half, tok], k_lo[pair][half, c:end],
                                  start=False, stop=(end < wide(m)))
                    pe.matmul(psZ[:, t * P:(t + 1) * P], ident_r[:], mask_r[:], start=False, stop=True).then_inc(scored, 1)

                def turn(m, a):
                    pe.wait_ge(w_done, i0 + m + 1)
                    if m == 4:
                        pe.wait_ge(lowered, 8 * r + 8)
                    for kt in range(tile_of(m) + 1):
                        last = pe.transpose(psT[a][kt // 4][:, kt % 4 * P:(kt % 4 + 1) * P], w[m % 2][:, a, kt * P:(kt + 1) * P], k.ident[:])
                    last.then_inc(w_turned, 1)

                def multiply(m, a):
                    pe.wait_ge(wT0, 2 * i0 + 2 * m + a + 1)
                    if m == 0 and a == 0:
                        pe.wait_ge(v_loaded, 32)
                        pe.wait_ge(y_done, i0)
                    if m >= 2 and a == 0:
                        pe.wait_ge(y_done, i0 + m - 1)
                    for kt in range(tile_of(m) + 1):
                        if kt == 4:
                            pe.wait_ge(wT1, ROUND_SECOND * r + second(m) + a + 1)
                        last = pe.matmul(psO[m % 2][:, a * DS:(a + 1) * DS], wT[a][:, kt * P:(kt + 1) * P],
                                         v[:, kt, bass.ds(r * 4 * DS + (m // NT * 2 + a) * DS, DS)],
                                         start=(kt == 0), stop=(kt == tile_of(m)))
                    if a:
                        last.then_inc(product, 1)

                for group in range(4):
                    if group >= 2:
                        pe.wait_ge(lowered, 8 * r + group - 1)
                    turn_qk(0, group, psQ[group % 2])
                for m in range(2):
                    for a in range(2):
                        score(m, a)
                for m in range(STEPS + 1):
                    score(m + 2, 0)
                    if m >= 1:
                        turn(m - 1, 0)
                    if m >= 1:
                        turn(m - 1, 1)
                    score(m + 2, 1)
                    if m >= 1:
                        multiply(m - 1, 0)
                    if m >= 1:
                        multiply(m - 1, 1)
                    if turn_step(m) is not None:
                        pe.wait_ge(lowered, 8 * r + 4 + turn_step(m))
                        turn_qk(1, turn_step(m), psQ[turn_step(m) % 2])

        @block.scalar
        def _(act):
            act.wait_ge(mask_loaded, 16)
            act.copy(mask_r[:], mask_raw[:]).then_inc(mask_done, 1)
            act.copy(ident_r[:], k.ident[:]).then_inc(mask_done, 1)
            act.preload_act_table_set("natural_log_exp_and_others")
            with act.Fori(0, HS // 4) as r:
                i0 = act.snap(STEPS * r)

                def take_qk(pair, group, bank):
                    act.wait_ge(turned, 8 * r + 4 * pair + group + 1)
                    if group == 2:
                        if pair:
                            act.wait_ge(stacked[0], 128 * (r + 1))
                        else:
                            act.wait_ge(stacked[1], 128 * r)
                    act.activation((q_hi[pair], k_hi)[group // 2][:, (group % 2) * CH:(group % 2 + 1) * CH], bank, ACT.Copy,
                                   scale=DS ** -0.5 if group < 2 else 1.0).then_inc(taken, 1)

                def copy_z(m, a):
                    if m < STEPS:
                        act.wait_ge(scored, 2 * i0 + 2 * m + a + 1)
                        if m >= 3 and a == 0:
                            act.wait_ge(weighed, i0 + m - 2)
                        act.copy(z[m % 3][:, a, 0:wide(m)], psZ[:, 0:wide(m)]).then_inc(copied, 1)

                def exp(m):
                    if m < STEPS:
                        ap = soft[m % 2][:, :, 0:wide(m)]
                        act.wait_ge(capped, i0 + m + 1)
                        act.activation(ap, ap, ACT.Exp).then_inc(exped, 1)

                def log(m):
                    if m < STEPS:
                        ap = soft[m % 2][:, :, 0:wide(m)]
                        act.wait_ge(exped, i0 + m + 1)
                        act.activation(ap, ap, ACT.Ln, bias=1.0).then_inc(logged, 1)

                def weights(m):
                    if m < STEPS:
                        ap = w[m % 2][:, :, 0:wide(m)]
                        act.wait_ge(weighed, i0 + m + 1)
                        act.activation(ap, ap, ACT.Exp).then_inc(w_done, 1)

                def take(m, a):
                    cols = slice(0, min(wide(m), CH))
                    act.wait_ge(w_turned, 2 * i0 + 2 * m + a + 1)
                    act.wait_ge(product, i0 + m)
                    act.copy(wT[a][:, cols], psT[a][0][:, cols]).then_inc(wT0, 1)

                for group in range(4):
                    take_qk(0, group, psQ[group % 2])
                for m in range(2):
                    for a in range(2):
                        copy_z(m, a)
                exp(0)
                log(0)
                for m in range(STEPS + 1):
                    exp(m + 1)
                    copy_z(m + 2, 0)
                    if m >= 1:
                        take(m - 1, 0)
                    log(m + 1)
                    if m >= 1:
                        take(m - 1, 1)
                    copy_z(m + 2, 1)
                    if turn_step(m) is not None:
                        take_qk(1, turn_step(m), psQ[turn_step(m) % 2])
                    weights(m)

        @block.vector
        def _(dve):
            with dve.Fori(0, HS // 4) as r:
                i0 = dve.snap(STEPS * r)

                def lower_qk(pair, group):
                    bank, cols = psQ[group % 2], slice((group % 2) * CH, (group % 2 + 1) * CH)
                    if group == 0:
                        if pair:
                            dve.wait_ge(stacked[0], 128 * (r + 1))
                        else:
                            dve.wait_ge(stacked[1], 128 * r)
                    dve.wait_ge(taken, 8 * r + 4 * pair + group + 1)
                    dve.scalar_tensor_tensor(out=(q_lo, k_lo[pair])[group // 2][:, cols], in0=bank,
                                             scalar=DS ** -0.5 if group < 2 else 1.0,
                                             in1=(q_hi[pair], k_hi)[group // 2][:, cols].bitcast(F),
                                             op0=ALU.mult, op1=ALU.subtract).then_inc(lowered, 1)

                def cap(m):
                    if m < STEPS:
                        dve.wait_ge(copied, 2 * i0 + 2 * m + 2)
                        dve.tensor_scalar(soft[m % 2][:, :, 0:wide(m)], z[m % 3][:, :, 0:wide(m)], Z_TOP, None,
                                          ALU.min).then_inc(capped, 1)

                def soften(m):
                    p, cols = m % 2, slice(0, wide(m))
                    dve.wait_ge(logged, i0 + m + 1)
                    dve.tensor_tensor(soft[p][:, :, cols], z[m % 3][:, :, cols], soft[p][:, :, cols], ALU.max).then_inc(softed, 1)
                    dve.wait_ge(softed, i0 + m + 1)
                    for a in range(2):
                        back = soft[p][:, a, cols][:, ::-1]
                        dve.tensor_tensor_scan(T[p][:, a, cols][:, ::-1], back, back, 0.0, ALU.add, ALU.bypass).then_inc(summed, 1)

                def weigh(m):
                    p, cols = m % 2, slice(0, wide(m))
                    dve.wait_ge(summed, 2 * i0 + 2 * m + 2)
                    dve.wait_ge(w_turned, 2 * i0 + max(2 * m - 2, 0))
                    dve.tensor_tensor(w[p][:, :, cols], z[m % 3][:, :, cols], T[p][:, :, cols], ALU.subtract).then_inc(weighed, 1)

                def take(m, a):
                    if wide(m) > CH:
                        dve.wait_ge(w_turned, 2 * i0 + 2 * m + a + 1)
                        dve.wait_ge(product, i0 + m)
                        dve.tensor_copy(wT[a][:, CH:wide(m)], psT[a][1][:, 0:wide(m) - CH]).then_inc(wT1, 1)

                def rows(m):
                    dve.wait_ge(product, i0 + m + 1)
                    cols = bass.ds(r * 4 * DS + m // NT * 2 * DS, 2 * DS)
                    dve.tensor_tensor(y[:, tile_of(m), cols], psO[m % 2], g[:, tile_of(m), cols], ALU.mult).then_inc(y_done, 1)

                for group in range(4):
                    lower_qk(0, group)
                cap(0)
                for m in range(STEPS + 1):
                    cap(m + 1)
                    if m < STEPS:
                        soften(m)
                    if m >= 1:
                        take(m - 1, 0)
                        take(m - 1, 1)
                    if m < STEPS:
                        weigh(m)
                    if m >= 2:
                        rows(m - 2)
                    if turn_step(m) is not None:
                        lower_qk(1, turn_step(m))
                rows(STEPS - 1)


def norm_phase(nc, k, src, gain, dst):
    with ExitStack() as stack:
        s = Scope(nc, "fin", stack)
        x = s.sb("x", [P, NT, DM])
        out = s.sb("out", [P, NT, DM])
        gain_b, junk = s.sb("gain", [P, DM]), s.sb("junk", [P, DM], BF)
        ss, ms, sd, rs = (s.sb(n, [P, NT]) for n in ("ss", "ms", "sd", "rs"))
        loaded, gain_loaded = s.sems("loaded", NT), s.sem("gain_loaded")
        squared, meaned, rooted, inverted, ready, stored = (s.sem(n) for n in (
            "squared", "meaned", "rooted", "inverted", "ready", "stored"))
        block = s.block()

        @block.sync
        def _(sp):
            sp.dma_start(gain_b[:], row_to_all(gain, DM)).then_inc(gain_loaded, 16)
            for t in range(NT):
                sp.dma_start(x[:, t, :], src[t * P:(t + 1) * P, :]).then_inc(loaded[t], 16)
            for t in range(NT):
                sp.wait_ge(ready, t + 1)
                sp.dma_start(dst[t * P:(t + 1) * P, :], out[:, t, :]).then_inc(stored, 16)
            sp.wait_ge(stored, 16 * NT)

        @block.scalar
        def _(act):
            act.preload_act_table(ACT.Sqrt)
            for t in range(NT):
                act.wait_ge(loaded[t], 16)
                act.activation(junk[:], x[:, t, :], ACT.Square, accum_out=ss[:, t:t + 1]).then_inc(squared, 1)
                act.wait_ge(meaned, t + 1)
                act.activation(sd[:, t:t + 1], ms[:, t:t + 1], ACT.Sqrt).then_inc(rooted, 1)

        @block.vector
        def _(dve):
            dve.wait_ge(gain_loaded, 16)
            for t in range(NT):
                one = slice(t, t + 1)
                dve.wait_ge(squared, t + 1)
                dve.tensor_scalar(ms[:, one], ss[:, one], 1.0 / DM, EPS, ALU.mult, ALU.add).then_inc(meaned, 1)
                dve.wait_ge(rooted, t + 1)
                dve.reciprocal(rs[:, one], sd[:, one]).then_inc(inverted, 1)
                dve.wait_ge(inverted, t + 1)
                dve.scalar_tensor_tensor(out=out[:, t, :], in0=x[:, t, :], scalar=rs[:, one], in1=gain_b[:],
                                         op0=ALU.mult, op1=ALU.mult).then_inc(ready, 1)


class Shared:
    pass


def build(nc, a, out):
    with ExitStack() as stack:
        k = Shared()
        k.ps = stack.enter_context(nc.psum_tensor("ps", [P, 8, CH], F))
        k.ident = stack.enter_context(nc.sbuf_tensor("ident", [P, P], F))
        k.slot_w = stack.enter_context(nc.sbuf_tensor("slot_w", [P, TOP_K, NT], F))
        k.block_expert = stack.enter_context(nc.sbuf_tensor("block_expert", [P, MAX_BLOCKS + 1], I32))
        ident_loaded = stack.enter_context(nc.semaphore("ident_loaded"))

        def scratch(name, shape, dt=F):
            return nc.dram_tensor(name, shape, dt).ap()

        k.tri_dram = a["triangle"]
        k.xn, k.slot_y = scratch("xn", [SEQ, DM]), scratch("slot_y", [SEQ * TOP_K + P, DM])
        k.slot_rows = scratch("slot_rows", [MAX_BLOCKS * P, 2], I32)
        k.bias_rows = scratch("bias_rows", [P, PAIRS, OFFS, GRID])
        k.neg_rpb = scratch("neg_rpb", [HB, OFFS, 2 * WIN_C - 1])
        proj, att, h1, h2, h3, h4, h5 = (scratch(n, [SEQ, w]) for n, w in (
            ("proj", 6 * CH), ("att", DM), ("h1", DM), ("h2", DM), ("h3", DM), ("h4", DM), ("h5", DM)))
        ple, proj2, y, mod = scratch("ple", [SEQ, DM]), scratch("proj2", [SEQ, 8 * CH]), scratch("y", [SEQ, DM]), scratch("mod", [LAYERS, 3, DM])

        with ExitStack() as first:
            block = first.enter_context(nc.Block())

            @block.sync
            def _(sp):
                sp.dma_start(k.ident[:], a["ident"]).then_inc(ident_loaded, 16)
                sp.wait_ge(ident_loaded, 16)

        x = a["x"][0]
        dense_phase(nc, k, "mix_in", x, a["w_in"][0], proj, ["normrope", "normrope", "copy", "norm", "norm", "copy"],
                    gain=a["g_mix"][0], rope=(a["cos_64"], a["sin_64"], DQK), head=[DQK, DQK, 0, DB_H, DB_H, 0],
                    head_gain={0: a["g_qa"][0], 1: a["g_ka"][0], 3: a["g_qb"][0], 4: a["g_kb"][0]},
                    order=[2, 0, 1, 3, 4, 5])
        diff_attention_phase(nc, k, proj, att, [a[n][0] for n in ("lam_q1", "lam_k1", "lam_q2", "lam_k2")],
                             a["g_sub"][0], a["rpb"][0])
        neighbourhood_phase(nc, k, proj, att, a["neighbour"])
        dense_phase(nc, k, "mix_out", att, a["w_out"][0], h1, ["resid"] * 2, resid=x)
        router_phase(nc, k, h1, a["g_ffn"][0], a["w_rg"][0], a["w_re"][0], a["router"], a["token_ids"])
        expert_phase(nc, k, a["w1"][0], a["w3"][0], a["w2"][0])
        between_phase(nc, k, h1, h2, a["p"][0, 0], a["w_ple"][0], a["g_ple"][0], ple,
                      a["c_2"][0], a["w_ada_2"].rearrange("l k n -> (l k) n"), a["b_ada_2"], a["norm_g_2"], mod)
        dense_phase(nc, k, "ple_gate", h2, a["w_plg"][0], h3, ["gated"] * 2, gain=a["g_plg"][0], resid=h2, times=ple)
        for l, (h_in, h_out) in enumerate(((h3, h4), (h4, h5))):
            dense_phase(nc, k, f"in{l}", h_in, a["w_in_2"][l], proj2,
                        ["rope", "rope", "copy", "silu", "copy", "copy", "copy", "silu"],
                        gain=mod[l, 1], shift=mod[l, 0], rope=(a["cos_128"], a["sin_128"], DR),
                        order=[2, 0, 1, 4, 5, 6, 3, 7])
            retention_phase(nc, k, f"ret{l}", proj2, y, a["decay"], a["q_decay"], a["k_decay"], a["tile_decay"])
            stick_breaking_phase(nc, k, f"stick{l}", proj2, y, a["stick_mask"])
            dense_phase(nc, k, f"out{l}", y, a["w_out_2"][l], h_out, ["resid"] * 2, resid=h_in, gate=mod[l, 2])
        norm_phase(nc, k, h5, a["final_g_2"], out[0])


def rope_table(dim):
    inv = (10000.0 ** (-np.arange(0, dim, 2, dtype=np.float32) / dim)).astype(np.float32)
    angle = (np.arange(SEQ, dtype=np.float32)[:, None] * inv[None, :]).astype(np.float32)
    return np.cos(angle), np.concatenate([-np.sin(angle), np.sin(angle)], axis=1)


def shape_constants():
    f = np.float32
    c = {"ident": np.eye(P, dtype=f), "triangle": np.triu(np.ones((P, P), f), 1)}
    c["router"] = np.concatenate([np.arange(8, 0, -1), np.arange(NT) * P, np.arange(MAX_BLOCKS)]).astype(f)
    slots, spare = SEQ * TOP_K, MAX_BLOCKS * P
    c["token_ids"] = np.concatenate([np.stack([np.tile(np.arange(SEQ), TOP_K), np.arange(slots)], 1),
                                     np.stack([np.zeros(spare, int), slots + np.arange(spare) % P], 1)]).astype(np.int32)
    p, col = np.arange(P)[:, None], np.arange(P)[None, :]
    c["neighbour"] = np.concatenate([(col % 64 // DB_H == p // GRID).astype(f), np.tile(np.eye(GRID, dtype=f), (2, 1))], axis=1)
    c["cos_64"], c["sin_64"] = rope_table(DQK)
    c["cos_128"], c["sin_128"] = rope_table(DR)
    log_gamma = np.log1p(-2.0 ** (-5.0 - np.arange(HR)))
    n = np.arange(P)
    allowed = n[:, None] // 64 <= n[None, :] // 64
    decay = np.exp(np.abs(n[None, :] - n[:, None])[:, None, :] * log_gamma[None, :, None]) * allowed[:, None, :]
    c["decay"] = (decay * DR ** -0.5).astype(f)
    c["q_decay"] = np.exp((n + 1)[None, :] * log_gamma[:, None]).astype(f).reshape(-1)
    c["k_decay"] = (np.exp((P - 1 - n)[:, None] * log_gamma[None, :]) * DR ** -0.5).astype(f)
    c["tile_decay"] = np.tile(np.exp(P * log_gamma), (P, 1)).astype(f)
    c["stick_mask"] = np.where(col >= p, -BIG, 0.0).astype(f)
    return c


def kernel(**inputs):
    import concourse.bacc as bacc
    from concourse.bass_utils import run_bass_kernel_spmd

    nc = bacc.Bacc("TRN2", target_bir_lowering=False, num_devices=1)
    arrays, aps = {}, {}
    for name, array in (*inputs.items(), *shape_constants().items()):
        array = np.ascontiguousarray(array)
        arrays[f"in_{name}_dram"] = array
        aps[name] = nc.dram_tensor(f"in_{name}_dram", array.shape, mybir.dt.from_np(array.dtype), kind="ExternalInput").ap()
    out = nc.dram_tensor("out_0_dram", (1, SEQ, DM), F, kind="ExternalOutput").ap()
    build(nc, aps, out)
    result = run_bass_kernel_spmd(nc, [arrays], core_ids=[0])
    return result.results[0]["out_0_dram"]
```
